# Optimizing a Trainium2 kernel written in Bass

```python
import jax, jax.numpy as jnp
from jax import lax
import numpy as np

D_MODEL = 1024
BATCH = 1
SEQ = 512
DEPTH = 2

CHUNK = 64
N_META = 16
META_PAD = CHUNK - N_META
N_A_LAYERS = DEPTH // 2
N_B_LAYERS = DEPTH - N_A_LAYERS
ROPE_THETA = 10000.0
NORM_EPS = 1e-6
NEG_INF = -1e30

RET_HEADS = 4
RET_QK_DIM = D_MODEL // RET_HEADS
RET_V_DIM = 2 * RET_QK_DIM
RET_QK_WIDTH = RET_HEADS * RET_QK_DIM
RET_VAL_WIDTH = RET_HEADS * RET_V_DIM
RET_IN_WIDTH = 2 * RET_QK_WIDTH + 2 * RET_VAL_WIDTH

SWA_HEAD_DIM = 64
SWA_Q_HEADS = D_MODEL // SWA_HEAD_DIM
SWA_KV_HEADS = 4
SWA_GROUP = SWA_Q_HEADS // SWA_KV_HEADS
SWA_WINDOW = 128
WINDOW_CHUNKS = SWA_WINDOW // CHUNK
KV_WIDTH = SWA_KV_HEADS * SWA_HEAD_DIM

N_GROUPS = 4
EXPERTS_PER_GROUP = 4
N_EXPERTS = N_GROUPS * EXPERTS_PER_GROUP
EXPERT_FF = 256
TOP_K_INNER = 2

kernel_name = "yoco_retention_swa_sink_hier_moe"

def rms_norm(x, g):
    xf = x.astype(jnp.float32)
    y = xf * lax.rsqrt(jnp.mean(xf * xf, axis=-1, keepdims=True) + NORM_EPS)
    return (y * g.astype(jnp.float32)).astype(x.dtype)

def rope(x, pos):
    half = x.shape[-1] // 2
    inv = ROPE_THETA ** (-jnp.arange(half, dtype=jnp.float32) / half)
    ang = pos.astype(jnp.float32)[:, None] * inv[None, :]
    cos = jnp.cos(ang)[None, :, None, :]
    sin = jnp.sin(ang)[None, :, None, :]
    xf = x.astype(jnp.float32)
    x1, x2 = xf[..., :half], xf[..., half:]
    return jnp.concatenate([x1 * cos - x2 * sin, x2 * cos + x1 * sin], axis=-1).astype(x.dtype)

def to_chunks(t):
    b, l, h, d = t.shape
    return t.reshape(b, l // CHUNK, CHUNK, h, d).transpose(1, 0, 3, 2, 4)

def retention(h, w_in, w_out, pos, valid):
    b, l, _ = h.shape
    proj = h @ w_in
    q, k, v, g = jnp.split(proj, [RET_QK_WIDTH, 2 * RET_QK_WIDTH, 2 * RET_QK_WIDTH + RET_VAL_WIDTH], axis=-1)
    q = rope(q.reshape(b, l, RET_HEADS, RET_QK_DIM), pos)
    k = rope(k.reshape(b, l, RET_HEADS, RET_QK_DIM), pos) * (RET_QK_DIM ** -0.5)
    k = k * valid[None, :, None, None]
    v = v.reshape(b, l, RET_HEADS, RET_V_DIM)
    qc, kc, vc = to_chunks(q), to_chunks(k), to_chunks(v)

    log_gamma = jnp.log1p(-jnp.exp2(-5.0 - jnp.arange(RET_HEADS, dtype=jnp.float32)))
    idx = jnp.arange(CHUNK, dtype=jnp.float32)
    diff = idx[:, None] - idx[None, :]
    inner_decay = jnp.where(diff >= 0, jnp.exp(log_gamma[:, None, None] * jnp.maximum(diff, 0.0)), 0.0)
    q_decay = jnp.exp(log_gamma[:, None] * (idx + 1.0))[..., None]
    k_decay = jnp.exp(log_gamma[:, None] * (CHUNK - 1.0 - idx))[..., None]
    chunk_decay = jnp.exp(log_gamma * CHUNK)[None, :, None, None]

    def step(state, xs):
        qi, ki, vi = xs
        s = jnp.einsum('bhqd,bhkd->bhqk', qi, ki) * inner_decay
        o = jnp.einsum('bhqk,bhkv->bhqv', s, vi) + jnp.einsum('bhqd,bhdv->bhqv', qi * q_decay, state)
        state = state * chunk_decay + jnp.einsum('bhkd,bhkv->bhdv', ki * k_decay, vi)
        return state, o

    state0 = jnp.zeros((b, RET_HEADS, RET_QK_DIM, RET_V_DIM), jnp.float32)
    _, o = lax.scan(step, state0, (qc, kc, vc))
    o = o.transpose(1, 0, 3, 2, 4).reshape(b, l, RET_HEADS, RET_V_DIM).astype(jnp.float32)
    mu = jnp.mean(o, axis=-1, keepdims=True)
    var = jnp.mean(jnp.square(o - mu), axis=-1, keepdims=True)
    on = ((o - mu) * lax.rsqrt(var + NORM_EPS)).reshape(b, l, RET_VAL_WIDTH)
    y = (jax.nn.silu(g.astype(jnp.float32)) * on).astype(h.dtype)
    return y @ w_out

def shared_kv(x, kv_norm, kv_w, kv_b, pos):
    b, l, _ = x.shape
    kv = rms_norm(x, kv_norm) @ kv_w + kv_b
    k, v = jnp.split(kv, 2, axis=-1)
    k = rope(k.reshape(b, l, SWA_KV_HEADS, SWA_HEAD_DIM), pos)
    v = v.reshape(b, l, SWA_KV_HEADS, SWA_HEAD_DIM)
    return k, v

def band(t):
    n_c = t.shape[1]
    parts = [jnp.pad(t, ((0, 0), (s, 0), (0, 0), (0, 0), (0, 0)))[:, :n_c] for s in reversed(range(WINDOW_CHUNKS))]
    return jnp.concatenate(parts, axis=2)

def swa_sink_attention(h, w_q, b_q, sinks, w_o, b_o, k_sh, v_sh, pos):
    b, l, _ = h.shape
    n_c = l // CHUNK
    q = rope((h @ w_q + b_q).reshape(b, l, SWA_Q_HEADS, SWA_HEAD_DIM), pos) * (SWA_HEAD_DIM ** -0.5)
    q = q.reshape(b, n_c, CHUNK, SWA_KV_HEADS, SWA_GROUP, SWA_HEAD_DIM)
    kb = band(k_sh.reshape(b, n_c, CHUNK, SWA_KV_HEADS, SWA_HEAD_DIM))
    vb = band(v_sh.reshape(b, n_c, CHUNK, SWA_KV_HEADS, SWA_HEAD_DIM))
    k_meta = k_sh[:, META_PAD:CHUNK]
    v_meta = v_sh[:, META_PAD:CHUNK]
    c_idx = jnp.arange(n_c)[:, None]
    j_idx = jnp.arange(WINDOW_CHUNKS * CHUNK)[None, :]
    band_valid = (c_idx - (WINDOW_CHUNKS - 1)) * CHUNK + j_idx >= CHUNK

    s_meta = jnp.einsum('bnqkgd,bmkd->bnkgqm', q, k_meta).astype(jnp.float32)
    s_band = jnp.einsum('bnqkgd,bnjkd->bnkgqj', q, kb).astype(jnp.float32)
    s_band = jnp.where(band_valid[None, :, None, None, None, :], s_band, NEG_INF)
    sink = jnp.broadcast_to(sinks.astype(jnp.float32).reshape(1, 1, SWA_KV_HEADS, SWA_GROUP, 1, 1),
                            s_meta.shape[:-1] + (1,))
    p = jax.nn.softmax(jnp.concatenate([s_meta, s_band, sink], axis=-1), axis=-1)
    p_meta = p[..., :N_META].astype(v_sh.dtype)
    p_band = p[..., N_META:N_META + WINDOW_CHUNKS * CHUNK].astype(v_sh.dtype)
    o = (jnp.einsum('bnkgqm,bmkd->bnqkgd', p_meta, v_meta)
         + jnp.einsum('bnkgqj,bnjkd->bnqkgd', p_band, vb))
    return o.reshape(b, l, SWA_Q_HEADS * SWA_HEAD_DIM) @ w_o + b_o

def hier_moe(h, w_group, w_router, w_gate, w_up, w_down):
    b, l, d = h.shape
    t = h.reshape(-1, d)
    g_probs = jax.nn.softmax((t @ w_group).astype(jnp.float32), axis=-1)
    g_sel = jnp.argmax(g_probs, axis=-1)
    g_w = jnp.take_along_axis(g_probs, g_sel[:, None], axis=-1)
    e_logits = (t @ w_router).astype(jnp.float32).reshape(-1, N_GROUPS, EXPERTS_PER_GROUP)
    e_logits = jnp.take_along_axis(e_logits, g_sel[:, None, None], axis=1)[:, 0]
    top_p, top_i = lax.top_k(jax.nn.softmax(e_logits, axis=-1), TOP_K_INNER)
    weights = g_w * top_p / jnp.sum(top_p, axis=-1, keepdims=True)
    expert_idx = g_sel[:, None] * EXPERTS_PER_GROUP + top_i
    gates = jnp.sum(jax.nn.one_hot(expert_idx, N_EXPERTS, dtype=jnp.float32) * weights[..., None], axis=1)
    a = jnp.einsum('td,edf->tef', t, w_gate)
    u = jnp.einsum('td,edf->tef', t, w_up)
    hid = jax.nn.silu(a) * u * gates[:, :, None].astype(t.dtype)
    y = jnp.einsum('tef,efd->td', hid, w_down)
    return y.reshape(b, l, d)

def setup_inputs(seed: int = 0) -> dict:
    key = jax.random.key(seed)
    ks = jax.random.split(key, 24)
    f32 = jnp.float32

    def nrm(k, shape, fan_in):
        return jax.random.normal(k, shape, f32) * (fan_in ** -0.5)

    def gain(k, shape):
        return 1.0 + 0.02 * jax.random.normal(k, shape, f32)

    return {
        "x": jax.random.normal(ks[0], (BATCH, SEQ, D_MODEL), f32),
        "meta_tokens": jax.random.normal(ks[1], (N_META, D_MODEL), f32),
        "ret_norm": gain(ks[2], (N_A_LAYERS, D_MODEL)),
        "ret_w_in": nrm(ks[3], (N_A_LAYERS, D_MODEL, RET_IN_WIDTH), D_MODEL),
        "ret_w_out": nrm(ks[4], (N_A_LAYERS, RET_VAL_WIDTH, D_MODEL), RET_VAL_WIDTH),
        "kv_norm": gain(ks[5], (D_MODEL,)),
        "kv_w": nrm(ks[6], (D_MODEL, 2 * KV_WIDTH), D_MODEL),
        "kv_b": 0.02 * jax.random.normal(ks[7], (2 * KV_WIDTH,), f32),
        "swa_norm": gain(ks[8], (N_B_LAYERS, D_MODEL)),
        "swa_w_q": nrm(ks[9], (N_B_LAYERS, D_MODEL, SWA_Q_HEADS * SWA_HEAD_DIM), D_MODEL),
        "swa_b_q": 0.02 * jax.random.normal(ks[10], (N_B_LAYERS, SWA_Q_HEADS * SWA_HEAD_DIM), f32),
        "swa_sinks": 0.5 * jax.random.normal(ks[11], (N_B_LAYERS, SWA_Q_HEADS), f32),
        "swa_w_o": nrm(ks[12], (N_B_LAYERS, SWA_Q_HEADS * SWA_HEAD_DIM, D_MODEL), SWA_Q_HEADS * SWA_HEAD_DIM),
        "swa_b_o": 0.02 * jax.random.normal(ks[13], (N_B_LAYERS, D_MODEL), f32),
        "moe_norm": gain(ks[14], (DEPTH, D_MODEL)),
        "moe_w_group": nrm(ks[15], (DEPTH, D_MODEL, N_GROUPS), D_MODEL),
        "moe_w_router": nrm(ks[16], (DEPTH, D_MODEL, N_EXPERTS), D_MODEL),
        "moe_w_gate": nrm(ks[17], (DEPTH, N_EXPERTS, D_MODEL, EXPERT_FF), D_MODEL),
        "moe_w_up": nrm(ks[18], (DEPTH, N_EXPERTS, D_MODEL, EXPERT_FF), D_MODEL),
        "moe_w_down": nrm(ks[19], (DEPTH, N_EXPERTS, EXPERT_FF, D_MODEL), EXPERT_FF),
        "final_norm": gain(ks[20], (D_MODEL,)),
    }

def reference(x, meta_tokens, ret_norm, ret_w_in, ret_w_out, kv_norm, kv_w, kv_b,
              swa_norm, swa_w_q, swa_b_q, swa_sinks, swa_w_o, swa_b_o,
              moe_norm, moe_w_group, moe_w_router, moe_w_gate, moe_w_up, moe_w_down,
              final_norm):
    b = x.shape[0]
    pad = jnp.zeros((b, META_PAD, D_MODEL), x.dtype)
    meta = jnp.broadcast_to(meta_tokens.astype(x.dtype)[None], (b, N_META, D_MODEL))
    h = jnp.concatenate([pad, meta, x], axis=1)
    l = h.shape[1]
    idx = jnp.arange(l, dtype=jnp.int32)
    pos = idx - META_PAD
    valid = (idx >= META_PAD).astype(h.dtype)

    k_sh = None
    v_sh = None
    for i in range(DEPTH):
        if i < N_A_LAYERS:
            h = h + retention(rms_norm(h, ret_norm[i]), ret_w_in[i], ret_w_out[i], pos, valid)
        else:
            if i == N_A_LAYERS:
                k_sh, v_sh = shared_kv(h, kv_norm, kv_w, kv_b, pos)
            j = i - N_A_LAYERS
            h = h + swa_sink_attention(rms_norm(h, swa_norm[j]), swa_w_q[j], swa_b_q[j], swa_sinks[j],
                                       swa_w_o[j], swa_b_o[j], k_sh, v_sh, pos)
        h = h + hier_moe(rms_norm(h, moe_norm[i]), moe_w_group[i], moe_w_router[i],
                         moe_w_gate[i], moe_w_up[i], moe_w_down[i])

    return rms_norm(h, final_norm)[:, CHUNK:]


_drawn_inputs = setup_inputs


def setup_inputs(seed=0):
    import zlib

    import numpy as np

    out = dict(_drawn_inputs(seed))
    spreads = {}
    factors = {'kv_norm': 6.954,
     'swa_norm': 7.414,
     'swa_b_q': 5.684,
     'swa_sinks': 8.0,
     'final_norm': 8.7,
     'kv_b': 3.83,
     'swa_b_o': 8.0}
    for name, (base, spread) in spreads.items():
        noise = np.random.default_rng([zlib.crc32(name.encode()), seed]).standard_normal(out[name].shape)
        drawn = base * np.exp(spread * noise) if base else spread * noise
        out[name] = __import__('jax').numpy.asarray(drawn.astype(out[name].dtype))
    for name, factor in factors.items():
        out[name] = (out[name] * factor).astype(out[name].dtype)
    return out
```

```python
import numpy as np
from contextlib import ExitStack
import concourse.bass as bass
from concourse import mybir

D = 1024
KT = D // 128
SEQ, N_META, CHUNK = 512, 16, 64
POS = N_META + SEQ
NT = SEQ // 128
META = NT
HALF = POS // 2
HEADS, QK, VD = 4, 256, 512
KV_HEADS, Q_HEADS, HD = 4, 16, 64
GROUPS, PER_GROUP = 4, 4
EXPERTS = GROUPS * PER_GROUP
FF = 256
EPS = 1e-6
BLK = 128
RING = 3


def blocks_needed(tokens):
    return (2 * tokens - EXPERTS) // BLK + EXPERTS


NBLK = [-(-blocks_needed(POS) // RING) * RING, -(-blocks_needed(SEQ) // RING) * RING]
MAXBLK = max(NBLK)
SLOTS = MAXBLK * BLK

C_ID, C_ONE, C_512, C_TRI = 0, 128, 256, 384
C_REV, C_THR, C_BLK, C_VALID, C_NH = 512, 516, 521, 545, 550
NCONST = 560
NRT = 2 * POS + HEADS * POS
NST = 5 * 32 * 3 + 512


def tables():
    f = np.float32
    c = np.zeros((128, NCONST), f)
    c[:, C_ID:C_ID + 128] = np.eye(128)
    c[:, C_ONE:C_ONE + 128] = 1.0
    c[:, C_512:C_512 + 128] = 1.0 / VD
    c[:, C_TRI:C_TRI + 128] = np.arange(128)[:, None] < np.arange(128)[None, :]
    c[:, C_REV:C_REV + 4] = [4, 3, 2, 1]
    c[:, C_THR:C_THR + 5] = np.arange(5) * BLK
    c[:, C_BLK:C_BLK + MAXBLK] = np.arange(MAXBLK)
    c[:, C_VALID:C_VALID + 5] = 1.0
    c[N_META:, C_VALID + META] = 0.0
    c[:, C_NH:C_NH + 5] = -0.5
    r = np.zeros((128, NRT), f)
    inv = (f(10000.0) ** (-np.arange(128, dtype=f) / f(128))).astype(f)
    ang = np.arange(POS, dtype=f)[None, :] * inv[:, None]
    r[:, 0:POS], r[:, POS:2 * POS] = np.cos(ang), np.sin(ang)
    lg = np.log1p(-np.exp2(-5.0 - np.arange(HEADS)))
    diff = np.arange(POS)[None, :] - np.arange(128)[:, None]
    for h in range(HEADS):
        dec = np.where(diff >= 0, np.exp(lg[h] * np.maximum(diff, 0)), 0.0) * QK ** -0.5
        r[:, 2 * POS + h * POS:2 * POS + (h + 1) * POS] = dec
    s = np.zeros((128, NST), f)
    inv = (f(10000.0) ** (-np.arange(32, dtype=f) / f(32))).astype(f)
    for t in range(5):
        pos = np.arange(128, dtype=f) + (0 if t == META else N_META + 128 * t)
        ang = pos[:, None] * inv[None, :]
        s[:, t * 32:t * 32 + 32] = np.cos(ang)
        s[:, 160 + t * 64:160 + t * 64 + 32] = -np.sin(ang)
        s[:, 160 + t * 64 + 32:160 + t * 64 + 64] = np.sin(ang)
    for v in range(2):
        m = np.full((128, 256), -1e30, f)
        m[:, 128:144] = 0.0
        m[0:64, 0:64] = 0.0
        m[64:128, 0:128] = 0.0
        if v:
            m[0:64, 192:256] = 0.0
        s[:, 480 + 256 * v:480 + 256 * v + 256] = m
    return c, r, s


class Fills:

    def __init__(self, full, free):
        self.full, self.free = full, free
        self.total = [0] * 8
        self.at = {}

    def phase(self, order, rounds=1):
        per = [sum(1 for _, b in order if b == k) for k in range(8)]
        seen = list(self.total)
        for name, b in order:
            assert name not in self.at, name
            self.at[name] = (b, seen[b], per[b])
            seen[b] += 1
        self.total = [self.total[k] + rounds * per[k] for k in range(8)]
        return list(self.total)

    def bank(self, name):
        return self.at[name][0]

    def wait_free(self, eng, name, i=0):
        b, n, per = self.at[name]
        if n or not isinstance(i, int):
            eng.wait_ge(self.free[b], i * per + n)

    def wait_full(self, eng, name, i=0):
        b, n, per = self.at[name]
        eng.wait_ge(self.full[b], i * per + (n + 1))

    def wait_read(self, eng, name, i=0):
        b, n, per = self.at[name]
        eng.wait_ge(self.free[b], i * per + (n + 1))


class Steps:

    def __init__(self, eng, sem):
        self.eng, self.sem, self.n, self.i, self.per, self.off = eng, sem, 0, None, 0, 0

    def rounds(self, i, per):
        self.i, self.per, self.off = i, per, 0

    def end(self, rounds):
        assert self.off == self.per, (self.off, self.per)
        self.n, self.i = self.n + rounds * self.per, None

    def count(self):
        return self.n if self.i is None else self.i * self.per + (self.n + self.off)

    def done(self, ins):
        ins.then_inc(self.sem, 1)
        if self.i is None:
            self.n += 1
        else:
            self.off += 1

    def wait(self):
        self.eng.wait_ge(self.sem, self.count())

    def __call__(self, ins):
        self.done(ins)
        self.wait()


def build(nc, a, out, dbg=None):
    F, I = mybir.dt.float32, mybir.dt.int32
    ALU, ACT, AX = mybir.AluOpType, mybir.ActivationFunctionType, mybir.AxisListType
    X, XY = AX.X, AX.XY
    ctx = ExitStack()
    with ctx:
        def sem(name):
            return ctx.enter_context(nc.semaphore(name))

        def sb(name, shape, dt=F):
            return ctx.enter_context(nc.sbuf_tensor(name, shape, dt))

        def col0(t):
            return 0 if t == META else N_META + 128 * t

        def rows(t):
            return N_META if t == META else 128

        con = sb("con", [128, NCONST])
        ident, ones, mean512, tri = (con[:, c:c + 128] for c in (C_ID, C_ONE, C_512, C_TRI))
        gains = sb("gains", [128, 5, KT])
        G_RET, G_KV, G_SWA, G_MOE = 0, 1, 2, (3, 4)
        wr = sb("wr", [128, 2, KT, 20])
        h = sb("h", [128, 5, D])
        ring = sb("ring", [128, RING, KT, 512])
        xT = sb("xT", [128, KT, POS])
        ss, var, rstd = sb("ss", [128, 5]), sb("var", [128, 5]), sb("rstd", [128, 5])
        eb_i = sb("eb_i", [1, 2, MAXBLK], I)
        slot_i = sb("slot_i", [128, 2, 5], I)
        ps = ctx.enter_context(nc.psum_tensor("ps", [128, 8, 512], F))

        ARENA = 29400
        arena = sb("arena", [128, ARENA])

        class Carve:

            def __init__(self):
                self.at = 0

            def __call__(self, *shape):
                n = int(np.prod(shape))
                v = arena[:, self.at:self.at + n]
                self.at += n
                assert self.at <= ARENA, self.at
                if len(shape) == 1:
                    return v
                names = "abcd"[:len(shape)]
                return v.rearrange(f"p ({' '.join(names)}) -> p {' '.join(names)}",
                                   **dict(zip(names[1:], shape[1:])))

        cv = Carve()
        ret_xn = cv(5, D)
        cv.at = 0
        yT = cv(16, POS)
        rope_c, rope_s = cv(POS), cv(POS)
        decay = cv(HEADS, POS)
        qT, kT = cv(2, POS), cv(2, POS)
        v_tm = cv(5, VD)
        gate_t, gate = cv(4, POS), cv(4, POS)
        s_meta, s_t = cv(POS), cv(NT, 512)
        o_fm, sq = cv(4, POS), cv(4, POS)
        vr, rs = cv(POS), cv(POS)
        zero = cv(D)
        ret_junk = s_t.rearrange("p a b -> p (a b)")[:, 0:D]
        cv = Carve()
        xn = cv(5, D)
        down = cv(RING, 2, D)
        xg = cv(RING, D)
        xgT = cv(RING, KT, 128)
        yo = cv(RING, D)
        th, hid1, hid = cv(FF), cv(FF), cv(FF)
        hidT = cv(2, 128)
        lg = cv(5, 20)
        small = cv(2200)
        gat = cv(2, 2, D)
        cv = Carve()
        xn1 = cv(5, D)
        xTk = cv(KT, POS)
        kT2 = cv(4, POS)
        kr, kA, kB = cv(2, 4, 128), cv(4, 64), cv(4, 64)
        kvs = cv(2, 512)
        V, VX = cv(5, 256), cv(NT, 256)
        qs, qA, qr, oN = cv(D), cv(D), cv(D), cv(D)
        qT1, oT1 = cv(KT, 128), cv(KT, 128)
        stab = cv(NST)
        sink_b, mx, nmx, es, sx, sm, rc = (cv(16) for _ in range(7))
        kvb, qb, bo = cv(512), cv(D), cv(D)
        PT = cv(2, 4, 128)
        P = arena[:, 0:16 * 256].rearrange("p (h k) -> p h k", h=16)
        wo_b = arena[:, 5 * D:5 * D + KT * 512].rearrange("p (k n) -> p k n", k=KT)
        swa_junk = qs
        cv = Carve()
        fo = cv(NT, D)
        fin_g = cv(D)
        fin_junk = cv(D)

        slot_rows = nc.dram_tensor("slot_rows", (SLOTS, D), F).ap()
        slot_out = nc.dram_tensor("slot_out", (SLOTS, D), F).ap()

        full = [sem(f"bank_full{b}") for b in range(8)]
        free = [sem(f"bank_free{b}") for b in range(8)]
        fl = Fills(full, free)
        w_in = [sem(f"weights_in{s}") for s in range(RING)]
        s_const, s_x, s_zero, s_zeroed, s_rt, s_gains = (sem(n) for n in (
            "const_in", "x_in", "zero_made", "slots_zeroed", "ret_tables_in", "gains_in"))
        s_init = sem("stats_cleared")

        TILES5 = [META, 0, 1, 2, 3]
        A, B, C, E = 0, 2, 4, 6

        def norm_plan(tag, tiles):
            fl.phase([(f"{tag}{t}", 2 * (n % 4)) for n, t in enumerate(tiles)])

        norm_plan("n0_", TILES5)
        fl.phase([("Q1", A), ("Q2", B), ("K1", C), ("K2", E), ("V01", A), ("V23", B), ("V4", C),
                  ("G0", E), ("G1", A), ("G2", B), ("G3", C), ("SM", E), ("S01", A), ("S23", B),
                  ("O0", C), ("O1", E), ("O2", A), ("O3", B), ("MU", C), ("VAR", E)], HEADS)
        fl.phase([("W0_01", A), ("W0_23", B), ("W0_4", C), ("W1_01", E), ("W1_23", A), ("W1_4", B)])
        t_blocks, t_blocks_end = {}, {}

        def moe_plan(l):
            norm_plan(f"m{l}_", TILES5[l:])
            fl.phase([(f"LG{l}", 0), (f"RK{l}", 2)])
            t_blocks[l] = list(fl.total)
            fl.phase([(f"XF{l}", 0)])

            def round_of(z, last):
                return [(f"{x}{l}{z}{j}", b) for j in range(RING) for x, b in
                        (("GU", 2 + j), ("XT", 0), ("HT", 5), ("YA", 6), ("YB", 7))
                        if not (last and x == "XT" and j == RING - 1)]
            fl.phase(round_of("r", False), NBLK[l] // RING - 1)
            fl.phase(round_of("z", True))
            t_blocks_end[l] = list(fl.total)

        moe_plan(0)
        norm_plan("n1_", TILES5)
        t_norm1 = list(fl.total)
        fl.phase([(f"KV{t}", n) for n, t in enumerate(TILES5)])
        fl.phase([(f"KT{t}", 5 + n % 3) for n, t in enumerate(TILES5)])
        t_kv = list(fl.total)
        plan = [("Qa0", 4), ("Qb0", 5), ("QT0", 0)]
        for t in range(NT):
            plan += [(f"S{t}_{p}", p % 6) for p in range(8)]
            if t + 1 < NT:
                plan += [(f"Qa{t + 1}", 4), (f"Qb{t + 1}", 5)]
            plan += [(f"AV{t}", 6)] + [(f"PT{t}_{p}", p % 4) for p in range(8)]
            if t + 1 < NT:
                plan += [(f"QT{t + 1}", 0)]
            plan += [(f"OT{t}", 2), (f"WO{t}", 4)]
        fl.phase(plan)
        t_swa = list(fl.total)
        moe_plan(1)

        def all_read(eng, totals):
            for b in range(8):
                if totals[b]:
                    eng.wait_ge(free[b], totals[b])

        def pair(b):
            return ps[:, b:b + 2, 0:HALF]

        def halves(ap):
            return ap.rearrange("p (g c) -> p g c", g=2)

        def sigs(names, tag):
            return {n: sem(f"{n}{tag}") for n in names.split()}

        nrm = {k: sigs("sq_done var_done rstd_done xn_done", k) for k in ("_r", "_m0", "_s", "_m1", "_f")}
        q_ready, k_ready, gt_done, squared, var_copied, rs_ready, y_ready, wo_first = (sem(n) for n in (
            "q_ready", "k_ready", "gate_tanh_done", "squared", "var_copied", "rs_ready", "y_ready", "w_out_half_read"))
        mo = [sigs("lg_ready eg_in eg_out d_in d_out mask_ready eb_ready slot_ready scattered blocks_stored "
                   "tanh_done y_out0 y_out1 y_out2 x_in0 x_in1 x_in2 down_in0 down_in1 down_in2 "
                   "gathered0 gathered1 gath_used", f"_{l}") for l in range(2)]
        s_swat, kv_evac, kr_ready, V_ready, VX_zero, VX_ready = (sem(n) for n in (
            "swa_tables_in", "kv_evac", "k_rotated", "V_ready", "VX_zeroed", "VX_ready"))
        q_rot, m_ready, p_exp, snk_exp, bo_added = (sem(n) for n in (
            "q_rotated", "max_ready", "p_exp", "sink_exp", "bo_added"))
        wo_b_in = sem("w_o_b_in")
        fin_done, s_out, fin_in = sem("final_done"), sem("out_stored"), sem("final_gain_in")
        dsem = {k: sem(f"dve_steps_{k}") for k in "nraskf"}
        dsem_m = [sem(f"dve_steps_moe{l}") for l in range(2)]

        N_WO = 3 * HEADS
        N_M = [N_WO + 4, N_WO + 4 + NBLK[0] + 4]
        N_KV = N_M[0] + NBLK[0]
        N_Q, N_O = N_KV + 1, N_KV + 3

        def w_at(n):
            return ring[:, n % RING]

        def w_wait(eng, n, i=0):
            eng.wait_ge(w_in[n % RING], i * 16 + 16 * (n // RING + 1))

        def flat(ap):
            return ap.rearrange("p a b -> p (a b)")

        def view(at, *shape):
            v = small[:, at:at + int(np.prod(shape))]
            if len(shape) == 1:
                return v
            names = "abc"[:len(shape)]
            return v.rearrange(f"p ({' '.join(names)}) -> p {' '.join(names)}", **dict(zip(names[1:], shape[1:])))

        sizes = dict(MASK=80, T1=5, TOP=5, EQ=20, OHG=20, EG=20, G44=80, SEL=20, M1=5, M2=5, OH1=20, OH2=20, DX=5,
                     MA=80, MB=80, W1=5, W2=5, PRE=96, C5=80, NB=16, Z16=16, INCL=16, EB=16 * MAXBLK, EBS=MAXBLK,
                     BASE=16, SL=80, SF=10)
        ends = np.cumsum([0] + list(sizes.values())).tolist()
        (MASK, T1, TOP, EQ, OHG, EG, G44, SEL, M1, M2, OH1, OH2, DX, MA, MB, W1, W2, PRE, C5, NB, Z16, INCL, EB, EBS,
         BASE, SL, SF) = ends[:-1]
        block = ctx.enter_context(nc.Block())

        def x_used(eng, l, j, i):
            if j == 0:
                b, n, per = fl.at[f"XF{l}"]
                _, nr, perr = fl.at[f"XT{l}r{RING - 1}"]
                assert nr - perr == n, (nr, perr, n)
                eng.wait_ge(full[b], i * perr + (n + 1))
            else:
                fl.wait_full(eng, f"XT{l}r{j - 1}", i)

        def head_pair(p):
            return (4 * (p // 2) + p % 2, 4 * (p // 2) + p % 2 + 2)

        def block_ready(eng, l, i, last_round):
            b, n, per = fl.at[f"XF{l}"]
            _, nr, perr = fl.at[f"XT{l}r{RING - 1}"]
            if last_round:
                i = NBLK[l] // RING - 1
            eng.wait_ge(free[b], i * perr + (n + 1))

        def masks(l):
            return small[:, 0:EXPERTS * 5]

        @block.sync
        def _(sp):
            def chunk(n, src):
                sp.dma_start(flat(w_at(n)), src).then_inc(w_in[n % RING], 16)

            for t in range(NT):
                sp.dma_start(h[:, t, :], a["x"][0, 128 * t:128 * t + 128, :]).then_inc(s_x, 16)
            for j in range(RING):
                chunk(j, a["w_ret"][0, j])
            with sp.Fori(0, HEADS - 1) as i:
                for j, last in ((0, "K2"), (1, "V4"), (2, "G3")):
                    fl.wait_full(sp, last, i)
                    nxt = a["w_ret"][1:HEADS]
                    chunk_src = nxt[bass.ds(i, 1), j].rearrange("a p c -> p (a c)")
                    chunk(j, chunk_src)
            for j, last in ((0, "K2"), (1, "V4"), (2, "G3")):
                fl.wait_full(sp, last, HEADS - 1)
                chunk(N_WO + j, a["w_ret_out"][j])
            sp.wait_ge(wo_first, 1)
            chunk(N_WO + 3, a["w_ret_out"][3])

            def experts(l):
                m = mo[l]
                gu_d, dn_d = a["w_gu"][l], a["w_down"][l]
                sp.wait_ge(m["eb_ready"], 1)
                sp.wait_ge(m["scattered"], 16 * 2 * (5 - l))

                def loads(b_of_slots, j, before):
                    e = sp.value_load(eb_i[0:1, l, b_of_slots], min_val=0, max_val=EXPERTS - 1)
                    before("gu")
                    chunk(N_M[l] + j, gu_d[bass.ds(e, 1)].rearrange("a p c -> p (a c)"))
                    before("x")
                    sp.dma_start(xg[:, j, :], rows_of(slot_rows, j, b_of_slots)).then_inc(m[f"x_in{j}"], 16)
                    before("down")
                    sp.dma_start(flat(down[:, j]), dn_d[bass.ds(e, 1)].rearrange("a p c -> p (a c)"))\
                        .then_inc(m[f"down_in{j}"], 16)

                def rows_of(table, j, b_of_slots):
                    if isinstance(b_of_slots, slice):
                        return table[b_of_slots.start * BLK:b_of_slots.stop * BLK, :]
                    v = table[BLK * RING:, :].rearrange("(i j p) c -> i j p c", j=RING, p=BLK)
                    return v[bass.ds(loop_i[0], 1), j].rearrange("a p c -> p (a c)")

                loop_i = [None]
                for j in range(RING):
                    loads(slice(j, j + 1), j, lambda what: None)
                rounds = NBLK[l] // RING
                with sp.Fori(0, rounds - 1) as i:
                    loop_i[0] = i
                    for j in range(RING):
                        def reuse(what, j=j, i=i):
                            if what == "gu":
                                fl.wait_full(sp, f"GU{l}r{j}", i)
                            elif what == "x":
                                x_used(sp, l, j, i)
                            else:
                                fl.wait_full(sp, f"YB{l}r{j}", i)
                        loads(bass.ds(i * RING + (RING + j), 1), j, reuse)

            experts(0)
            for n, last, src in ((N_KV, 0, a["w_kv"][0]), (N_Q, 1, a["w_q"][0]), (N_Q + 1, 2, a["w_q"][1])):
                fl.wait_full(sp, f"GU0z{last}")
                chunk(n, src)
            sp.wait_ge(mo[0]["gath_used"], 5)
            for dst, src in ((stab, a["t_swa"]), (sink_b, a["swa_sinks"][0].partition_broadcast(128)),
                             (kvb, a["kv_b"].partition_broadcast(128)),
                             (qb, a["swa_b_q"][0].partition_broadcast(128)),
                             (bo, a["swa_b_o"][0].partition_broadcast(128))):
                sp.dma_start(dst, src).then_inc(s_swat, 16)
            fl.wait_full(sp, f"KV{TILES5[-1]}")
            chunk(N_O, a["w_o"][0])
            sp.dma_start(flat(wo_b), a["w_o"][1]).then_inc(wo_b_in, 16)
            experts(1)
            sp.wait_ge(mo[1]["gath_used"], NT)
            sp.dma_start(fin_g, a["final_norm"].partition_broadcast(128)).then_inc(fin_in, 16)
            for t in range(NT):
                sp.wait_ge(fin_done, t + 1)
                sp.dma_start(out[0, 128 * t:128 * t + 128, :], fo[:, t, :]).then_inc(s_out, 16)
            sp.wait_ge(s_out, 16 * NT)

        @block.tensor
        def _(pe):
            mm = nc.tensor.matmul

            def transposed(tag, tiles, src, sig):
                for n, t in enumerate(tiles):
                    r, b = rows(t), fl.bank(f"{tag}{t}")
                    fl.wait_free(pe, f"{tag}{t}")
                    pe.wait_ge(sig["xn_done"], n + 1)
                    for k in range(KT):
                        last = nc.tensor.transpose(ps[:, b + k // 4, 128 * (k % 4):128 * (k % 4) + r],
                                                   src[0:r, t, 128 * k:128 * k + 128], ident[0:r, 0:r])
                    last.then_inc(full[b], 1)

            pe.wait_ge(s_const, 16)
            transposed("n0_", TILES5, ret_xn, nrm["_r"])
            for t in TILES5:
                fl.wait_read(pe, f"n0_{t}")
            with pe.Fori(0, HEADS) as i:
                for m, name in enumerate(("Q1", "Q2", "K1", "K2")):
                    b = fl.bank(name)
                    fl.wait_free(pe, name, i)
                    if m == 0:
                        w_wait(pe, 0, i)
                    for g in range(2):
                        for k in range(KT):
                            last = mm(ps[:, b + g, 0:HALF], w_at(0)[:, k, 128 * m:128 * m + 128],
                                      xT[:, k, HALF * g:HALF * g + HALF], start=(k == 0), stop=(k == KT - 1))
                    last.then_inc(full[b], 1)
                w_wait(pe, 1, i)
                for name, tiles in (("V01", (0, 1)), ("V23", (2, 3)), ("V4", (META,))):
                    b = fl.bank(name)
                    fl.wait_free(pe, name, i)
                    for g, t in enumerate(tiles):
                        for k in range(KT):
                            last = mm(ps[0:rows(t), b + g, :], xT[:, k, col0(t):col0(t) + rows(t)],
                                      w_at(1)[:, k, :], start=(k == 0), stop=(k == KT - 1))
                    last.then_inc(full[b], 1)
                w_wait(pe, 2, i)
                for m in range(4):
                    b = fl.bank(f"G{m}")
                    fl.wait_free(pe, f"G{m}", i)
                    for g in range(2):
                        for k in range(KT):
                            last = mm(ps[:, b + g, 0:HALF], w_at(2)[:, k, 128 * m:128 * m + 128],
                                      xT[:, k, HALF * g:HALF * g + HALF], start=(k == 0), stop=(k == KT - 1))
                    last.then_inc(full[b], 1)
                pe.wait_ge(q_ready, i * 2 + 2)
                pe.wait_ge(k_ready, i * 2 + 2)
                b = fl.bank("SM")
                fl.wait_free(pe, "SM", i)
                for g in range(2):
                    for k in range(2):
                        last = mm(ps[0:N_META, b + g, 0:HALF], kT[:, k, 0:N_META],
                                  qT[:, k, HALF * g:HALF * g + HALF], start=(k == 0), stop=(k == 1))
                last.then_inc(full[b], 1)
                for name, tiles in (("S01", (0, 1)), ("S23", (2, 3))):
                    b = fl.bank(name)
                    fl.wait_free(pe, name, i)
                    for g, t in enumerate(tiles):
                        for k in range(2):
                            last = mm(ps[:, b + g, 0:POS - col0(t)], kT[:, k, col0(t):col0(t) + 128],
                                      qT[:, k, col0(t):POS], start=(k == 0), stop=(k == 1))
                    last.then_inc(full[b], 1)
                for name in ("V01", "V23", "V4", "SM", "S01", "S23"):
                    fl.wait_read(pe, name, i)
                for m in range(4):
                    b = fl.bank(f"O{m}")
                    fl.wait_free(pe, f"O{m}", i)
                    for g in range(2):
                        lo, hi = HALF * g, HALF * g + HALF
                        tiles = [t for t in range(NT) if col0(t) < hi]
                        mm(ps[:, b + g, 0:HALF], v_tm[0:N_META, META, 128 * m:128 * m + 128],
                           s_meta[0:N_META, lo:hi], start=True, stop=False)
                        for t in tiles:
                            c = max(col0(t), lo)
                            last = mm(ps[:, b + g, c - lo:HALF], v_tm[:, t, 128 * m:128 * m + 128],
                                      s_t[:, t, c - col0(t):hi - col0(t)], start=False, stop=(t == tiles[-1]))
                    last.then_inc(full[b], 1)
                for name, src in (("MU", o_fm), ("VAR", sq)):
                    b = fl.bank(name)
                    fl.wait_free(pe, name, i)
                    if name == "MU":
                        for m in range(4):
                            fl.wait_read(pe, f"O{m}", i)
                    else:
                        pe.wait_ge(squared, i + 1)
                    for g in range(2):
                        for m in range(4):
                            last = mm(ps[:, b + g, 0:HALF], mean512, src[:, m, HALF * g:HALF * g + HALF],
                                      start=(m == 0), stop=(m == 3))
                    last.then_inc(full[b], 1)
            pe.wait_ge(y_ready, HEADS)
            for hf in range(2):
                groups = ((f"W{hf}_01", (0, 1)), (f"W{hf}_23", (2, 3)), (f"W{hf}_4", (META,)))
                for c in range(2):
                    n = N_WO + 2 * hf + c
                    w_wait(pe, n)
                    for name, tiles in groups:
                        b = fl.bank(name)
                        if c == 0:
                            fl.wait_free(pe, name)
                        for g, t in enumerate(tiles):
                            for k in range(KT):
                                last = mm(ps[0:rows(t), b + g, :], yT[:, KT * c + k, col0(t):col0(t) + rows(t)],
                                          w_at(n)[:, k, :], start=(c == 0 and k == 0), stop=(c == 1 and k == KT - 1))
                        if c == 1:
                            last.then_inc(full[b], 1)
                    if c == 0:
                        last.then_inc(wo_first, 1)

            def experts(l):
                m, tiles = mo[l], TILES5[l:]
                transposed(f"m{l}_", tiles, xn, nrm[f"_m{l}"])
                for t in tiles:
                    fl.wait_read(pe, f"m{l}_{t}")
                for t in tiles:
                    for k in range(KT):
                        last = mm(ps[0:rows(t), 0, 20 * t:20 * t + 20], xT[:, k, col0(t):col0(t) + rows(t)],
                                  wr[:, l, k, :], start=(k == 0), stop=(k == KT - 1))
                last.then_inc(full[0], 1)
                n = EXPERTS * (5 - l)
                pe.wait_ge(m["mask_ready"], 1)
                mm(ps[:, 2, 0:n], tri, masks(l)[:, 0:n], start=True, stop=True)
                mm(ps[:, 2, 128:128 + n], ones, masks(l)[:, 0:n], start=True, stop=True).then_inc(full[2], 1)
                all_read(pe, t_blocks[l])

                def transpose_block(name, j, i, xj):
                    fl.wait_free(pe, name, i)
                    for k in range(KT):
                        last = nc.tensor.transpose(ps[:, k // 4, 128 * (k % 4):128 * (k % 4) + 128],
                                                   xg[:, xj, 128 * k:128 * k + 128], ident)
                    last.then_inc(full[0], 1)

                def a_round(z, i, last_round):
                    for j in range(RING):
                        n = N_M[l] + j
                        if last_round:
                            n += NBLK[l] - RING
                        if j == 0:
                            block_ready(pe, l, i, last_round)
                        else:
                            fl.wait_read(pe, f"XT{l}{z}{j - 1}", i)
                        w_wait(pe, n, i)
                        fl.wait_free(pe, f"GU{l}{z}{j}", i)
                        for k in range(KT):
                            last = mm(ps[:, 2 + j, :], xgT[:, j, k, :], w_at(N_M[l] + j)[:, k, :],
                                      start=(k == 0), stop=(k == KT - 1))
                        last.then_inc(full[2 + j], 1)
                        if not (last_round and j == RING - 1):
                            jn = (j + 1) % RING
                            rnd = (NBLK[l] // RING - 1) if last_round else i
                            pe.wait_ge(m[f"x_in{jn}"], rnd * 16 + (16 if jn else 32))
                            transpose_block(f"XT{l}{z}{j}", j, i, jn)
                        fl.wait_free(pe, f"HT{l}{z}{j}", i)
                        fl.wait_read(pe, f"GU{l}{z}{j}", i)
                        for k in range(2):
                            last = nc.tensor.transpose(ps[:, 5, 128 * k:128 * k + 128],
                                                       hid[:, 128 * k:128 * k + 128], ident)
                        last.then_inc(full[5], 1)
                        rnd = (NBLK[l] // RING - 1) if last_round else i
                        pe.wait_ge(m[f"down_in{j}"], rnd * 16 + 16)
                        fl.wait_read(pe, f"HT{l}{z}{j}", i)
                        for c, x in enumerate(("YA", "YB")):
                            fl.wait_free(pe, f"{x}{l}{z}{j}", i)
                            for k in range(2):
                                last = mm(ps[:, 6 + c, :], hidT[:, k, :], down[:, j, k, 512 * c:512 * c + 512],
                                          start=(k == 0), stop=(k == 1))
                            last.then_inc(full[6 + c], 1)

                pe.wait_ge(m["x_in0"], 16)
                transpose_block(f"XF{l}", 0, 0, 0)
                with pe.Fori(0, NBLK[l] // RING - 1) as i:
                    a_round("r", i, False)
                a_round("z", 0, True)

            experts(0)

            all_read(pe, t_blocks_end[0])
            transposed("n1_", TILES5, xn1, nrm["_s"])
            w_wait(pe, N_KV)
            all_read(pe, t_norm1)
            for t in TILES5:
                b = fl.bank(f"KV{t}")
                fl.wait_free(pe, f"KV{t}")
                for k in range(KT):
                    last = mm(ps[0:rows(t), b, :], xTk[:, k, col0(t):col0(t) + rows(t)], w_at(N_KV)[:, k, :],
                              start=(k == 0), stop=(k == KT - 1))
                last.then_inc(full[b], 1)
            for n, t in enumerate(TILES5):
                b, r = fl.bank(f"KT{t}"), rows(t)
                fl.wait_free(pe, f"KT{t}")
                pe.wait_ge(kr_ready, n + 1)
                for j in range(KV_HEADS):
                    last = nc.tensor.transpose(ps[:, b, 128 * j:128 * j + r], kr[0:r, n % 2, j, :], ident[0:r, 0:r])
                last.then_inc(full[b], 1)
            all_read(pe, t_kv)

            def project_q(t):
                for c, name in enumerate((f"Qa{t}", f"Qb{t}")):
                    w_wait(pe, N_Q + c)
                    fl.wait_free(pe, name)
                    for k in range(KT):
                        last = mm(ps[:, 4 + c, :], xT[:, k, col0(t):col0(t) + 128], w_at(N_Q + c)[:, k, :],
                                  start=(k == 0), stop=(k == KT - 1))
                    last.then_inc(full[4 + c], 1)

            def transpose_q(t):
                fl.wait_free(pe, f"QT{t}")
                pe.wait_ge(q_rot, t + 1)
                for k in range(KT):
                    last = nc.tensor.transpose(ps[:, k // 4, 128 * (k % 4):128 * (k % 4) + 128],
                                               qr[:, 128 * k:128 * k + 128], ident)
                last.then_inc(full[0], 1)

            project_q(0)
            transpose_q(0)
            for t in range(NT):
                fl.wait_read(pe, f"QT{t}")
                prev = col0(t) - CHUNK if t else 0
                for p in range(8):
                    b = fl.bank(f"S{t}_{p}")
                    fl.wait_free(pe, f"S{t}_{p}")
                    for g, hd in enumerate(head_pair(p)):
                        o = 64 * (hd % 2)
                        q = qT1[o:o + 64, hd // 2, :]
                        for at, c, n in ((0, col0(t), 128), (128, 0, CHUNK), (128 + CHUNK, prev, CHUNK)):
                            last = mm(ps[:, b, 256 * g + at:256 * g + at + n], q,
                                      kT2[o:o + 64, hd // 4, c:c + n], start=True, stop=True)
                    last.then_inc(full[b], 1)
                if t + 1 < NT:
                    project_q(t + 1)
                fl.wait_free(pe, f"AV{t}")

                def weigh(p):
                    fl.wait_read(pe, f"PT{t}_{p}")
                    for g in range(2):
                        hd = 2 * p + g
                        dst = ps[:, 6 + hd // 8, 64 * (hd % 8):64 * (hd % 8) + 64]
                        j = 64 * (hd // 4)
                        mm(dst, PT[:, p % 2, 2 * g, :], V[:, t, j:j + 64], start=True, stop=False)
                        last = mm(dst, PT[:, p % 2, 2 * g + 1, :], VX[:, t, j:j + 64], start=False, stop=True)
                    if p == 7:
                        last.then_inc(full[6], 1)

                if t == 0:
                    pe.wait_ge(V_ready, 5)
                    pe.wait_ge(VX_ready, 2 * NT - 1)
                for p in range(8):
                    b = fl.bank(f"PT{t}_{p}")
                    fl.wait_free(pe, f"PT{t}_{p}")
                    pe.wait_ge(p_exp, 16 * t + 2 * p + 2)
                    for g in range(2):
                        for c in range(2):
                            last = nc.tensor.transpose(ps[:, b, 128 * (2 * g + c):128 * (2 * g + c) + 128],
                                                       P[:, 2 * p + g, 128 * c:128 * c + 128], ident)
                    last.then_inc(full[b], 1)
                    if p:
                        weigh(p - 1)
                weigh(7)
                if t + 1 < NT:
                    transpose_q(t + 1)
                fl.wait_free(pe, f"OT{t}")
                fl.wait_read(pe, f"AV{t}")
                for k in range(KT):
                    last = nc.tensor.transpose(ps[:, 2 + k // 4, 128 * (k % 4):128 * (k % 4) + 128],
                                               oN[:, 128 * k:128 * k + 128], ident)
                last.then_inc(full[2], 1)
                fl.wait_free(pe, f"WO{t}")
                if t + 1 < NT:
                    fl.wait_read(pe, f"Qb{t + 1}")
                fl.wait_read(pe, f"OT{t}")
                w_wait(pe, N_O)
                pe.wait_ge(wo_b_in, 16)
                for c, w in enumerate((w_at(N_O), wo_b)):
                    for k in range(KT):
                        last = mm(ps[:, 4 + c, :], oT1[:, k, :], w[:, k, :],
                                  start=(k == 0), stop=(k == KT - 1))
                last.then_inc(full[4], 1)
            all_read(pe, t_swa)
            experts(1)

        @block.scalar
        def _(act):
            def squares(tiles, sig, junk, ready):
                for n, t in enumerate(tiles):
                    ready(t)
                    r = rows(t)
                    if n:
                        act.wait_ge(sig["sq_done"], n)
                    nc.scalar.activation(junk[0:r], h[0:r, t, :], ACT.Square,
                                         accum_out=ss[0:r, t:t + 1]).then_inc(sig["sq_done"], 1)

            act.dma_start(h[0:N_META, META, :], a["meta_tokens"]).then_inc(s_x, 16)
            act.dma_start(con[:, :], a["t_con"]).then_inc(s_const, 16)
            act.dma_start(flat(gains[:, :, :]), a["gains"]).then_inc(s_gains, 16)
            act.dma_start(wr[:, :, :, :].rearrange("p a b c -> p (a b c)"), a["w_route"]).then_inc(s_gains, 16)
            act.dma_start(arena[:, 16 * POS:16 * POS + NRT], a["t_ret"]).then_inc(s_rt, 16)
            act.wait_ge(s_zero, 1)
            act.dma_start(slot_rows.rearrange("(b p) c -> p b c", p=128),
                          zero.unsqueeze(1).to_broadcast([128, MAXBLK, D])).then_inc(s_zeroed, 16)
            act.wait_ge(s_init, 1)
            act.wait_ge(s_x, 80)
            squares(TILES5, nrm["_r"], ret_junk, lambda t: None)
            with act.Fori(0, HEADS) as i:
                for name, t, n in (("V01", 0, 2), ("V23", 2, 2)):
                    b = fl.bank(name)
                    fl.wait_full(act, name, i)
                    nc.scalar.activation(v_tm[:, t:t + n, :], ps[:, b:b + 2, :], ACT.Copy).then_inc(free[b], 1)
                b = fl.bank("V4")
                fl.wait_full(act, "V4", i)
                nc.scalar.activation(v_tm[0:N_META, META, :], ps[0:N_META, b, :], ACT.Copy).then_inc(free[b], 1)
                for m in range(4):
                    fl.wait_full(act, f"G{m}", i)
                    nc.scalar.activation(halves(gate_t[:, m, :]), pair(fl.bank(f"G{m}")), ACT.Tanh, scale=0.5)\
                        .then_inc(gt_done, 1)
                for m in range(4):
                    fl.wait_full(act, f"O{m}", i)
                    nc.scalar.activation(halves(o_fm[:, m, :]), pair(fl.bank(f"O{m}")), ACT.Copy)\
                        .then_inc(free[fl.bank(f"O{m}")], 1)
                fl.wait_read(act, "MU", i)
                nc.scalar.activation(flat(sq), flat(o_fm), ACT.Square).then_inc(squared, 1)
                fl.wait_full(act, "VAR", i)
                nc.scalar.activation(halves(vr), pair(fl.bank("VAR")), ACT.Copy, bias=EPS)\
                    .then_inc(free[fl.bank("VAR")], 1)

            def experts(l, ready):
                m = mo[l]
                squares(TILES5[l:], nrm[f"_m{l}"], xg[:, 0, :], ready)
                act.wait_ge(m["eg_in"], 1)
                nc.scalar.activation(view(EG, 5 - l, 4), view(EG, 5 - l, 4), ACT.Exp).then_inc(m["eg_out"], 1)
                act.wait_ge(m["d_in"], 1)
                nc.scalar.activation(view(DX, 5 - l), view(DX, 5 - l), ACT.Exp).then_inc(m["d_out"], 1)

                def a_round(z, i, last_round):
                    rnd = (NBLK[l] // RING - 1) if last_round else i
                    for j in range(RING):
                        fl.wait_full(act, f"GU{l}{z}{j}", i)
                        nc.scalar.activation(th, ps[:, 2 + j, 0:FF], ACT.Tanh, scale=0.5).then_inc(m["tanh_done"], 1)
                        fl.wait_full(act, f"HT{l}{z}{j}", i)
                        nc.scalar.activation(flat(hidT), ps[:, 5, 0:FF], ACT.Copy).then_inc(free[5], 1)
                        fl.wait_full(act, f"YA{l}{z}{j}", i)
                        act.wait_ge(m[f"y_out{j}"], rnd * 16 + 16)
                        nc.scalar.activation(yo[:, j, 0:512], ps[:, 6, :], ACT.Copy).then_inc(free[6], 1)
                        fl.wait_read(act, f"YA{l}{z}{j}", i)
                        fl.wait_read(act, f"YB{l}{z}{j}", i)
                        if last_round:
                            b = NBLK[l] - RING + j
                            dst = slot_out[b * BLK:b * BLK + BLK, :]
                        else:
                            dst = slot_out[0:(NBLK[l] - RING) * BLK, :].rearrange(
                                "(i j p) c -> i j p c", j=RING, p=BLK)[bass.ds(i, 1), j].rearrange("a p c -> p (a c)")
                        act.dma_start(dst, yo[:, j, :]).then_inc(m[f"y_out{j}"], 16)

                with act.Fori(0, NBLK[l] // RING - 1) as i:
                    a_round("r", i, False)
                a_round("z", 0, True)

            def after_retention(t):
                for hf in range(2):
                    fl.wait_read(act, f"W{hf}_4" if t == META else f"W{hf}_{'01' if t < 2 else '23'}")

            experts(0, after_retention)
            squares(TILES5, nrm["_s"], swa_junk, lambda t: act.wait_ge(mo[0]["gath_used"], TILES5.index(t) + 1))
            for n, t in enumerate(TILES5):
                b, r = fl.bank(f"KT{t}"), rows(t)
                fl.wait_full(act, f"KT{t}")
                nc.scalar.activation(kT2[:, :, col0(t):col0(t) + r],
                                     ps[:, b, :].rearrange("p (j c) -> p j c", j=4)[:, :, 0:r], ACT.Copy)\
                    .then_inc(free[b], 1)

            def q_out(t):
                fl.wait_full(act, f"QT{t}")
                nc.scalar.activation(flat(qT1), flat(ps[:, 0:2, :]), ACT.Copy).then_inc(free[0], 1)

            q_out(0)
            for t in range(NT):
                for g in range(2):
                    act.wait_ge(m_ready, 2 * t + g + 1)
                    for hd in range(8 * g, 8 * g + 8):
                        nc.scalar.activation(P[:, hd, :], P[:, hd, :], ACT.Exp, bias=nmx[:, hd:hd + 1],
                                             accum_out=sm[:, hd:hd + 1]).then_inc(p_exp, 1)
                    nc.scalar.activation(sx[:, 8 * g:8 * g + 8], es[:, 8 * g:8 * g + 8], ACT.Exp).then_inc(snk_exp, 1)
                for p in range(1, 8, 2):
                    b = fl.bank(f"PT{t}_{p}")
                    fl.wait_full(act, f"PT{t}_{p}")
                    nc.scalar.activation(flat(PT[:, 1]), ps[:, b, :], ACT.Copy).then_inc(free[b], 1)
                if t + 1 < NT:
                    q_out(t + 1)
                fl.wait_full(act, f"OT{t}")
                nc.scalar.activation(flat(oT1), flat(ps[:, 2:4, :]), ACT.Copy).then_inc(free[2], 1)
            experts(1, lambda t: fl.wait_read(act, f"WO{t}"))
            squares(TILES5[1:], nrm["_f"], fin_junk, lambda t: act.wait_ge(mo[1]["gath_used"], TILES5.index(t)))

        @block.vector
        def _(dve):
            V_ = nc.vector

            def norm(tiles, sig, dst):
                dve.wait_ge(sig["sq_done"], len(tiles))
                V_.tensor_scalar(var[:, :], ss[:, :], 1.0 / D, EPS, ALU.mult, ALU.add).then_inc(sig["var_done"], 1)
                dve.wait_ge(sig["rstd_done"], 1)
                for t in tiles:
                    r = rows(t)
                    V_.tensor_scalar(dst[0:r, t, :], h[0:r, t, :], rstd[0:r, t:t + 1], None, ALU.mult)\
                        .then_inc(sig["xn_done"], 1)

            def gained(dst, b, g, gain, c0, r, j=None):
                src = ps[:, b + g, :].rearrange("p (k c) -> p k c", k=4)[:, :, 0:r]
                return V_.tensor_tensor(dst[:, 4 * g:4 * g + 4, c0:c0 + r], src,
                                        gains[:, gain, 4 * g:4 * g + 4].unsqueeze(2).to_broadcast([128, 4, r]), ALU.mult)

            def feature_major(tag, tiles, gain):
                for t in tiles:
                    b = fl.bank(f"{tag}{t}")
                    fl.wait_full(dve, f"{tag}{t}")
                    gained(xT, b, 0, gain, col0(t), rows(t))
                    gained(xT, b, 1, gain, col0(t), rows(t)).then_inc(free[b], 1)

            V_.memset(ss[:, :], 1.0).then_inc(s_init, 1)
            V_.memset(zero, 0.0).then_inc(s_zero, 1)
            dve.wait_ge(s_x, 80)
            norm(TILES5, nrm["_r"], ret_xn)
            dve.wait_ge(s_gains, 32)
            feature_major("n0_", TILES5, G_RET)
            dve.wait_ge(s_rt, 16)
            step = Steps(dve, dsem["r"])
            tmp = [sq[:, n, :] for n in range(4)]
            with dve.Fori(0, HEADS) as i:
                step.rounds(i, 3)
                for lo, hi, dst, sig in (("Q1", "Q2", qT, q_ready), ("K1", "K2", kT, k_ready)):
                    bl, bh = fl.bank(lo), fl.bank(hi)
                    fl.wait_full(dve, lo, i)
                    V_.tensor_tensor(halves(tmp[0]), pair(bl), halves(rope_c), ALU.mult)
                    fl.wait_full(dve, hi, i)
                    step.done(V_.tensor_tensor(halves(tmp[1]), pair(bh), halves(rope_s), ALU.mult))
                    V_.tensor_tensor(halves(tmp[2]), pair(bh), halves(rope_c), ALU.mult).then_inc(free[bh], 1)
                    V_.tensor_tensor(halves(tmp[3]), pair(bl), halves(rope_s), ALU.mult).then_inc(free[bl], 1)
                    step.wait()
                    V_.tensor_tensor(dst[:, 0, :], tmp[0], tmp[1], ALU.subtract).then_inc(sig, 1)
                    fl.wait_read(dve, hi, i)
                    fl.wait_read(dve, lo, i)
                    V_.tensor_tensor(dst[:, 1, :], tmp[2], tmp[3], ALU.add).then_inc(sig, 1)
                    dve.wait_ge(sig, i * 2 + 2)
                for m in range(4):
                    b = fl.bank(f"G{m}")
                    dve.wait_ge(gt_done, i * 4 + (m + 1))
                    V_.scalar_tensor_tensor(halves(gate[:, m, :]), halves(gate_t[:, m, :]), 1.0, pair(b),
                                            ALU.add, ALU.mult).then_inc(free[b], 1)
                dec = decay[:, bass.ds(i, 1), :].rearrange("p a c -> p (a c)")
                fl.wait_full(dve, "SM", i)
                V_.tensor_tensor(halves(s_meta[0:N_META, :]), pair(fl.bank("SM"))[0:N_META], halves(dec[0:N_META, :]),
                                 ALU.mult).then_inc(free[fl.bank("SM")], 1)
                for name, tiles in (("S01", (0, 1)), ("S23", (2, 3))):
                    b = fl.bank(name)
                    fl.wait_full(dve, name, i)
                    for g, t in enumerate(tiles):
                        n = POS - col0(t)
                        last = V_.tensor_tensor(s_t[:, t, 0:n], ps[:, b + g, 0:n], dec[:, 0:n], ALU.mult)
                    last.then_inc(free[b], 1)
                fl.wait_full(dve, "MU", i)
                mu = pair(fl.bank("MU"))
                for m in range(4):
                    last = V_.tensor_tensor(halves(o_fm[:, m, :]), halves(o_fm[:, m, :]), mu, ALU.subtract)
                last.then_inc(free[fl.bank("MU")], 1)
                dve.wait_ge(rs_ready, i + 1)
                for m in range(4):
                    last = V_.tensor_tensor(o_fm[:, m, :], o_fm[:, m, :], rs, ALU.mult)
                step(last)
                dst = yT[:, bass.ds(i * 4, 4), :]
                V_.scalar_tensor_tensor(dst, o_fm, 0.5, gate, ALU.mult, ALU.mult).then_inc(y_ready, 1)
            step.end(HEADS)
            for hf in range(2):
                for name, t, n in ((f"W{hf}_01", 0, 2), (f"W{hf}_23", 2, 2)):
                    b = fl.bank(name)
                    fl.wait_full(dve, name)
                    hh = h[:, t:t + n, 512 * hf:512 * hf + 512]
                    V_.tensor_tensor(hh, ps[:, b:b + 2, :], hh, ALU.add).then_inc(free[b], 1)
                b = fl.bank(f"W{hf}_4")
                fl.wait_full(dve, f"W{hf}_4")
                hh = h[0:N_META, META, 512 * hf:512 * hf + 512]
                V_.tensor_tensor(hh, ps[0:N_META, b, :], hh, ALU.add).then_inc(free[b], 1)

            def experts(l):
                m, tiles, nt, t0 = mo[l], TILES5[l:], 5 - l, 0
                fl.wait_read(dve, "W1_4" if l == 0 else f"WO{NT - 1}")
                step = Steps(dve, dsem_m[l])
                if l == 0:
                    step.done(V_.memset(lg[:, META, :], 0.0))
                norm(tiles, nrm[f"_m{l}"], xn)
                feature_major(f"m{l}_", tiles, G_MOE[l])
                fl.wait_full(dve, f"LG{l}")
                if l == 0:
                    step.wait()
                    V_.tensor_copy(lg[0:N_META, META, :], ps[0:N_META, 0, 20 * META:20 * META + 20])
                V_.tensor_copy(flat(lg[:, 0:NT, :]), ps[:, 0, 0:20 * NT]).then_inc(free[0], 1)
                fl.wait_read(dve, f"LG{l}")
                g, e = lg[:, 0:nt, 0:GROUPS], lg[:, 0:nt, GROUPS:20]
                ge = e.rearrange("p t (g e) -> p t g e", g=GROUPS)
                rev = con[:, C_REV:C_REV + 4].unsqueeze(1).to_broadcast([128, nt, 4])

                def v(at, *shape):
                    return view(at, *shape)

                def over4(x):
                    return x.unsqueeze(2).to_broadcast([128, nt, 4])

                def first_max(src, top, eq, one):
                    step(V_.tensor_reduce(top, src, X, ALU.max))
                    step(V_.tensor_tensor(eq, src, over4(top), ALU.is_ge))
                    step(V_.tensor_tensor(eq, eq, rev, ALU.mult))
                    step(V_.tensor_reduce(v(T1, nt), eq, X, ALU.max))
                    step(V_.tensor_tensor(one, eq, over4(v(T1, nt)), ALU.is_equal))

                first_max(g, v(TOP, nt), v(EQ, nt, 4), v(OHG, nt, 4))
                V_.tensor_tensor(v(EG, nt, 4), g, over4(v(TOP, nt)), ALU.subtract).then_inc(m["eg_in"], 1)
                g4 = v(G44, nt, 4, 4)
                for t in range(nt):
                    last = V_.tensor_tensor(g4[:, t], ge[:, t],
                                            v(OHG, nt, 4)[:, t].unsqueeze(2).to_broadcast([128, 4, 4]), ALU.mult)
                step(last)
                step(V_.tensor_reduce(v(SEL, nt, 4), g4.rearrange("p t g e -> p t e g"), X, ALU.add))
                first_max(v(SEL, nt, 4), v(M1, nt), v(EQ, nt, 4), v(OH1, nt, 4))
                step(V_.scalar_tensor_tensor(v(SEL, nt, 4), v(OH1, nt, 4), -1e30, v(SEL, nt, 4), ALU.mult, ALU.add))
                first_max(v(SEL, nt, 4), v(M2, nt), v(EQ, nt, 4), v(OH2, nt, 4))
                V_.tensor_tensor(v(DX, nt), v(M2, nt), v(M1, nt), ALU.subtract).then_inc(m["d_in"], 1)
                if l == 0:
                    step(V_.tensor_tensor(v(OHG, nt, 4), v(OHG, nt, 4), over4(con[:, C_VALID:C_VALID + nt]), ALU.mult))
                for at, oh in ((MA, OH1), (MB, OH2)):
                    for t in range(nt):
                        last = V_.tensor_tensor(v(at, nt, 4, 4)[:, t],
                                                v(OHG, nt, 4)[:, t].unsqueeze(2).to_broadcast([128, 4, 4]),
                                                v(oh, nt, 4)[:, t].unsqueeze(1).to_broadcast([128, 4, 4]), ALU.mult)
                step(last)
                V_.tensor_tensor(masks(l)[:, 0:16 * nt], v(MA, 16 * nt), v(MB, 16 * nt), ALU.add)\
                    .then_inc(m["mask_ready"], 1)
                dve.wait_ge(m["eg_out"], 1)
                step(V_.tensor_reduce(v(T1, nt), v(EG, nt, 4), X, ALU.add))
                step(V_.reciprocal(v(TOP, nt), v(T1, nt)))
                dve.wait_ge(m["d_out"], 1)
                step(V_.tensor_scalar(v(T1, nt), v(DX, nt), 1.0, None, ALU.add))
                step(V_.reciprocal(v(T1, nt), v(T1, nt)))
                step(V_.tensor_tensor(v(W1, nt), v(TOP, nt), v(T1, nt), ALU.mult))
                step(V_.tensor_tensor(v(W2, nt), v(W1, nt), v(DX, nt), ALU.mult))
                fl.wait_full(dve, f"RK{l}")
                before = v(PRE, 6, 16)
                step(V_.memset(before[:, 0, :], 0.0))
                for t in range(nt):
                    step(V_.tensor_tensor(before[:, t + 1, :], ps[:, 2, 128 + 16 * t:144 + 16 * t], before[:, t, :], ALU.add))
                count = before[:, nt, :]
                step(V_.tensor_tensor(v(C5, 16, 5), count.unsqueeze(2).to_broadcast([128, 16, 5]),
                                      con[:, C_THR:C_THR + 5].unsqueeze(1).to_broadcast([128, 16, 5]), ALU.is_gt))
                step(V_.tensor_reduce(v(NB, 16), v(C5, 16, 5), X, ALU.add))
                step(V_.memset(v(Z16, 16), 0.0))
                step(V_.tensor_tensor_scan(v(INCL, 16), v(NB, 16), v(Z16, 16), 0.0, ALU.add, ALU.add))
                eb = v(EB, MAXBLK, 16)[0:1]
                step(V_.tensor_tensor(eb, v(INCL, 16)[0:1].unsqueeze(1).to_broadcast([1, MAXBLK, 16]),
                                      con[0:1, C_BLK:C_BLK + MAXBLK].unsqueeze(2).to_broadcast([1, MAXBLK, 16]), ALU.is_le))
                step(V_.tensor_reduce(v(EBS, MAXBLK)[0:1], eb, X, ALU.add))
                V_.tensor_scalar(eb_i[0:1, l, :], v(EBS, MAXBLK)[0:1], float(EXPERTS - 1), None, ALU.min)\
                    .then_inc(m["eb_ready"], 1)
                step(V_.tensor_tensor(v(BASE, 16), v(INCL, 16), v(NB, 16), ALU.subtract))
                step(V_.tensor_scalar(v(BASE, 16), v(BASE, 16), float(BLK), None, ALU.mult))
                sl = v(SL, nt, 16)
                V_.tensor_tensor(sl, ps[:, 2, 0:16 * nt].rearrange("p (t e) -> p t e", e=16), before[:, 0:nt, :],
                                 ALU.add).then_inc(free[2], 1)
                fl.wait_read(dve, f"RK{l}")
                step(V_.tensor_tensor(sl, sl, v(BASE, 16).unsqueeze(1).to_broadcast([128, nt, 16]), ALU.add))
                for n, at in enumerate((MA, MB)):
                    step(V_.tensor_tensor(v(at, nt, 16), v(at, nt, 16), sl, ALU.mult))
                    step(V_.tensor_reduce(v(SF, 2, 5)[:, n, 0:nt], v(at, nt, 16), X, ALU.add))
                V_.tensor_copy(slot_i[:, :, 0:nt], v(SF, 2, 5)[:, :, 0:nt]).then_inc(m["slot_ready"], 1)

                def widen(name, b, j, i):
                    fl.wait_full(dve, name, i)
                    for g in range(2):
                        src = ps[:, g, :].rearrange("p (k c) -> p k c", k=4)
                        last = V_.tensor_tensor(xgT[:, j, 4 * g:4 * g + 4, :], src,
                                                gains[:, G_MOE[l], 4 * g:4 * g + 4].unsqueeze(2)
                                                .to_broadcast([128, 4, 128]), ALU.mult)
                    last.then_inc(free[0], 1)

                def a_round(z, i, last_round):
                    rnd = (NBLK[l] // RING - 1) if last_round else i
                    for j in range(RING):
                        if last_round:
                            dve.wait_ge(m["tanh_done"], rnd * RING + j + 1)
                        else:
                            dve.wait_ge(m["tanh_done"], i * RING + (j + 1))
                        step(V_.scalar_tensor_tensor(hid1, th, 1.0, ps[:, 2 + j, 0:FF], ALU.add, ALU.mult))
                        V_.scalar_tensor_tensor(hid, hid1, 0.5, ps[:, 2 + j, FF:2 * FF], ALU.mult, ALU.mult)\
                            .then_inc(free[2 + j], 1)
                        if not (last_round and j == RING - 1):
                            widen(f"XT{l}{z}{j}", 0, (j + 1) % RING, i)
                        fl.wait_full(dve, f"YB{l}{z}{j}", i)
                        dve.wait_ge(m[f"y_out{j}"], rnd * 16 + 16)
                        V_.tensor_copy(yo[:, j, 512:1024], ps[:, 7, :]).then_inc(free[7], 1)

                for j in range(RING):
                    V_.memset(v(Z16, 16)[:, j:j + 1], 0.0).then_inc(m[f"y_out{j}"], 16)
                widen(f"XF{l}", 0, 0, 0)
                with dve.Fori(0, NBLK[l] // RING - 1) as i:
                    step.rounds(i, RING)
                    a_round("r", i, False)
                step.end(NBLK[l] // RING - 1)
                a_round("z", 0, True)
                for n, t in enumerate(tiles):
                    r = rows(t)
                    dve.wait_ge(m[f"gathered{n % 2}"], 32 * (n // 2 + 1))
                    step(V_.scalar_tensor_tensor(h[0:r, t, :], gat[0:r, n % 2, 0, :], v(W1, nt)[0:r, t:t + 1],
                                                 h[0:r, t, :], ALU.mult, ALU.add))
                    V_.scalar_tensor_tensor(h[0:r, t, :], gat[0:r, n % 2, 1, :], v(W2, nt)[0:r, t:t + 1],
                                            h[0:r, t, :], ALU.mult, ALU.add).then_inc(m["gath_used"], 1)

            experts(0)

            step = Steps(dve, dsem["a"])
            dve.wait_ge(mo[0]["gath_used"], 5)
            norm(TILES5, nrm["_s"], xn1)
            for t in TILES5:
                b = fl.bank(f"n1_{t}")
                fl.wait_full(dve, f"n1_{t}")
                for gx in range(2):
                    last = gained(xTk, b, gx, G_KV, col0(t), rows(t))
                if t != META:
                    for gx in range(2):
                        last = gained(xT, b, gx, G_SWA, col0(t), rows(t))
                last.then_inc(free[b], 1)
            dve.wait_ge(s_swat, 80)

            def rotate(x, t, r, nh, A_, B_, outs):
                cos = stab[0:r, 32 * t:32 * t + 32].unsqueeze(1)
                sin = stab[0:r, 160 + 64 * t:160 + 64 * t + 64]
                xv = x.rearrange("p (h c) -> p h c", c=32)
                step.done(V_.tensor_tensor(A_.rearrange("p (h c) -> p h c", c=32), xv,
                                           cos.to_broadcast([r, 2 * nh, 32]), ALU.mult))
                x4, b4 = (y.rearrange("p (h s c) -> p h s c", s=2, c=32) for y in (x, B_))
                for s in range(2):
                    step.done(V_.tensor_tensor(b4[:, :, s, :], x4[:, :, 1 - s, :],
                                               sin[:, 32 * s:32 * s + 32].unsqueeze(1).to_broadcast([r, nh, 32]), ALU.mult))
                step.wait()
                for o in outs:
                    last = V_.tensor_tensor(o, A_.rearrange("p (h c) -> p h c", c=64),
                                            B_.rearrange("p (h c) -> p h c", c=64), ALU.add)
                return last

            for n, t in enumerate(TILES5):
                b, r = fl.bank(f"KV{t}"), rows(t)
                fl.wait_full(dve, f"KV{t}")
                if n >= 2:
                    dve.wait_ge(V_ready, n - 1)
                V_.tensor_tensor(kvs[0:r, n % 2, :], ps[0:r, b, :], kvb[0:r, :], ALU.add).then_inc(free[b], 1)
                fl.wait_read(dve, f"KV{t}")
                if n >= 2:
                    fl.wait_full(dve, f"KT{TILES5[n - 2]}")
                if n:
                    dve.wait_ge(kr_ready, n)
                rotate(kvs[0:r, n % 2, 0:256], t, r, 4, flat(kA)[0:r], flat(kB)[0:r],
                       [kr[0:r, n % 2, :, 0:64], kr[0:r, n % 2, :, 64:128]]).then_inc(kr_ready, 1)

            def rotate_q(t):
                for c, name in enumerate((f"Qa{t}", f"Qb{t}")):
                    fl.wait_full(dve, name)
                    if c == 0 and t:
                        fl.wait_full(dve, f"QT{t - 1}")
                        dve.wait_ge(q_rot, t)
                    V_.tensor_tensor(qs[:, 512 * c:512 * c + 512], ps[:, 4 + c, :], qb[:, 512 * c:512 * c + 512],
                                     ALU.add).then_inc(free[4 + c], 1)
                fl.wait_read(dve, f"Qa{t}")
                fl.wait_read(dve, f"Qb{t}")
                rotate(qs, t, 128, 16, qA, qr, [qr.rearrange("p (h c) -> p h c", c=64)]).then_inc(q_rot, 1)

            rotate_q(0)
            for t in range(NT):
                mask = stab[:, 480 + 256 * min(t, 1):480 + 256 * min(t, 1) + 256].unsqueeze(1).to_broadcast([128, 2, 256])
                for g in range(2):
                    for p in range(4 * g, 4 * g + 4):
                        b = fl.bank(f"S{t}_{p}")
                        fl.wait_full(dve, f"S{t}_{p}")
                        h0 = head_pair(p)[0]
                        V_.scalar_tensor_tensor(P[:, h0:h0 + 3:2, :], ps[:, b, :].rearrange("p (h k) -> p h k", h=2),
                                                HD ** -0.5, mask, ALU.mult, ALU.add).then_inc(free[b], 1)
                        fl.wait_read(dve, f"S{t}_{p}")
                        step.done(V_.tensor_reduce(mx[:, h0:h0 + 3:2], P[:, h0:h0 + 3:2, :], X, ALU.max))
                    step.wait()
                    c = slice(8 * g, 8 * g + 8)
                    step(V_.tensor_tensor(mx[:, c], mx[:, c], sink_b[:, c], ALU.max))
                    if t:
                        dve.wait_ge(p_exp, 16 * t)
                        dve.wait_ge(snk_exp, 2 * t)
                    step(V_.tensor_tensor(es[:, c], sink_b[:, c], mx[:, c], ALU.subtract))
                    V_.tensor_scalar(nmx[:, c], mx[:, c], -1.0, None, ALU.mult).then_inc(m_ready, 1)
                if t + 1 < NT:
                    rotate_q(t + 1)
                for p in range(0, 8, 2):
                    b = fl.bank(f"PT{t}_{p}")
                    fl.wait_full(dve, f"PT{t}_{p}")
                    V_.tensor_copy(flat(PT[:, 0]), ps[:, b, :]).then_inc(free[b], 1)
                dve.wait_ge(snk_exp, 2 * t + 2)
                dve.wait_ge(p_exp, 16 * t + 16)
                step(V_.tensor_tensor(rc, sm, sx, ALU.add))
                step(V_.reciprocal(rc, rc))
                fl.wait_full(dve, f"AV{t}")
                if t:
                    fl.wait_full(dve, f"OT{t - 1}")
                V_.tensor_tensor(oN.rearrange("p (h c) -> p h c", c=64),
                                 flat(ps[:, 6:8, :]).rearrange("p (h c) -> p h c", c=64),
                                 rc.unsqueeze(2).to_broadcast([128, 16, 64]), ALU.mult).then_inc(free[6], 1)
                fl.wait_full(dve, f"WO{t}")
                dve.wait_ge(bo_added, t + 1)
                V_.tensor_tensor(h[:, t, :], flat(ps[:, 4:6, :]), h[:, t, :], ALU.add).then_inc(free[4], 1)
            experts(1)
            sig = nrm["_f"]
            dve.wait_ge(sig["sq_done"], NT)
            V_.tensor_scalar(var[:, :], ss[:, :], 1.0 / D, EPS, ALU.mult, ALU.add).then_inc(sig["var_done"], 1)
            dve.wait_ge(sig["rstd_done"], 1)
            dve.wait_ge(fin_in, 16)
            for t in range(NT):
                V_.scalar_tensor_tensor(fo[:, t, :], h[:, t, :], rstd[:, t:t + 1], fin_g, ALU.mult, ALU.mult)\
                    .then_inc(fin_done, 1)

        @block.gpsimd
        def _(pool):
            G = nc.gpsimd

            def power(sig):
                pool.wait_ge(sig["var_done"], 1)
                G.tensor_tensor(rstd[:, :], var[:, :], con[:, C_NH:C_NH + 5], ALU.pow).then_inc(sig["rstd_done"], 1)

            pool.wait_ge(s_const, 16)
            power(nrm["_r"])
            with pool.Fori(0, HEADS) as i:
                fl.wait_read(pool, "VAR", i)
                G.tensor_tensor(rs, vr, con[:, C_NH:C_NH + 1].to_broadcast([128, POS]), ALU.pow).then_inc(rs_ready, 1)

            def experts(l):
                m, tiles = mo[l], TILES5[l:]
                power(nrm[f"_m{l}"])
                pool.wait_ge(m["slot_ready"], 1)
                if l == 0:
                    pool.wait_ge(s_zeroed, 16)
                for t in tiles:
                    r = rows(t)
                    for c in range(2):
                        G.indirect_dma_start(slot_rows, bass.IndirectOffsetOnAxis(slot_i[0:r, c, t:t + 1], 0),
                                             xn[0:r, t, :], None).then_inc(m["scattered"], 16)
                for j in range(RING):
                    pool.wait_ge(m[f"y_out{j}"], 16 * (NBLK[l] // RING + 1))
                for n, t in enumerate(tiles):
                    r = rows(t)
                    if n >= 2:
                        pool.wait_ge(m["gath_used"], n - 1)
                    for c in range(2):
                        G.indirect_dma_start(gat[0:r, n % 2, c, :], None, slot_out,
                                             bass.IndirectOffsetOnAxis(slot_i[0:r, c, t:t + 1], 0))\
                            .then_inc(m[f"gathered{n % 2}"], 16)

            experts(0)
            power(nrm["_s"])
            pool.wait_ge(s_swat, 80)
            for t in range(NT):
                pool.wait_ge(nrm["_s"]["xn_done"], t + 2)
                G.tensor_tensor(h[:, t, :], h[:, t, :], bo, ALU.add).then_inc(bo_added, 1)
            G.memset(flat(VX), 0.0).then_inc(VX_zero, 1)
            for n, t in enumerate(TILES5):
                r = rows(t)
                fl.wait_read(pool, f"KV{t}")
                G.tensor_copy(V[0:r, t, :], kvs[0:r, n % 2, 256:512]).then_inc(V_ready, 1)
            pool.wait_ge(VX_zero, 1)
            pool.wait_ge(V_ready, 5)
            for t in range(NT):
                G.tensor_copy(VX[0:N_META, t, :], V[0:N_META, META, :]).then_inc(VX_ready, 1)
                if t:
                    G.tensor_copy(VX[64:128, t, :], V[64:128, t - 1, :]).then_inc(VX_ready, 1)
            experts(1)
            power(nrm["_f"])



_NAMES = ["x", "meta_tokens", "kv_b", "swa_b_q", "swa_sinks", "swa_b_o", "final_norm"]


def _chunks(w):
    kk, nn = w.shape[0] // D, w.shape[1] // 512
    w = w.reshape(kk, KT, 128, nn, 512).transpose(3, 0, 2, 1, 4)
    return np.ascontiguousarray(w.reshape(nn * kk, 128, KT * 512))


def _layout(i):
    out = {n: np.ascontiguousarray(i[n]) for n in _NAMES}
    w = i["ret_w_in"][0]
    heads = []
    for hd in range(HEADS):
        qk = np.concatenate([w[:, QK * hd:QK * hd + QK], w[:, D + QK * hd:D + QK * hd + QK]], axis=1)
        vg = [w[:, 2 * D + n * HEADS * VD + VD * hd:2 * D + n * HEADS * VD + VD * hd + VD] for n in range(2)]
        heads.append(np.stack([_chunks(x)[0] for x in (qk, *vg)]))
    out["w_ret"] = np.stack(heads)
    out["w_ret_out"] = _chunks(i["ret_w_out"][0])
    out["w_kv"], out["w_q"], out["w_o"] = _chunks(i["kv_w"]), _chunks(i["swa_w_q"][0]), _chunks(i["swa_w_o"][0])
    gu = np.concatenate([i["moe_w_gate"], i["moe_w_up"]], axis=3)
    out["w_gu"] = np.ascontiguousarray(gu.reshape(2, EXPERTS, KT, 128, 512).transpose(0, 1, 3, 2, 4)).reshape(
        2, EXPERTS, 128, KT * 512)
    dn = i["moe_w_down"].reshape(2, EXPERTS, 2, 128, D).transpose(0, 1, 3, 2, 4)
    out["w_down"] = np.ascontiguousarray(dn).reshape(2, EXPERTS, 128, 2 * D)
    route = np.concatenate([i["moe_w_group"], i["moe_w_router"]], axis=2)
    out["w_route"] = np.ascontiguousarray(route.reshape(2, KT, 128, 20).transpose(2, 0, 1, 3)).reshape(128, -1)
    g = np.stack([i["ret_norm"][0], i["kv_norm"], i["swa_norm"][0], i["moe_norm"][0], i["moe_norm"][1]])
    out["gains"] = np.ascontiguousarray(g.reshape(5, KT, 128).transpose(2, 0, 1)).reshape(128, -1)
    return out


def kernel(**inputs):
    import concourse.bacc as _bacc
    from concourse.bass_utils import run_bass_kernel_spmd as _run

    nc = _bacc.Bacc("TRN2", target_bir_lowering=False, num_devices=1)
    arrays = _layout({n: np.asarray(v) for n, v in inputs.items()})
    arrays["t_con"], arrays["t_ret"], arrays["t_swa"] = tables()
    aps = {n: nc.dram_tensor(f"in_{n}", v.shape, mybir.dt.from_np(v.dtype), kind="ExternalInput").ap()
           for n, v in arrays.items()}
    out = nc.dram_tensor("out", (1, SEQ, D), mybir.dt.float32, kind="ExternalOutput").ap()
    build(nc, aps, out)
    return _run(nc, [{f"in_{n}": v for n, v in arrays.items()}], core_ids=[0]).results[0]["out"]
```

```python
import numpy as np
from contextlib import ExitStack
import concourse.bass as bass
from concourse import mybir

D = 1024
KT = D // 128
SEQ, N_META, CHUNK = 512, 16, 64
POS = N_META + SEQ
NT = SEQ // 128
META = NT
HALF = POS // 2
HEADS, QK, VD = 4, 256, 512
KV_HEADS, Q_HEADS, HD = 4, 16, 64
GROUPS, PER_GROUP = 4, 4
EXPERTS = GROUPS * PER_GROUP
FF = 256
EPS = 1e-6
BLK = 128
RING = 3


def blocks_needed(tokens):
    return EXPERTS + (2 * tokens - 1) // BLK


NBLK = [blocks_needed(POS), blocks_needed(SEQ)]
MAXBLK = max(NBLK)
SLOTS = MAXBLK * BLK

C_ID, C_ONE, C_512, C_TRI = 0, 128, 256, 384
C_REV, C_THR, C_BLK, C_VALID, C_NH, C_EPS, C_FIRST, C_OVER = 512, 516, 521, 545, 550, 555, 556, 572
NCONST = 588
NRT = 2 * POS + HEADS * POS
NST = 5 * 32 * 3 + 512


def tables():
    f = np.float32
    c = np.zeros((128, NCONST), f)
    c[:, C_ID:C_ID + 128] = np.eye(128)
    c[:, C_ONE:C_ONE + 128] = 1.0
    c[:, C_512:C_512 + 128] = 1.0 / VD
    c[:, C_TRI:C_TRI + 128] = np.arange(128)[:, None] < np.arange(128)[None, :]
    c[:, C_REV:C_REV + 4] = [4, 3, 2, 1]
    c[:, C_THR:C_THR + 4] = np.arange(1, 5) * BLK
    c[:, C_FIRST:C_FIRST + EXPERTS] = np.arange(EXPERTS) * BLK
    c[:, C_OVER:C_OVER + EXPERTS] = EXPERTS - 1 - np.arange(EXPERTS)
    c[:, C_BLK:C_BLK + MAXBLK] = np.arange(MAXBLK)
    c[:, C_VALID:C_VALID + 5] = 1.0
    c[N_META:, C_VALID + META] = 0.0
    c[:, C_NH:C_NH + 5] = -0.5
    c[:, C_EPS] = EPS
    r = np.zeros((128, NRT), f)
    inv = (f(10000.0) ** (-np.arange(128, dtype=f) / f(128))).astype(f)
    ang = np.arange(POS, dtype=f)[None, :] * inv[:, None]
    r[:, 0:POS], r[:, POS:2 * POS] = np.cos(ang), np.sin(ang)
    lg = np.log1p(-np.exp2(-5.0 - np.arange(HEADS)))
    diff = np.arange(POS)[None, :] - np.arange(128)[:, None]
    for h in range(HEADS):
        dec = np.where(diff >= 0, np.exp(lg[h] * np.maximum(diff, 0)), 0.0) * QK ** -0.5
        r[:, 2 * POS + h * POS:2 * POS + (h + 1) * POS] = dec
    s = np.zeros((128, NST), f)
    inv = (f(10000.0) ** (-np.arange(32, dtype=f) / f(32))).astype(f)
    for t in range(5):
        pos = np.arange(128, dtype=f) + (0 if t == META else N_META + 128 * t)
        ang = pos[:, None] * inv[None, :]
        s[:, t * 32:t * 32 + 32] = np.cos(ang)
        s[:, 160 + t * 64:160 + t * 64 + 32] = -np.sin(ang)
        s[:, 160 + t * 64 + 32:160 + t * 64 + 64] = np.sin(ang)
    for v in range(2):
        m = np.full((128, 256), -1e30, f)
        m[:, 128:144] = 0.0
        m[0:64, 0:64] = 0.0
        m[64:128, 0:128] = 0.0
        if v:
            m[0:64, 192:256] = 0.0
        s[:, 480 + 256 * v:480 + 256 * v + 256] = m
    return c, r, s


class Fills:

    def __init__(self, full, free):
        self.full, self.free = full, free
        self.total = [0] * 8
        self.at = {}

    def phase(self, order, rounds=1):
        per = [sum(1 for _, b in order if b == k) for k in range(8)]
        seen = list(self.total)
        for name, b in order:
            assert name not in self.at, name
            self.at[name] = (b, seen[b], per[b])
            seen[b] += 1
        self.total = [self.total[k] + rounds * per[k] for k in range(8)]
        return list(self.total)

    def bank(self, name):
        return self.at[name][0]

    def wait_free(self, eng, name, i=0):
        b, n, per = self.at[name]
        if n or not isinstance(i, int):
            eng.wait_ge(self.free[b], i * per + n)

    def wait_full(self, eng, name, i=0):
        b, n, per = self.at[name]
        eng.wait_ge(self.full[b], i * per + (n + 1))

    def wait_read(self, eng, name, i=0):
        b, n, per = self.at[name]
        eng.wait_ge(self.free[b], i * per + (n + 1))


class Steps:

    def __init__(self, eng, sem):
        self.eng, self.sem, self.n, self.i, self.per, self.off = eng, sem, 0, None, 0, 0

    def rounds(self, i, per):
        self.i, self.per, self.off = i, per, 0

    def end(self, rounds):
        assert self.off == self.per, (self.off, self.per)
        self.n, self.i = self.n + rounds * self.per, None

    def count(self):
        return self.n if self.i is None else self.i * self.per + (self.n + self.off)

    def done(self, ins):
        ins.then_inc(self.sem, 1)
        if self.i is None:
            self.n += 1
        else:
            self.off += 1

    def wait(self):
        self.eng.wait_ge(self.sem, self.count())

    def __call__(self, ins):
        self.done(ins)
        self.wait()


def build(nc, a, out, dbg=None):
    F, I = mybir.dt.float32, mybir.dt.int32
    ALU, ACT, AX = mybir.AluOpType, mybir.ActivationFunctionType, mybir.AxisListType
    X, XY = AX.X, AX.XY
    ctx = ExitStack()
    with ctx:
        def sem(name):
            return ctx.enter_context(nc.semaphore(name))

        def sb(name, shape, dt=F):
            return ctx.enter_context(nc.sbuf_tensor(name, shape, dt))

        def col0(t):
            return 0 if t == META else N_META + 128 * t

        def rows(t):
            return N_META if t == META else 128

        con = sb("con", [128, NCONST])
        ident, ones, mean512, tri = (con[:, c:c + 128] for c in (C_ID, C_ONE, C_512, C_TRI))
        gains = sb("gains", [128, 5, KT])
        G_RET, G_KV, G_SWA, G_MOE = 0, 1, 2, (3, 4)
        wr = sb("wr", [128, 2, KT, 20])
        h = sb("h", [128, 5, D])
        ring = sb("ring", [128, RING, KT, 512])
        xT = sb("xT", [128, KT, POS])
        ss, var, rstd = sb("ss", [128, 5]), sb("var", [128, 5]), sb("rstd", [128, 5])
        eb_i = sb("eb_i", [1, 2, MAXBLK - EXPERTS], I)
        slot_i = sb("slot_i", [128, 2, 5], I)
        ps = ctx.enter_context(nc.psum_tensor("ps", [128, 8, 512], F))

        ARENA = 29400
        arena = sb("arena", [128, ARENA])

        class Carve:

            def __init__(self):
                self.at = 0

            def __call__(self, *shape):
                n = int(np.prod(shape))
                v = arena[:, self.at:self.at + n]
                self.at += n
                assert self.at <= ARENA, self.at
                if len(shape) == 1:
                    return v
                names = "abcd"[:len(shape)]
                return v.rearrange(f"p ({' '.join(names)}) -> p {' '.join(names)}",
                                   **dict(zip(names[1:], shape[1:])))

        cv = Carve()
        ret_xn = cv(5, D)
        cv.at = 0
        yT = cv(16, POS)
        rope_c, rope_s = cv(POS), cv(POS)
        decay = cv(HEADS, POS)
        qT, kT = cv(2, POS), cv(2, POS)
        v_tm = cv(5, VD)
        gate_t, gate = cv(4, POS), cv(4, POS)
        s_meta, s_t = cv(POS), cv(NT, 512)
        o_fm, sq = cv(4, POS), cv(4, POS)
        vr, rs = cv(POS), cv(POS)
        zero = cv(D)
        ret_junk = s_t.rearrange("p a b -> p (a b)")[:, 0:D]
        cv = Carve()
        down = cv(RING, 2, D)
        xg = cv(RING, D)
        xgT = cv(RING, KT, 128)
        yo = cv(RING, D)
        moe_junk = arena[:, cv.at:cv.at + D]
        cv.at = 5 * D + KT * POS
        gat = cv(5, 2, D)
        next_junk = arena[:, cv.at:cv.at + D]
        th, hid1, hid = cv(RING, FF), cv(FF), cv(RING, FF)
        hidT = cv(2, 128)
        lg = cv(5, 20)
        small = cv(2200)
        xn = cv(5, D)
        cv = Carve()
        xn1 = cv(5, D)
        xTk = cv(KT, POS)
        kT2 = cv(4, POS)
        kr, kA, kB = cv(2, 4, 128), cv(4, 64), cv(4, 64)
        kvs = cv(2, 512)
        V, VX = cv(5, 256), cv(NT, 256)
        qs, qA, qr, oN = cv(D), cv(D), cv(D), cv(D)
        qT1, oT1 = cv(KT, 128), cv(KT, 128)
        stab = cv(NST)
        sink_b, mx, nmx, es, sx, sm, rc = (cv(16) for _ in range(7))
        kvb, qb, bo = cv(512), cv(D), cv(D)
        PT = cv(2, 4, 128)
        P = arena[:, 0:16 * 256].rearrange("p (h k) -> p h k", h=16)
        wo_b = arena[:, 5 * D:5 * D + KT * 512].rearrange("p (k n) -> p k n", k=KT)
        cv = Carve()
        fo = cv(NT, D)
        fin_g = cv(D)

        slot_rows = nc.dram_tensor("slot_rows", (SLOTS, D), F).ap()
        slot_out = nc.dram_tensor("slot_out", (SLOTS, D), F).ap()

        full = [sem(f"bank_full{b}") for b in range(8)]
        free = [sem(f"bank_free{b}") for b in range(8)]
        fl = Fills(full, free)
        w_in = [sem(f"weights_in{s}") for s in range(RING)]
        x_in = [sem(f"x_in_{t}") for t in range(5)]
        s_const, s_zero, s_zeroed, s_rt, s_gains = (sem(n) for n in (
            "const_in", "zero_made", "slots_zeroed", "ret_tables_in", "gains_in"))

        TILES5 = [META, 0, 1, 2, 3]
        MOE_TILES = [[0, 1, 2, 3, META], [0, 1, 2, 3]]
        A, B, C, E = 0, 2, 4, 6

        def norm_plan(tag, tiles):
            fl.phase([(f"{tag}{t}", 2 * (n % 4)) for n, t in enumerate(tiles)])

        norm_plan("n0_", TILES5)

        def head_plan(z, rounds):
            names = ("Q1", "Q2", "K1", "K2", "MU", "V01", "V23", "V4", "SM", "S01", "S23", "VAR",
                     "G0", "G1", "G2", "G3", "O0", "O1", "O2", "O3")
            fl.phase([(x + z, (A, B, C, E)[n % 4]) for n, x in enumerate(names)
                      if z == "r" or x not in ("MU", "VAR")], rounds)

        head_plan("a", 1)
        head_plan("r", HEADS - 1)
        fl.phase([("MUt", A), ("VARt", A), ("W0_01", B), ("W0_23", C), ("W0_4", E),
                  ("W1_01", A), ("W1_23", B), ("W1_4", C)])
        t_blocks, t_blocks_end = {}, {}

        def moe_plan(l):
            norm_plan(f"m{l}_", MOE_TILES[l])
            fl.phase([(f"LG{l}", 0), (f"RK{l}", 2)])
            t_blocks[l] = list(fl.total)
            for b in range(8):
                fl.total[b] += (0, len(range(b - 2, NBLK[l], RING)), NBLK[l])[(b in (2, 3, 4)) + 2 * (b in (0, 5, 6, 7))]
            t_blocks_end[l] = list(fl.total)

        moe_plan(0)
        norm_plan("n1_", TILES5)
        t_norm1 = list(fl.total)
        fl.phase([(f"KV{t}", n) for n, t in enumerate(TILES5)])
        fl.phase([(f"KT{t}", 5 + n % 3) for n, t in enumerate(TILES5)])
        t_kv = list(fl.total)
        plan = [("Qa0", 4), ("Qb0", 5), ("QT0", 0)]
        for t in range(NT):
            plan += [(f"S{t}_{p}", p % 6) for p in range(8)]
            if t + 1 < NT:
                plan += [(f"Qa{t + 1}", 4), (f"Qb{t + 1}", 5)]
            plan += [(f"AV{t}", 6)] + [(f"PT{t}_{p}", p % 4) for p in range(8)]
            if t + 1 < NT:
                plan += [(f"QT{t + 1}", 0)]
            plan += [(f"OT{t}", 2), (f"WO{t}", 4)]
        fl.phase(plan)
        t_swa = list(fl.total)
        moe_plan(1)

        def all_read(eng, totals):
            for b in range(8):
                if totals[b]:
                    eng.wait_ge(free[b], totals[b])

        def pair(b):
            return ps[:, b:b + 2, 0:HALF]

        def halves(ap):
            return ap.rearrange("p (g c) -> p g c", g=2)

        def sigs(names, tag):
            return {n: sem(f"{n}{tag}") for n in names.split()}

        nrm = {k: sigs("sq_done var_done rstd_done xn_done", k) for k in ("_r", "_m0", "_s", "_m1", "_f")}
        q_ready, k_ready, gt_done, squared, y_ready, wo_used = (sem(n) for n in (
            "q_ready", "k_ready", "gate_tanh_done", "squared", "y_ready", "w_out_used"))
        mo = [sigs("lg_ready eg_in eg_out d_in d_out mask_ready eb_ready slot_ready scattered blocks_stored "
                   "tanh_done y_out0 y_out1 y_out2 x_in0 x_in1 x_in2 down_in0 down_in1 down_in2 "
                   "gathered0 gathered1 gathered2 gathered3 gathered4 gath_used", f"_{l}") for l in range(2)]
        s_swat, kv_evac, kr_ready, V_ready, VX_zero, VX_ready = (sem(n) for n in (
            "swa_tables_in", "kv_evac", "k_rotated", "V_ready", "VX_zeroed", "VX_ready"))
        q_rot, m_ready, p_exp, snk_exp, bo_added = (sem(n) for n in (
            "q_rotated", "max_ready", "p_exp", "sink_exp", "bo_added"))
        wo_b_in = sem("w_o_b_in")
        fin_done, s_out, fin_in = sem("final_done"), sem("out_stored"), sem("final_gain_in")
        dsem = {k: sem(f"dve_steps_{k}") for k in "nraskf"}
        dsem_m = [sem(f"dve_steps_moe{l}") for l in range(2)]

        N_WO = 3 * HEADS
        N_M = [N_WO + 4, N_WO + 4 + NBLK[0] + 4]
        N_KV = N_M[0] + NBLK[0]
        N_Q, N_O = N_KV + 1, N_KV + 3

        def w_at(n):
            return ring[:, n % RING]

        def w_wait(eng, n, i=0):
            eng.wait_ge(w_in[n % RING], i * 16 + 16 * (n // RING + 1))

        def flat(ap):
            return ap.rearrange("p a b -> p (a b)")

        def view(at, *shape):
            v = small[:, at:at + int(np.prod(shape))]
            if len(shape) == 1:
                return v
            names = "abc"[:len(shape)]
            return v.rearrange(f"p ({' '.join(names)}) -> p {' '.join(names)}", **dict(zip(names[1:], shape[1:])))

        sizes = dict(MASK=80, OV=80, T1=5, TOP=5, EQ=20, OHG=20, EG=20, G44=80, SEL=20, M1=5, M2=5, OH1=20, OH2=20, DX=5,
                     MA=80, MB=80, W1=5, W2=5, PRE=96, C5=80, NB=16, Z16=16, INCL=16, EB=16 * MAXBLK, EBS=MAXBLK,
                     BASE=16, SL=80, SF=10)
        ends = np.cumsum([0] + list(sizes.values())).tolist()
        (MASK, OV, T1, TOP, EQ, OHG, EG, G44, SEL, M1, M2, OH1, OH2, DX, MA, MB, W1, W2, PRE, C5, NB, Z16, INCL, EB, EBS,
         BASE, SL, SF) = ends[:-1]
        block = ctx.enter_context(nc.Block())

        B_ROWS, B_HID, B_YA, B_YB = 0, 5, 6, 7

        def gu_bank(k):
            return 2 + k % RING

        def block_count(l, b, k, i):
            if b in (2, 3, 4):
                return i + (t_blocks[l][b] + k // RING + 1)
            return i * RING + (t_blocks[l][b] + k + 1)

        def block_full(eng, l, b, k, i=0):
            eng.wait_ge(full[b], block_count(l, b, k, i))

        def block_read(eng, l, b, k, i=0):
            eng.wait_ge(free[b], block_count(l, b, k, i))

        def stage(k, i, unit=16):
            return i * unit + unit * (k // RING + 1)

        def block_index(k, i):
            return slice(k, k + 1) if isinstance(i, int) else bass.ds(i * RING + k, 1)

        def outputs_read(eng, n):
            for m in range(4):
                b, at, _ = fl.at[f"O{m}a"]
                per = fl.at[f"O{m}r"][2]
                eng.wait_ge(free[b], n * per + (at + 1))

        def head_pair(p):
            return (4 * (p // 2) + p % 2, 4 * (p // 2) + p % 2 + 2)

        def masks(l):
            return small[:, 0:EXPERTS * 5]

        @block.sync
        def _(sp):
            def chunk(n, src):
                sp.dma_start(flat(w_at(n)), src).then_inc(w_in[n % RING], 16)

            for t in range(NT):
                sp.dma_start(h[:, t, :], a["x"][0, 128 * t:128 * t + 128, :]).then_inc(x_in[t], 16)
            for j in range(RING):
                chunk(j, a["w_ret"][0, j])
            for j, last in enumerate(("K2", "V4", "G3")):
                fl.wait_full(sp, last + "a")
                chunk(RING + j, a["w_ret"][1, j])
            with sp.Fori(0, HEADS - 2) as i:
                for j, last in enumerate(("K2", "V4", "G3")):
                    fl.wait_full(sp, last + "r", i)
                    chunk(j, a["w_ret"][2:HEADS][bass.ds(i, 1), j].rearrange("a p c -> p (a c)"))
            for j, last in enumerate(("K2", "V4", "G3")):
                fl.wait_full(sp, last + "r", HEADS - 2)
                chunk(N_WO + j, a["w_ret_out"][j])
            sp.wait_ge(wo_used, 1)
            chunk(N_WO + 3, a["w_ret_out"][3])

            def first_weights(l, readers):
                for k, used in enumerate(readers):
                    used()
                    chunk(N_M[l] + k, a["w_gu"][l, k])
                for k in range(RING):
                    sp.dma_start(flat(down[:, k]), a["w_down"][l, k]).then_inc(mo[l][f"down_in{k}"], 16)

            def experts(l):
                m = mo[l]
                gu_d, dn_d = a["w_gu"][l], a["w_down"][l]
                x_blocks = slot_rows.rearrange("(b p) c -> b p c", p=BLK)

                def load_rows(k, i):
                    sp.dma_start(xg[:, k % RING, :], x_blocks[block_index(k, i)].rearrange("a p c -> p (a c)"))\
                        .then_inc(m[f"x_in{k % RING}"], 16)

                def load_block(k, i):
                    if k < EXPERTS:
                        e = block_index(k, i)
                    else:
                        e = sp.value_load(eb_i[0:1, l, k - EXPERTS:k - EXPERTS + 1], min_val=0, max_val=EXPERTS - 1)
                        e = bass.ds(e, 1)
                    block_full(sp, l, B_ROWS, k - RING, i)
                    load_rows(k, i)
                    block_full(sp, l, gu_bank(k), k - RING, i)
                    chunk(N_M[l] + k, gu_d[e].rearrange("a p c -> p (a c)"))
                    block_full(sp, l, B_YB, k - RING, i)
                    sp.dma_start(flat(down[:, k % RING]), dn_d[e].rearrange("a p c -> p (a c)"))\
                        .then_inc(m[f"down_in{k % RING}"], 16)

                sp.wait_ge(m["scattered"], 16 * 2 * (5 - l))
                for k in range(RING):
                    load_rows(k, 0)
                rounds = EXPERTS // RING - 1
                with sp.Fori(0, rounds) as i:
                    for k in range(RING, 2 * RING):
                        load_block(k, i)
                sp.wait_ge(m["eb_ready"], 1)
                for k in range(RING * (rounds + 1), NBLK[l]):
                    load_block(k, 0)

            first_weights(0, (lambda: fl.wait_full(sp, "W0_4"), lambda: sp.wait_ge(wo_used, 2),
                              lambda: fl.wait_full(sp, "W1_4")))
            experts(0)
            sp.wait_ge(mo[0]["gath_used"], 5)
            chunk(N_KV, a["w_kv"][0])
            for dst, src in ((stab, a["t_swa"]), (sink_b, a["swa_sinks"][0].partition_broadcast(128)),
                             (kvb, a["kv_b"].partition_broadcast(128)),
                             (qb, a["swa_b_q"][0].partition_broadcast(128)),
                             (bo, a["swa_b_o"][0].partition_broadcast(128))):
                sp.dma_start(dst, src).then_inc(s_swat, 16)
            chunk(N_Q, a["w_q"][0])
            chunk(N_Q + 1, a["w_q"][1])
            fl.wait_full(sp, f"KV{TILES5[-1]}")
            chunk(N_O, a["w_o"][0])
            sp.dma_start(flat(wo_b), a["w_o"][1]).then_inc(wo_b_in, 16)
            first_weights(1, (lambda: fl.wait_full(sp, f"Qa{NT - 1}"), lambda: fl.wait_full(sp, f"Qb{NT - 1}"),
                              lambda: fl.wait_full(sp, f"WO{NT - 1}")))
            experts(1)
            for j in range(RING):
                sp.wait_ge(mo[1][f"y_out{j}"], 16 * (len(range(j, NBLK[1], RING)) + 1))
            sp.dma_start(fin_g, a["final_norm"].partition_broadcast(128)).then_inc(fin_in, 16)
            for t in range(NT):
                sp.wait_ge(fin_done, t + 1)
                sp.dma_start(out[0, 128 * t:128 * t + 128, :], fo[:, t, :]).then_inc(s_out, 16)
            sp.wait_ge(s_out, 16 * NT)

        @block.tensor
        def _(pe):
            mm = nc.tensor.matmul

            def transposed(tag, tiles, src, sig):
                for n, t in enumerate(tiles):
                    r, b = rows(t), fl.bank(f"{tag}{t}")
                    fl.wait_free(pe, f"{tag}{t}")
                    pe.wait_ge(sig["xn_done"], n + 1)
                    for k in range(KT):
                        last = nc.tensor.transpose(ps[:, b + k // 4, 128 * (k % 4):128 * (k % 4) + r],
                                                   src[0:r, t, 128 * k:128 * k + 128], ident[0:r, 0:r])
                    last.then_inc(full[b], 1)

            pe.wait_ge(s_const, 16)
            transposed("n0_", TILES5, ret_xn, nrm["_r"])
            for t in TILES5:
                fl.wait_read(pe, f"n0_{t}")

            def feature_major_product(name, i, w, m):
                b = fl.bank(name)
                fl.wait_free(pe, name, i)
                for g in range(2):
                    for k in range(KT):
                        last = mm(ps[:, b + g, 0:HALF], w[:, k, 128 * m:128 * m + 128],
                                  xT[:, k, HALF * g:HALF * g + HALF], start=(k == 0), stop=(k == KT - 1))
                last.then_inc(full[b], 1)

            def head_mean(name, src, i):
                b = fl.bank(name)
                fl.wait_free(pe, name, i)
                for g in range(2):
                    for m in range(4):
                        last = mm(ps[:, b + g, 0:HALF], mean512, src[:, m, HALF * g:HALF * g + HALF],
                                  start=(m == 0), stop=(m == 3))
                last.then_inc(full[b], 1)

            def head(z, i):
                n0 = RING if z == "r" else 0
                hd = i + 1 if z == "r" else 0
                w_wait(pe, n0, i)
                for m, name in enumerate(("Q1", "Q2", "K1", "K2")):
                    feature_major_product(name + z, i, w_at(0), m)
                if z == "r":
                    outputs_read(pe, i)
                    head_mean("MUr", o_fm, i)
                w_wait(pe, n0 + 1, i)
                for name, tiles in (("V01", (0, 1)), ("V23", (2, 3)), ("V4", (META,))):
                    b = fl.bank(name + z)
                    fl.wait_free(pe, name + z, i)
                    for g, t in enumerate(tiles):
                        for k in range(KT):
                            last = mm(ps[0:rows(t), b + g, :], xT[:, k, col0(t):col0(t) + rows(t)],
                                      w_at(1)[:, k, :], start=(k == 0), stop=(k == KT - 1))
                    last.then_inc(full[b], 1)
                pe.wait_ge(q_ready, hd * 2 + 2)
                pe.wait_ge(k_ready, hd * 2 + 2)
                b = fl.bank("SM" + z)
                fl.wait_free(pe, "SM" + z, i)
                for g in range(2):
                    for k in range(2):
                        last = mm(ps[0:N_META, b + g, 0:HALF], kT[:, k, 0:N_META],
                                  qT[:, k, HALF * g:HALF * g + HALF], start=(k == 0), stop=(k == 1))
                last.then_inc(full[b], 1)
                for name, tiles in (("S01", (0, 1)), ("S23", (2, 3))):
                    b = fl.bank(name + z)
                    fl.wait_free(pe, name + z, i)
                    for g, t in enumerate(tiles):
                        for k in range(2):
                            last = mm(ps[:, b + g, 0:POS - col0(t)], kT[:, k, col0(t):col0(t) + 128],
                                      qT[:, k, col0(t):POS], start=(k == 0), stop=(k == 1))
                    last.then_inc(full[b], 1)
                if z == "r":
                    pe.wait_ge(squared, i + 1)
                    head_mean("VARr", sq, i)
                w_wait(pe, n0 + 2, i)
                for m in range(4):
                    feature_major_product(f"G{m}{z}", i, w_at(2), m)
                for name in ("SM", "S01", "S23"):
                    fl.wait_read(pe, name + z, i)
                for m in range(4):
                    b = fl.bank(f"O{m}{z}")
                    fl.wait_free(pe, f"O{m}{z}", i)
                    for g in range(2):
                        lo, hi = HALF * g, HALF * g + HALF
                        tiles = [t for t in range(NT) if col0(t) < hi]
                        mm(ps[:, b + g, 0:HALF], v_tm[0:N_META, META, 128 * m:128 * m + 128],
                           s_meta[0:N_META, lo:hi], start=True, stop=False)
                        for t in tiles:
                            c = max(col0(t), lo)
                            last = mm(ps[:, b + g, c - lo:HALF], v_tm[:, t, 128 * m:128 * m + 128],
                                      s_t[:, t, c - col0(t):hi - col0(t)], start=False, stop=(t == tiles[-1]))
                    last.then_inc(full[b], 1)

            head("a", 0)
            with pe.Fori(0, HEADS - 1) as i:
                head("r", i)
            outputs_read(pe, HEADS - 1)
            head_mean("MUt", o_fm, 0)
            for hf in range(2):
                groups = [(f"W{hf}_01", (0, 1)), (f"W{hf}_23", (2, 3)), (f"W{hf}_4", (META,))]
                for c in range(2):
                    n = N_WO + 2 * hf + c
                    pe.wait_ge(y_ready, HEADS if hf or c else HEADS // 2)
                    w_wait(pe, n)
                    for name, tiles in groups:
                        b = fl.bank(name)
                        if c == 0:
                            fl.wait_free(pe, name)
                        for g, t in enumerate(tiles):
                            for k in range(KT):
                                last = mm(ps[0:rows(t), b + g, :], yT[:, KT * c + k, col0(t):col0(t) + rows(t)],
                                          w_at(n)[:, k, :], start=(c == 0 and k == 0), stop=(c == 1 and k == KT - 1))
                        if c == 1:
                            last.then_inc(full[b], 1)
                        elif name == "W0_01":
                            pe.wait_ge(squared, HEADS)
                            head_mean("VARt", sq, 0)
                    if c == 0:
                        last.then_inc(wo_used, 1)

            def experts(l):
                m, tiles = mo[l], MOE_TILES[l]
                transposed(f"m{l}_", tiles, xn, nrm[f"_m{l}"])
                for n, t in enumerate(tiles):
                    fl.wait_read(pe, f"m{l}_{t}")
                    if n == 0:
                        fl.wait_free(pe, f"LG{l}")
                    for k in range(KT):
                        last = mm(ps[0:rows(t), 0, 20 * t:20 * t + 20], xT[:, k, col0(t):col0(t) + rows(t)],
                                  wr[:, l, k, :], start=(k == 0), stop=(k == KT - 1))
                last.then_inc(full[0], 1)
                n = EXPERTS * (5 - l)
                pe.wait_ge(m["mask_ready"], 1)
                mm(ps[:, 2, 0:n], tri, masks(l)[:, 0:n], start=True, stop=True)
                mm(ps[:, 2, 128:128 + n], ones, masks(l)[:, 0:n], start=True, stop=True).then_inc(full[2], 1)
                all_read(pe, t_blocks[l])

                def rows_to_features(k, i):
                    pe.wait_ge(m[f"x_in{k % RING}"], stage(k, i))
                    if k:
                        block_read(pe, l, B_ROWS, k - 1, i)
                    for c in range(KT):
                        last = nc.tensor.transpose(ps[:, c // 4, 128 * (c % 4):128 * (c % 4) + 128],
                                                   xg[:, k % RING, 128 * c:128 * c + 128], ident)
                    last.then_inc(full[B_ROWS], 1)

                def gate_up(k, i):
                    b = gu_bank(k)
                    w_wait(pe, N_M[l] + k, i)
                    block_read(pe, l, B_ROWS, k, i)
                    if k >= RING:
                        block_read(pe, l, b, k - RING, i)
                    for c in range(KT):
                        last = mm(ps[:, b, :], xgT[:, k % RING, c, :], w_at(N_M[l] + k)[:, c, :],
                                  start=(c == 0), stop=(c == KT - 1))
                    last.then_inc(full[b], 1)

                def hidden_to_features(k, i):
                    block_read(pe, l, gu_bank(k), k, i)
                    for c in range(2):
                        last = nc.tensor.transpose(ps[:, B_HID, 128 * c:128 * c + 128],
                                                   hid[:, k % RING, 128 * c:128 * c + 128], ident)
                    last.then_inc(full[B_HID], 1)

                def down_project(k, i):
                    pe.wait_ge(m[f"down_in{k % RING}"], stage(k, i))
                    block_read(pe, l, B_HID, k, i)
                    for half, b in enumerate((B_YA, B_YB)):
                        if k:
                            block_read(pe, l, b, k - 1, i)
                        for c in range(2):
                            last = mm(ps[:, b, :], hidT[:, c, :], down[:, k % RING, c, 512 * half:512 * half + 512],
                                      start=(c == 0), stop=(c == 1))
                        last.then_inc(full[b], 1)

                def block_step(k, i):
                    gate_up(k, i)
                    hidden_to_features(k - 1, i)
                    if k + 1 < NBLK[l]:
                        rows_to_features(k + 1, i)
                    down_project(k - 1, i)

                rows_to_features(0, 0)
                gate_up(0, 0)
                rows_to_features(1, 0)
                for k in range(1, RING):
                    block_step(k, 0)
                rounds = (NBLK[l] - 1 - RING) // RING
                with pe.Fori(0, rounds) as i:
                    for k in range(RING, 2 * RING):
                        block_step(k, i)
                for k in range(RING * (1 + rounds), NBLK[l]):
                    block_step(k, 0)
                hidden_to_features(NBLK[l] - 1, 0)
                down_project(NBLK[l] - 1, 0)

            experts(0)

            all_read(pe, t_blocks_end[0])
            transposed("n1_", TILES5, xn1, nrm["_s"])
            w_wait(pe, N_KV)
            all_read(pe, t_norm1)
            for t in TILES5:
                b = fl.bank(f"KV{t}")
                fl.wait_free(pe, f"KV{t}")
                for k in range(KT):
                    last = mm(ps[0:rows(t), b, :], xTk[:, k, col0(t):col0(t) + rows(t)], w_at(N_KV)[:, k, :],
                              start=(k == 0), stop=(k == KT - 1))
                last.then_inc(full[b], 1)
            for n, t in enumerate(TILES5):
                b, r = fl.bank(f"KT{t}"), rows(t)
                fl.wait_free(pe, f"KT{t}")
                pe.wait_ge(kr_ready, n + 1)
                for j in range(KV_HEADS):
                    last = nc.tensor.transpose(ps[:, b, 128 * j:128 * j + r], kr[0:r, n % 2, j, :], ident[0:r, 0:r])
                last.then_inc(full[b], 1)
            all_read(pe, t_kv)

            def project_q(t):
                for c, name in enumerate((f"Qa{t}", f"Qb{t}")):
                    w_wait(pe, N_Q + c)
                    fl.wait_free(pe, name)
                    for k in range(KT):
                        last = mm(ps[:, 4 + c, :], xT[:, k, col0(t):col0(t) + 128], w_at(N_Q + c)[:, k, :],
                                  start=(k == 0), stop=(k == KT - 1))
                    last.then_inc(full[4 + c], 1)

            def transpose_q(t):
                fl.wait_free(pe, f"QT{t}")
                pe.wait_ge(q_rot, t + 1)
                for k in range(KT):
                    last = nc.tensor.transpose(ps[:, k // 4, 128 * (k % 4):128 * (k % 4) + 128],
                                               qr[:, 128 * k:128 * k + 128], ident)
                last.then_inc(full[0], 1)

            project_q(0)
            transpose_q(0)
            for t in range(NT):
                fl.wait_read(pe, f"QT{t}")
                prev = col0(t) - CHUNK if t else 0
                for p in range(8):
                    b = fl.bank(f"S{t}_{p}")
                    fl.wait_free(pe, f"S{t}_{p}")
                    for g, hd in enumerate(head_pair(p)):
                        o = 64 * (hd % 2)
                        q = qT1[o:o + 64, hd // 2, :]
                        for at, c, n in ((0, col0(t), 128), (128, 0, CHUNK), (128 + CHUNK, prev, CHUNK)):
                            last = mm(ps[:, b, 256 * g + at:256 * g + at + n], q,
                                      kT2[o:o + 64, hd // 4, c:c + n], start=True, stop=True)
                    last.then_inc(full[b], 1)
                if t + 1 < NT:
                    project_q(t + 1)
                fl.wait_free(pe, f"AV{t}")

                def weigh(p):
                    fl.wait_read(pe, f"PT{t}_{p}")
                    for g in range(2):
                        hd = 2 * p + g
                        dst = ps[:, 6 + hd // 8, 64 * (hd % 8):64 * (hd % 8) + 64]
                        j = 64 * (hd // 4)
                        mm(dst, PT[:, p % 2, 2 * g, :], V[:, t, j:j + 64], start=True, stop=False)
                        last = mm(dst, PT[:, p % 2, 2 * g + 1, :], VX[:, t, j:j + 64], start=False, stop=True)
                    if p == 7:
                        last.then_inc(full[6], 1)

                if t == 0:
                    pe.wait_ge(V_ready, 5)
                    pe.wait_ge(VX_ready, 2 * NT - 1)
                for p in range(8):
                    b = fl.bank(f"PT{t}_{p}")
                    fl.wait_free(pe, f"PT{t}_{p}")
                    pe.wait_ge(p_exp, 16 * t + 2 * p + 2)
                    for g in range(2):
                        for c in range(2):
                            last = nc.tensor.transpose(ps[:, b, 128 * (2 * g + c):128 * (2 * g + c) + 128],
                                                       P[:, 2 * p + g, 128 * c:128 * c + 128], ident)
                    last.then_inc(full[b], 1)
                    if p:
                        weigh(p - 1)
                weigh(7)
                if t + 1 < NT:
                    transpose_q(t + 1)
                fl.wait_free(pe, f"OT{t}")
                fl.wait_read(pe, f"AV{t}")
                for k in range(KT):
                    last = nc.tensor.transpose(ps[:, 2 + k // 4, 128 * (k % 4):128 * (k % 4) + 128],
                                               oN[:, 128 * k:128 * k + 128], ident)
                last.then_inc(full[2], 1)
                fl.wait_free(pe, f"WO{t}")
                if t + 1 < NT:
                    fl.wait_read(pe, f"Qb{t + 1}")
                fl.wait_read(pe, f"OT{t}")
                w_wait(pe, N_O)
                pe.wait_ge(wo_b_in, 16)
                for c, w in enumerate((w_at(N_O), wo_b)):
                    for k in range(KT):
                        last = mm(ps[:, 4 + c, :], oT1[:, k, :], w[:, k, :],
                                  start=(k == 0), stop=(k == KT - 1))
                last.then_inc(full[4], 1)
            all_read(pe, t_swa)
            experts(1)

        @block.scalar
        def _(act):
            def squares(tiles, sig, junk, ready):
                for n, t in enumerate(tiles):
                    ready(t)
                    r = rows(t)
                    if n:
                        act.wait_ge(sig["sq_done"], n)
                    nc.scalar.activation(junk[0:r], h[0:r, t, :], ACT.Square,
                                         accum_out=ss[0:r, t:t + 1]).then_inc(sig["sq_done"], 1)

            act.dma_start(h[0:N_META, META, :], a["meta_tokens"]).then_inc(x_in[META], 16)
            act.dma_start(con[:, :], a["t_con"]).then_inc(s_const, 16)
            act.dma_start(flat(gains[:, :, :]), a["gains"]).then_inc(s_gains, 16)
            act.dma_start(wr[:, :, :, :].rearrange("p a b c -> p (a b c)"), a["w_route"]).then_inc(s_gains, 16)
            act.dma_start(arena[:, 16 * POS:16 * POS + NRT], a["t_ret"]).then_inc(s_rt, 16)
            act.wait_ge(s_zero, 1)
            act.dma_start(slot_rows.rearrange("(b p) c -> p b c", p=128),
                          zero.unsqueeze(1).to_broadcast([128, MAXBLK, D])).then_inc(s_zeroed, 16)
            squares(TILES5, nrm["_r"], ret_junk, lambda t: act.wait_ge(x_in[t], 16))

            def square_outputs(z, i):
                fl.wait_read(act, "MU" + z, i)
                nc.scalar.activation(flat(sq), flat(o_fm), ACT.Square).then_inc(squared, 1)

            def deviation(z, i):
                b = fl.bank("VAR" + z)
                fl.wait_full(act, "VAR" + z, i)
                nc.scalar.activation(halves(vr), pair(b), ACT.Sqrt, bias=con[:, C_EPS:C_EPS + 1]).then_inc(free[b], 1)

            def head(z, i):
                if z == "r":
                    square_outputs(z, i)
                for name, t, n in (("V01", 0, 2), ("V23", 2, 2)):
                    b = fl.bank(name + z)
                    fl.wait_full(act, name + z, i)
                    nc.scalar.activation(v_tm[:, t:t + n, :], ps[:, b:b + 2, :], ACT.Copy).then_inc(free[b], 1)
                b = fl.bank("V4" + z)
                fl.wait_full(act, "V4" + z, i)
                nc.scalar.activation(v_tm[0:N_META, META, :], ps[0:N_META, b, :], ACT.Copy).then_inc(free[b], 1)
                if z == "r":
                    deviation(z, i)
                for m in range(4):
                    fl.wait_full(act, f"G{m}{z}", i)
                    nc.scalar.activation(halves(gate_t[:, m, :]), pair(fl.bank(f"G{m}{z}")), ACT.Tanh, scale=0.5)\
                        .then_inc(gt_done, 1)
                for m in range(4):
                    b = fl.bank(f"O{m}{z}")
                    fl.wait_full(act, f"O{m}{z}", i)
                    nc.scalar.activation(halves(o_fm[:, m, :]), pair(b), ACT.Copy).then_inc(free[b], 1)

            head("a", 0)
            with act.Fori(0, HEADS - 1) as i:
                head("r", i)
            square_outputs("t", 0)
            deviation("t", 0)

            def experts(l, ready):
                m = mo[l]
                squares(MOE_TILES[l], nrm[f"_m{l}"], moe_junk, ready)
                act.wait_ge(m["eg_in"], 1)
                nc.scalar.activation(view(EG, 5 - l, 4), view(EG, 5 - l, 4), ACT.Exp).then_inc(m["eg_out"], 1)
                act.wait_ge(m["d_in"], 1)
                nc.scalar.activation(view(DX, 5 - l), view(DX, 5 - l), ACT.Exp).then_inc(m["d_out"], 1)

                def tanh_of(k, i):
                    b = gu_bank(k)
                    block_full(act, l, b, k, i)
                    if k >= RING:
                        block_read(act, l, b, k - RING, i)
                    nc.scalar.activation(th[:, k % RING, :], ps[:, b, 0:FF], ACT.Tanh, scale=0.5)\
                        .then_inc(m["tanh_done"], 1)

                def hidden_of(k, i):
                    block_full(act, l, B_HID, k, i)
                    nc.scalar.activation(flat(hidT), ps[:, B_HID, 0:FF], ACT.Copy).then_inc(free[B_HID], 1)

                def results_of(k, i):
                    j = k % RING
                    block_full(act, l, B_YA, k, i)
                    act.wait_ge(m[f"y_out{j}"], stage(k, i))
                    nc.scalar.activation(yo[:, j, 0:512], ps[:, B_YA, :], ACT.Copy).then_inc(free[B_YA], 1)
                    block_read(act, l, B_YA, k, i)
                    block_read(act, l, B_YB, k, i)
                    act.dma_start(slot_out.rearrange("(b p) c -> b p c", p=BLK)[block_index(k, i)]
                                  .rearrange("a p c -> p (a c)"), yo[:, j, :]).then_inc(m[f"y_out{j}"], 16)

                tanh_of(0, 0)

                def block_step(k, i):
                    hidden_of(k - 1, i)
                    tanh_of(k, i)
                    results_of(k - 1, i)

                for k in range(1, RING):
                    block_step(k, 0)
                rounds = NBLK[l] // RING - 1
                with act.Fori(0, rounds) as i:
                    for k in range(RING, 2 * RING):
                        block_step(k, i)
                for k in range(RING * (1 + rounds), NBLK[l]):
                    block_step(k, 0)
                hidden_of(NBLK[l] - 1, 0)
                results_of(NBLK[l] - 1, 0)

            def after_retention(t):
                for hf in range(2):
                    fl.wait_read(act, f"W{hf}_4" if t == META else f"W{hf}_{'01' if t < 2 else '23'}")

            experts(0, after_retention)
            squares(TILES5, nrm["_s"], next_junk, lambda t: act.wait_ge(mo[0]["gath_used"], TILES5.index(t) + 1))
            for n, t in enumerate(TILES5):
                b, r = fl.bank(f"KT{t}"), rows(t)
                fl.wait_full(act, f"KT{t}")
                nc.scalar.activation(kT2[:, :, col0(t):col0(t) + r],
                                     ps[:, b, :].rearrange("p (j c) -> p j c", j=4)[:, :, 0:r], ACT.Copy)\
                    .then_inc(free[b], 1)

            def q_out(t):
                fl.wait_full(act, f"QT{t}")
                nc.scalar.activation(flat(qT1), flat(ps[:, 0:2, :]), ACT.Copy).then_inc(free[0], 1)

            q_out(0)
            for t in range(NT):
                for g in range(2):
                    act.wait_ge(m_ready, 2 * t + g + 1)
                    for hd in range(8 * g, 8 * g + 8):
                        nc.scalar.activation(P[:, hd, :], P[:, hd, :], ACT.Exp, bias=nmx[:, hd:hd + 1],
                                             accum_out=sm[:, hd:hd + 1]).then_inc(p_exp, 1)
                    nc.scalar.activation(sx[:, 8 * g:8 * g + 8], es[:, 8 * g:8 * g + 8], ACT.Exp).then_inc(snk_exp, 1)
                for p in range(1, 8, 2):
                    b = fl.bank(f"PT{t}_{p}")
                    fl.wait_full(act, f"PT{t}_{p}")
                    nc.scalar.activation(flat(PT[:, 1]), ps[:, b, :], ACT.Copy).then_inc(free[b], 1)
                if t + 1 < NT:
                    q_out(t + 1)
                fl.wait_full(act, f"OT{t}")
                nc.scalar.activation(flat(oT1), flat(ps[:, 2:4, :]), ACT.Copy).then_inc(free[2], 1)
            experts(1, lambda t: fl.wait_read(act, f"WO{t}"))
            squares(MOE_TILES[1], nrm["_f"], next_junk, lambda t: act.wait_ge(mo[1]["gath_used"], t + 1))

        @block.vector
        def _(dve):
            V_ = nc.vector

            def norm_tile(sig, n, t, dst):
                r = rows(t)
                dve.wait_ge(sig["rstd_done"], n + 1)
                V_.tensor_scalar(dst[0:r, t, :], h[0:r, t, :], rstd[0:r, t:t + 1], None, ALU.mult)\
                    .then_inc(sig["xn_done"], 1)

            def gained(dst, b, g, gain, c0, r, j=None):
                src = ps[:, b + g, :].rearrange("p (k c) -> p k c", k=4)[:, :, 0:r]
                return V_.tensor_tensor(dst[:, 4 * g:4 * g + 4, c0:c0 + r], src,
                                        gains[:, gain, 4 * g:4 * g + 4].unsqueeze(2).to_broadcast([128, 4, r]), ALU.mult)

            def feature_major(tag, t, gain):
                b = fl.bank(f"{tag}{t}")
                fl.wait_full(dve, f"{tag}{t}")
                gained(xT, b, 0, gain, col0(t), rows(t))
                gained(xT, b, 1, gain, col0(t), rows(t)).then_inc(free[b], 1)

            V_.memset(zero, 0.0).then_inc(s_zero, 1)
            for n, t in enumerate(TILES5):
                norm_tile(nrm["_r"], n, t, ret_xn)
                if n == 1:
                    dve.wait_ge(s_gains, 32)
                if n:
                    feature_major("n0_", TILES5[n - 1], G_RET)
            feature_major("n0_", TILES5[-1], G_RET)
            dve.wait_ge(s_rt, 16)
            step = Steps(dve, dsem["r"])
            tmp = [sq[:, n, :] for n in range(4)]

            def center(z, i):
                fl.wait_full(dve, "MU" + z, i)
                b = fl.bank("MU" + z)
                for m in range(4):
                    last = V_.tensor_tensor(halves(o_fm[:, m, :]), halves(o_fm[:, m, :]), pair(b), ALU.subtract)
                last.then_inc(free[b], 1)

            def gated(z, i):
                fl.wait_read(dve, "VAR" + z, i)
                step(V_.reciprocal(rs, vr))
                for m in range(4):
                    last = V_.tensor_tensor(o_fm[:, m, :], o_fm[:, m, :], rs, ALU.mult)
                step(last)
                dst = yT[:, bass.ds(i * 4, 4), :] if z == "r" else yT[:, 4 * HEADS - 4:4 * HEADS, :]
                V_.scalar_tensor_tensor(dst, o_fm, 0.5, gate, ALU.mult, ALU.mult).then_inc(y_ready, 1)
                if z == "r":
                    dve.wait_ge(y_ready, i + 1)

            def head(z, i):
                hd = i + 1 if z == "r" else 0
                for lo, hi, dst, sig in (("Q1", "Q2", qT, q_ready), ("K1", "K2", kT, k_ready)):
                    bl, bh = fl.bank(lo + z), fl.bank(hi + z)
                    fl.wait_full(dve, lo + z, i)
                    V_.tensor_tensor(halves(tmp[0]), pair(bl), halves(rope_c), ALU.mult)
                    fl.wait_full(dve, hi + z, i)
                    step.done(V_.tensor_tensor(halves(tmp[1]), pair(bh), halves(rope_s), ALU.mult))
                    V_.tensor_tensor(halves(tmp[2]), pair(bh), halves(rope_c), ALU.mult).then_inc(free[bh], 1)
                    V_.tensor_tensor(halves(tmp[3]), pair(bl), halves(rope_s), ALU.mult).then_inc(free[bl], 1)
                    step.wait()
                    V_.tensor_tensor(dst[:, 0, :], tmp[0], tmp[1], ALU.subtract).then_inc(sig, 1)
                    fl.wait_read(dve, hi + z, i)
                    fl.wait_read(dve, lo + z, i)
                    V_.tensor_tensor(dst[:, 1, :], tmp[2], tmp[3], ALU.add).then_inc(sig, 1)
                    dve.wait_ge(sig, hd * 2 + 2)
                if z == "r":
                    center(z, i)
                dec = decay[:, bass.ds(hd, 1), :].rearrange("p a c -> p (a c)") if z == "r" else decay[:, 0, :]
                b = fl.bank("SM" + z)
                fl.wait_full(dve, "SM" + z, i)
                V_.tensor_tensor(halves(s_meta[0:N_META, :]), pair(b)[0:N_META], halves(dec[0:N_META, :]),
                                 ALU.mult).then_inc(free[b], 1)
                for name, tiles in (("S01", (0, 1)), ("S23", (2, 3))):
                    b = fl.bank(name + z)
                    fl.wait_full(dve, name + z, i)
                    for g, t in enumerate(tiles):
                        n = POS - col0(t)
                        last = V_.tensor_tensor(s_t[:, t, 0:n], ps[:, b + g, 0:n], dec[:, 0:n], ALU.mult)
                    last.then_inc(free[b], 1)
                if z == "r":
                    gated(z, i)
                for m in range(4):
                    b = fl.bank(f"G{m}{z}")
                    dve.wait_ge(gt_done, hd * 4 + (m + 1))
                    V_.scalar_tensor_tensor(halves(gate[:, m, :]), halves(gate_t[:, m, :]), 1.0, pair(b),
                                            ALU.add, ALU.mult).then_inc(free[b], 1)

            head("a", 0)
            with dve.Fori(0, HEADS - 1) as i:
                step.rounds(i, 4)
                head("r", i)
            step.end(HEADS - 1)
            center("t", 0)
            gated("t", 0)
            dve.wait_ge(s_zeroed, 16)
            for hf in range(2):
                for name, t, n in ((f"W{hf}_01", 0, 2), (f"W{hf}_23", 2, 2)):
                    b = fl.bank(name)
                    fl.wait_full(dve, name)
                    hh = h[:, t:t + n, 512 * hf:512 * hf + 512]
                    V_.tensor_tensor(hh, ps[:, b:b + 2, :], hh, ALU.add).then_inc(free[b], 1)
                    if hf == 1:
                        for tt in (t, t + 1):
                            norm_tile(nrm["_m0"], tt, tt, xn)
                b = fl.bank(f"W{hf}_4")
                fl.wait_full(dve, f"W{hf}_4")
                hh = h[0:N_META, META, 512 * hf:512 * hf + 512]
                V_.tensor_tensor(hh, ps[0:N_META, b, :], hh, ALU.add).then_inc(free[b], 1)

            def experts(l):
                m, tiles, nt = mo[l], MOE_TILES[l], 5 - l
                step = Steps(dve, dsem_m[l])
                if l == 0:
                    step.done(V_.memset(lg[:, META, :], 0.0))
                feature_major(f"m{l}_", tiles[0], G_MOE[l])
                norm_tile(nrm[f"_m{l}"], nt - 1, tiles[-1], xn)
                for t in tiles[1:]:
                    feature_major(f"m{l}_", t, G_MOE[l])
                fl.wait_full(dve, f"LG{l}")
                if l == 0:
                    step.wait()
                    V_.tensor_copy(lg[0:N_META, META, :], ps[0:N_META, 0, 20 * META:20 * META + 20])
                V_.tensor_copy(flat(lg[:, 0:NT, :]), ps[:, 0, 0:20 * NT]).then_inc(free[0], 1)
                fl.wait_read(dve, f"LG{l}")
                g, e = lg[:, 0:nt, 0:GROUPS], lg[:, 0:nt, GROUPS:20]
                ge = e.rearrange("p t (g e) -> p t g e", g=GROUPS)
                rev = con[:, C_REV:C_REV + 4].unsqueeze(1).to_broadcast([128, nt, 4])

                def v(at, *shape):
                    return view(at, *shape)

                def over4(x):
                    return x.unsqueeze(2).to_broadcast([128, nt, 4])

                def first_max(src, top, eq, one):
                    step(V_.tensor_reduce(top, src, X, ALU.max))
                    step(V_.tensor_tensor(eq, src, over4(top), ALU.is_ge))
                    step(V_.tensor_tensor(eq, eq, rev, ALU.mult))
                    step(V_.tensor_reduce(v(T1, nt), eq, X, ALU.max))
                    step(V_.tensor_tensor(one, eq, over4(v(T1, nt)), ALU.is_equal))

                first_max(g, v(TOP, nt), v(EQ, nt, 4), v(OHG, nt, 4))
                V_.tensor_tensor(v(EG, nt, 4), g, over4(v(TOP, nt)), ALU.subtract).then_inc(m["eg_in"], 1)
                g4 = v(G44, nt, 4, 4)
                for t in range(nt):
                    last = V_.tensor_tensor(g4[:, t], ge[:, t],
                                            v(OHG, nt, 4)[:, t].unsqueeze(2).to_broadcast([128, 4, 4]), ALU.mult)
                step(last)
                step(V_.tensor_reduce(v(SEL, nt, 4), g4.rearrange("p t g e -> p t e g"), X, ALU.add))
                first_max(v(SEL, nt, 4), v(M1, nt), v(EQ, nt, 4), v(OH1, nt, 4))
                step(V_.scalar_tensor_tensor(v(SEL, nt, 4), v(OH1, nt, 4), -1e30, v(SEL, nt, 4), ALU.mult, ALU.add))
                first_max(v(SEL, nt, 4), v(M2, nt), v(EQ, nt, 4), v(OH2, nt, 4))
                V_.tensor_tensor(v(DX, nt), v(M2, nt), v(M1, nt), ALU.subtract).then_inc(m["d_in"], 1)
                if l == 0:
                    step(V_.tensor_tensor(v(OHG, nt, 4), v(OHG, nt, 4), over4(con[:, C_VALID:C_VALID + nt]), ALU.mult))
                for at, oh in ((MA, OH1), (MB, OH2)):
                    for t in range(nt):
                        last = V_.tensor_tensor(v(at, nt, 4, 4)[:, t],
                                                v(OHG, nt, 4)[:, t].unsqueeze(2).to_broadcast([128, 4, 4]),
                                                v(oh, nt, 4)[:, t].unsqueeze(1).to_broadcast([128, 4, 4]), ALU.mult)
                step(last)
                V_.tensor_tensor(masks(l)[:, 0:16 * nt], v(MA, 16 * nt), v(MB, 16 * nt), ALU.add)\
                    .then_inc(m["mask_ready"], 1)
                dve.wait_ge(m["eg_out"], 1)
                step(V_.tensor_reduce(v(T1, nt), v(EG, nt, 4), X, ALU.add))
                step(V_.reciprocal(v(TOP, nt), v(T1, nt)))
                dve.wait_ge(m["d_out"], 1)
                step(V_.tensor_scalar(v(T1, nt), v(DX, nt), 1.0, None, ALU.add))
                step(V_.reciprocal(v(T1, nt), v(T1, nt)))
                step(V_.tensor_tensor(v(W1, nt), v(TOP, nt), v(T1, nt), ALU.mult))
                step(V_.tensor_tensor(v(W2, nt), v(W1, nt), v(DX, nt), ALU.mult))
                fl.wait_full(dve, f"RK{l}")
                before = v(PRE, 6, 16)
                step(V_.memset(before[:, 0, :], 0.0))
                for t in range(nt):
                    step(V_.tensor_tensor(before[:, t + 1, :], ps[:, 2, 128 + 16 * t:144 + 16 * t], before[:, t, :], ALU.add))
                count = before[:, nt, :]
                step(V_.tensor_tensor(v(C5, 16, 4), count.unsqueeze(2).to_broadcast([128, 16, 4]),
                                      con[:, C_THR:C_THR + 4].unsqueeze(1).to_broadcast([128, 16, 4]), ALU.is_gt))
                step(V_.tensor_reduce(v(NB, 16), v(C5, 16, 4), X, ALU.add))
                step(V_.memset(v(Z16, 16), 0.0))
                step(V_.tensor_tensor_scan(v(INCL, 16), v(NB, 16), v(Z16, 16), 0.0, ALU.add, ALU.add))
                first = con[:, C_FIRST:C_FIRST + 16].unsqueeze(1).to_broadcast([128, nt, 16])
                step(V_.tensor_tensor(v(BASE, 16), v(INCL, 16), v(NB, 16), ALU.subtract))
                step(V_.tensor_tensor(v(BASE, 16), v(BASE, 16), con[:, C_OVER:C_OVER + 16], ALU.add))
                step(V_.tensor_scalar(v(BASE, 16), v(BASE, 16), float(BLK), None, ALU.mult))
                sl, over = v(SL, nt, 16), v(OV, nt, 16)
                V_.tensor_tensor(sl, ps[:, 2, 0:16 * nt].rearrange("p (t e) -> p t e", e=16), before[:, 0:nt, :],
                                 ALU.add).then_inc(free[2], 1)
                fl.wait_read(dve, f"RK{l}")
                step(V_.scalar_tensor_tensor(over, sl, BLK - 0.5, v(BASE, 16).unsqueeze(1).to_broadcast([128, nt, 16]),
                                             ALU.is_gt, ALU.mult))
                step(V_.tensor_tensor(sl, sl, first, ALU.add))
                step(V_.tensor_tensor(sl, sl, over, ALU.add))
                for n, at in enumerate((MA, MB)):
                    step(V_.tensor_tensor(v(at, nt, 16), v(at, nt, 16), sl, ALU.mult))
                    step(V_.tensor_reduce(v(SF, 2, 5)[:, n, 0:nt], v(at, nt, 16), X, ALU.add))
                V_.tensor_copy(slot_i[:, :, 0:nt], v(SF, 2, 5)[:, :, 0:nt]).then_inc(m["slot_ready"], 1)
                no = NBLK[l] - EXPERTS
                eb = v(EB, no, 16)[0:1]
                step(V_.tensor_tensor(eb, v(INCL, 16)[0:1].unsqueeze(1).to_broadcast([1, no, 16]),
                                      con[0:1, C_BLK:C_BLK + no].unsqueeze(2).to_broadcast([1, no, 16]), ALU.is_le))
                step(V_.tensor_reduce(v(EBS, no)[0:1], eb, X, ALU.add))
                V_.tensor_scalar(eb_i[0:1, l, 0:no], v(EBS, no)[0:1], float(EXPERTS - 1), None, ALU.min)\
                    .then_inc(m["eb_ready"], 1)

                def widen(k, i):
                    block_full(dve, l, B_ROWS, k, i)
                    for g in range(2):
                        last = gained(xgT[:, k % RING], 0, g, G_MOE[l], 0, BLK)
                    last.then_inc(free[B_ROWS], 1)

                def hidden(k, i):
                    b, j = gu_bank(k), k % RING
                    dve.wait_ge(m["tanh_done"], i * RING + (k + 1))
                    step(V_.scalar_tensor_tensor(hid1, th[:, j, :], 1.0, ps[:, b, 0:FF], ALU.add, ALU.mult))
                    V_.scalar_tensor_tensor(hid[:, j, :], hid1, 0.5, ps[:, b, FF:2 * FF], ALU.mult, ALU.mult)\
                        .then_inc(free[b], 1)

                def results_of(k, i):
                    j = k % RING
                    block_full(dve, l, B_YB, k, i)
                    dve.wait_ge(m[f"y_out{j}"], stage(k, i))
                    V_.tensor_copy(yo[:, j, 512:1024], ps[:, B_YB, :]).then_inc(free[B_YB], 1)

                for j in range(RING):
                    V_.memset(v(Z16, 16)[:, j:j + 1], 0.0).then_inc(m[f"y_out{j}"], 16)
                widen(0, 0)
                widen(1, 0)
                hidden(0, 0)
                rounds = (NBLK[l] - 2) // RING
                with dve.Fori(0, rounds) as i:
                    step.rounds(i, RING)
                    for k in range(1, 1 + RING):
                        widen(k + 1, i)
                        hidden(k, i)
                        results_of(k - 1, i)
                step.end(rounds)
                for k in range(1 + RING * rounds, NBLK[l]):
                    if k + 1 < NBLK[l]:
                        widen(k + 1, 0)
                    hidden(k, 0)
                    results_of(k - 1, 0)
                results_of(NBLK[l] - 1, 0)
                def combine(t):
                    r, n = rows(t), tiles.index(t)
                    dve.wait_ge(m[f"gathered{t}"], 32)
                    step(V_.scalar_tensor_tensor(h[0:r, t, :], gat[0:r, t, 0, :], v(W1, nt)[0:r, t:t + 1],
                                                 h[0:r, t, :], ALU.mult, ALU.add))
                    V_.scalar_tensor_tensor(h[0:r, t, :], gat[0:r, t, 1, :], v(W2, nt)[0:r, t:t + 1],
                                            h[0:r, t, :], ALU.mult, ALU.add).then_inc(m["gath_used"], 1)
                return combine

            combine = experts(0)

            step = Steps(dve, dsem["a"])

            def kv_features(t):
                b = fl.bank(f"n1_{t}")
                fl.wait_full(dve, f"n1_{t}")
                for gx in range(2):
                    last = gained(xTk, b, gx, G_KV, col0(t), rows(t))
                if t != META:
                    for gx in range(2):
                        last = gained(xT, b, gx, G_SWA, col0(t), rows(t))
                last.then_inc(free[b], 1)

            for n in range(len(TILES5) + 2):
                if n < len(TILES5):
                    combine(TILES5[n])
                if 1 <= n <= len(TILES5):
                    norm_tile(nrm["_s"], n - 1, TILES5[n - 1], xn1)
                if n >= 2:
                    kv_features(TILES5[n - 2])
            dve.wait_ge(s_swat, 80)

            def rotate(x, t, r, nh, A_, B_, outs):
                cos = stab[0:r, 32 * t:32 * t + 32].unsqueeze(1)
                sin = stab[0:r, 160 + 64 * t:160 + 64 * t + 64]
                xv = x.rearrange("p (h c) -> p h c", c=32)
                step.done(V_.tensor_tensor(A_.rearrange("p (h c) -> p h c", c=32), xv,
                                           cos.to_broadcast([r, 2 * nh, 32]), ALU.mult))
                x4, b4 = (y.rearrange("p (h s c) -> p h s c", s=2, c=32) for y in (x, B_))
                for s in range(2):
                    step.done(V_.tensor_tensor(b4[:, :, s, :], x4[:, :, 1 - s, :],
                                               sin[:, 32 * s:32 * s + 32].unsqueeze(1).to_broadcast([r, nh, 32]), ALU.mult))
                step.wait()
                for o in outs:
                    last = V_.tensor_tensor(o, A_.rearrange("p (h c) -> p h c", c=64),
                                            B_.rearrange("p (h c) -> p h c", c=64), ALU.add)
                return last

            for n, t in enumerate(TILES5):
                b, r = fl.bank(f"KV{t}"), rows(t)
                fl.wait_full(dve, f"KV{t}")
                if n >= 2:
                    dve.wait_ge(V_ready, n - 1)
                V_.tensor_tensor(kvs[0:r, n % 2, :], ps[0:r, b, :], kvb[0:r, :], ALU.add).then_inc(free[b], 1)
                fl.wait_read(dve, f"KV{t}")
                if n >= 2:
                    fl.wait_full(dve, f"KT{TILES5[n - 2]}")
                if n:
                    dve.wait_ge(kr_ready, n)
                rotate(kvs[0:r, n % 2, 0:256], t, r, 4, flat(kA)[0:r], flat(kB)[0:r],
                       [kr[0:r, n % 2, :, 0:64], kr[0:r, n % 2, :, 64:128]]).then_inc(kr_ready, 1)

            def rotate_q(t):
                for c, name in enumerate((f"Qa{t}", f"Qb{t}")):
                    fl.wait_full(dve, name)
                    if c == 0 and t:
                        fl.wait_full(dve, f"QT{t - 1}")
                        dve.wait_ge(q_rot, t)
                    V_.tensor_tensor(qs[:, 512 * c:512 * c + 512], ps[:, 4 + c, :], qb[:, 512 * c:512 * c + 512],
                                     ALU.add).then_inc(free[4 + c], 1)
                fl.wait_read(dve, f"Qa{t}")
                fl.wait_read(dve, f"Qb{t}")
                rotate(qs, t, 128, 16, qA, qr, [qr.rearrange("p (h c) -> p h c", c=64)]).then_inc(q_rot, 1)

            rotate_q(0)
            for t in range(NT):
                mask = stab[:, 480 + 256 * min(t, 1):480 + 256 * min(t, 1) + 256].unsqueeze(1).to_broadcast([128, 2, 256])
                for g in range(2):
                    for p in range(4 * g, 4 * g + 4):
                        b = fl.bank(f"S{t}_{p}")
                        fl.wait_full(dve, f"S{t}_{p}")
                        h0 = head_pair(p)[0]
                        V_.scalar_tensor_tensor(P[:, h0:h0 + 3:2, :], ps[:, b, :].rearrange("p (h k) -> p h k", h=2),
                                                HD ** -0.5, mask, ALU.mult, ALU.add).then_inc(free[b], 1)
                        fl.wait_read(dve, f"S{t}_{p}")
                        step.done(V_.tensor_reduce(mx[:, h0:h0 + 3:2], P[:, h0:h0 + 3:2, :], X, ALU.max))
                    step.wait()
                    c = slice(8 * g, 8 * g + 8)
                    step(V_.tensor_tensor(mx[:, c], mx[:, c], sink_b[:, c], ALU.max))
                    if t:
                        dve.wait_ge(p_exp, 16 * t)
                        dve.wait_ge(snk_exp, 2 * t)
                    step(V_.tensor_tensor(es[:, c], sink_b[:, c], mx[:, c], ALU.subtract))
                    V_.tensor_scalar(nmx[:, c], mx[:, c], -1.0, None, ALU.mult).then_inc(m_ready, 1)
                if t + 1 < NT:
                    rotate_q(t + 1)
                for p in range(0, 8, 2):
                    b = fl.bank(f"PT{t}_{p}")
                    fl.wait_full(dve, f"PT{t}_{p}")
                    V_.tensor_copy(flat(PT[:, 0]), ps[:, b, :]).then_inc(free[b], 1)
                dve.wait_ge(snk_exp, 2 * t + 2)
                dve.wait_ge(p_exp, 16 * t + 16)
                step(V_.tensor_tensor(rc, sm, sx, ALU.add))
                step(V_.reciprocal(rc, rc))
                fl.wait_full(dve, f"AV{t}")
                if t:
                    fl.wait_full(dve, f"OT{t - 1}")
                V_.tensor_tensor(oN.rearrange("p (h c) -> p h c", c=64),
                                 flat(ps[:, 6:8, :]).rearrange("p (h c) -> p h c", c=64),
                                 rc.unsqueeze(2).to_broadcast([128, 16, 64]), ALU.mult).then_inc(free[6], 1)
                if t == NT - 1:
                    for n in range(t):
                        norm_tile(nrm["_m1"], n, n, xn)
                fl.wait_full(dve, f"WO{t}")
                dve.wait_ge(bo_added, t + 1)
                V_.tensor_tensor(h[:, t, :], flat(ps[:, 4:6, :]), h[:, t, :], ALU.add).then_inc(free[4], 1)
            combine = experts(1)
            dve.wait_ge(fin_in, 16)
            for n in range(NT + 1):
                if n < NT:
                    combine(n)
                if n:
                    t = n - 1
                    dve.wait_ge(nrm["_f"]["rstd_done"], t + 1)
                    V_.scalar_tensor_tensor(fo[:, t, :], h[:, t, :], rstd[:, t:t + 1], fin_g, ALU.mult, ALU.mult)\
                        .then_inc(fin_done, 1)

        @block.gpsimd
        def _(pool):
            G = nc.gpsimd

            def deviations(tiles, sig):
                for n, t in enumerate(tiles):
                    r = rows(t)
                    pool.wait_ge(sig["sq_done"], n + 1)
                    G.tensor_scalar(var[0:r, t:t + 1], ss[0:r, t:t + 1], 1.0 / D, EPS, ALU.mult, ALU.add)\
                        .then_inc(sig["var_done"], 1)
                    pool.wait_ge(sig["var_done"], n + 1)
                    G.tensor_tensor(rstd[0:r, t:t + 1], var[0:r, t:t + 1], con[0:r, C_NH:C_NH + 1], ALU.pow)\
                        .then_inc(sig["rstd_done"], 1)

            pool.wait_ge(s_const, 16)
            deviations(TILES5, nrm["_r"])

            def experts(l):
                m, tiles = mo[l], MOE_TILES[l]
                deviations(tiles, nrm[f"_m{l}"])
                pool.wait_ge(m["slot_ready"], 1)
                if l == 0:
                    pool.wait_ge(s_zeroed, 16)
                for t in tiles:
                    r = rows(t)
                    for c in range(2):
                        G.indirect_dma_start(slot_rows, bass.IndirectOffsetOnAxis(slot_i[0:r, c, t:t + 1], 0),
                                             xn[0:r, t, :], None).then_inc(m["scattered"], 16)
                for j in range(RING):
                    pool.wait_ge(m[f"y_out{j}"], 16 * (len(range(j, NBLK[l], RING)) + 1))
                for t in TILES5[l:]:
                    r = rows(t)
                    for c in range(2):
                        G.indirect_dma_start(gat[0:r, t, c, :], None, slot_out,
                                             bass.IndirectOffsetOnAxis(slot_i[0:r, c, t:t + 1], 0))\
                            .then_inc(m[f"gathered{t}"], 16)

            experts(0)
            deviations(TILES5, nrm["_s"])
            pool.wait_ge(s_swat, 80)
            for t in range(NT):
                pool.wait_ge(nrm["_s"]["xn_done"], t + 2)
                G.tensor_tensor(h[:, t, :], h[:, t, :], bo, ALU.add).then_inc(bo_added, 1)
            G.memset(flat(VX), 0.0).then_inc(VX_zero, 1)
            for n, t in enumerate(TILES5):
                r = rows(t)
                fl.wait_read(pool, f"KV{t}")
                G.tensor_copy(V[0:r, t, :], kvs[0:r, n % 2, 256:512]).then_inc(V_ready, 1)
            pool.wait_ge(VX_zero, 1)
            pool.wait_ge(V_ready, 5)
            for t in range(NT):
                G.tensor_copy(VX[0:N_META, t, :], V[0:N_META, META, :]).then_inc(VX_ready, 1)
                if t:
                    G.tensor_copy(VX[64:128, t, :], V[64:128, t - 1, :]).then_inc(VX_ready, 1)
            experts(1)
            deviations(MOE_TILES[1], nrm["_f"])



_NAMES = ["x", "meta_tokens", "kv_b", "swa_b_q", "swa_sinks", "swa_b_o", "final_norm"]


def _chunks(w):
    kk, nn = w.shape[0] // D, w.shape[1] // 512
    w = w.reshape(kk, KT, 128, nn, 512).transpose(3, 0, 2, 1, 4)
    return np.ascontiguousarray(w.reshape(nn * kk, 128, KT * 512))


def _layout(i):
    out = {n: np.ascontiguousarray(i[n]) for n in _NAMES}
    w = i["ret_w_in"][0]
    heads = []
    for hd in range(HEADS):
        qk = np.concatenate([w[:, QK * hd:QK * hd + QK], w[:, D + QK * hd:D + QK * hd + QK]], axis=1)
        vg = [w[:, 2 * D + n * HEADS * VD + VD * hd:2 * D + n * HEADS * VD + VD * hd + VD] for n in range(2)]
        heads.append(np.stack([_chunks(x)[0] for x in (qk, *vg)]))
    out["w_ret"] = np.stack(heads)
    out["w_ret_out"] = _chunks(i["ret_w_out"][0])
    out["w_kv"], out["w_q"], out["w_o"] = _chunks(i["kv_w"]), _chunks(i["swa_w_q"][0]), _chunks(i["swa_w_o"][0])
    gu = np.concatenate([i["moe_w_gate"], i["moe_w_up"]], axis=3)
    out["w_gu"] = np.ascontiguousarray(gu.reshape(2, EXPERTS, KT, 128, 512).transpose(0, 1, 3, 2, 4)).reshape(
        2, EXPERTS, 128, KT * 512)
    dn = i["moe_w_down"].reshape(2, EXPERTS, 2, 128, D).transpose(0, 1, 3, 2, 4)
    out["w_down"] = np.ascontiguousarray(dn).reshape(2, EXPERTS, 128, 2 * D)
    route = np.concatenate([i["moe_w_group"], i["moe_w_router"]], axis=2)
    out["w_route"] = np.ascontiguousarray(route.reshape(2, KT, 128, 20).transpose(2, 0, 1, 3)).reshape(128, -1)
    g = np.stack([i["ret_norm"][0], i["kv_norm"], i["swa_norm"][0], i["moe_norm"][0], i["moe_norm"][1]])
    out["gains"] = np.ascontiguousarray(g.reshape(5, KT, 128).transpose(2, 0, 1)).reshape(128, -1)
    return out


def kernel(**inputs):
    import concourse.bacc as _bacc
    from concourse.bass_utils import run_bass_kernel_spmd as _run

    nc = _bacc.Bacc("TRN2", target_bir_lowering=False, num_devices=1)
    arrays = _layout({n: np.asarray(v) for n, v in inputs.items()})
    arrays["t_con"], arrays["t_ret"], arrays["t_swa"] = tables()
    aps = {n: nc.dram_tensor(f"in_{n}", v.shape, mybir.dt.from_np(v.dtype), kind="ExternalInput").ap()
           for n, v in arrays.items()}
    out = nc.dram_tensor("out", (1, SEQ, D), mybir.dt.float32, kind="ExternalOutput").ap()
    build(nc, aps, out)
    return _run(nc, [{f"in_{n}": v for n, v in arrays.items()}], core_ids=[0]).results[0]["out"]
```

```python
import numpy as np
from contextlib import ExitStack
import concourse.bass as bass
from concourse import mybir

D = 1024
KT = D // 128
SEQ, N_META, CHUNK = 512, 16, 64
POS = N_META + SEQ
NT = SEQ // 128
META = NT
HALF = POS // 2
HEADS, QK, VD = 4, 256, 512
KV_HEADS, Q_HEADS, HD = 4, 16, 64
GROUPS, PER_GROUP = 4, 4
EXPERTS = GROUPS * PER_GROUP
FF = 256
EPS = 1e-6
BLK = 128
RING = 3


def blocks_needed(tokens):
    return EXPERTS + (2 * tokens - 1) // BLK


NBLK = [blocks_needed(POS), blocks_needed(SEQ)]
MAXBLK = max(NBLK)
SLOTS = MAXBLK * BLK

C_ID, C_ONE, C_512, C_TRI = 0, 128, 256, 384
C_REV, C_THR, C_BLK, C_VALID, C_NH, C_EPS, C_FIRST, C_OVER = 512, 516, 521, 545, 550, 555, 556, 572
NCONST = 588
NRT = 2 * POS + HEADS * POS
NST = 5 * 32 * 3 + 512


def tables():
    f = np.float32
    c = np.zeros((128, NCONST), f)
    c[:, C_ID:C_ID + 128] = np.eye(128)
    c[:, C_ONE:C_ONE + 128] = 1.0
    c[:, C_512:C_512 + 128] = 1.0 / VD
    c[:, C_TRI:C_TRI + 128] = np.arange(128)[:, None] < np.arange(128)[None, :]
    c[:, C_REV:C_REV + 4] = [4, 3, 2, 1]
    c[:, C_THR:C_THR + 4] = np.arange(1, 5) * BLK
    c[:, C_FIRST:C_FIRST + EXPERTS] = np.arange(EXPERTS) * BLK
    c[:, C_OVER:C_OVER + EXPERTS] = EXPERTS - 1 - np.arange(EXPERTS)
    c[:, C_BLK:C_BLK + MAXBLK] = np.arange(MAXBLK)
    c[:, C_VALID:C_VALID + 5] = 1.0
    c[N_META:, C_VALID + META] = 0.0
    c[:, C_NH:C_NH + 5] = -0.5
    c[:, C_EPS] = EPS
    r = np.zeros((128, NRT), f)
    inv = (f(10000.0) ** (-np.arange(128, dtype=f) / f(128))).astype(f)
    ang = np.arange(POS, dtype=f)[None, :] * inv[:, None]
    r[:, 0:POS], r[:, POS:2 * POS] = np.cos(ang), np.sin(ang)
    lg = np.log1p(-np.exp2(-5.0 - np.arange(HEADS)))
    diff = np.arange(POS)[None, :] - np.arange(128)[:, None]
    for h in range(HEADS):
        dec = np.where(diff >= 0, np.exp(lg[h] * np.maximum(diff, 0)), 0.0) * QK ** -0.5
        r[:, 2 * POS + h * POS:2 * POS + (h + 1) * POS] = dec
    s = np.zeros((128, NST), f)
    inv = (f(10000.0) ** (-np.arange(32, dtype=f) / f(32))).astype(f)
    for t in range(5):
        pos = np.arange(128, dtype=f) + (0 if t == META else N_META + 128 * t)
        ang = pos[:, None] * inv[None, :]
        s[:, t * 32:t * 32 + 32] = np.cos(ang)
        s[:, 160 + t * 64:160 + t * 64 + 32] = -np.sin(ang)
        s[:, 160 + t * 64 + 32:160 + t * 64 + 64] = np.sin(ang)
    for v in range(2):
        m = np.full((128, 256), -1e30, f)
        m[:, 128:144] = 0.0
        m[0:64, 0:64] = 0.0
        m[64:128, 0:128] = 0.0
        if v:
            m[0:64, 192:256] = 0.0
        s[:, 480 + 256 * v:480 + 256 * v + 256] = m
    return c, r, s


class Fills:

    def __init__(self, full, free):
        self.full, self.free = full, free
        self.total = [0] * 8
        self.at = {}

    def phase(self, order, rounds=1):
        per = [sum(1 for _, b in order if b == k) for k in range(8)]
        seen = list(self.total)
        for name, b in order:
            assert name not in self.at, name
            self.at[name] = (b, seen[b], per[b])
            seen[b] += 1
        self.total = [self.total[k] + rounds * per[k] for k in range(8)]
        return list(self.total)

    def bank(self, name):
        return self.at[name][0]

    def wait_free(self, eng, name, i=0):
        b, n, per = self.at[name]
        if n or not isinstance(i, int):
            eng.wait_ge(self.free[b], i * per + n)

    def wait_full(self, eng, name, i=0):
        b, n, per = self.at[name]
        eng.wait_ge(self.full[b], i * per + (n + 1))

    def wait_read(self, eng, name, i=0):
        b, n, per = self.at[name]
        eng.wait_ge(self.free[b], i * per + (n + 1))


class Steps:

    def __init__(self, eng, sem):
        self.eng, self.sem, self.n, self.i, self.per, self.off = eng, sem, 0, None, 0, 0

    def rounds(self, i, per):
        self.i, self.per, self.off = i, per, 0

    def end(self, rounds):
        assert self.off == self.per, (self.off, self.per)
        self.n, self.i = self.n + rounds * self.per, None

    def count(self):
        return self.n if self.i is None else self.i * self.per + (self.n + self.off)

    def done(self, ins):
        ins.then_inc(self.sem, 1)
        if self.i is None:
            self.n += 1
        else:
            self.off += 1

    def wait(self):
        self.eng.wait_ge(self.sem, self.count())

    def __call__(self, ins):
        self.done(ins)
        self.wait()


def build(nc, a, out, dbg=None):
    F, I, R = mybir.dt.float32, mybir.dt.int32, mybir.dt.float32r
    ALU, ACT, AX = mybir.AluOpType, mybir.ActivationFunctionType, mybir.AxisListType
    X, XY = AX.X, AX.XY
    ctx = ExitStack()
    with ctx:
        def sem(name):
            return ctx.enter_context(nc.semaphore(name))

        def sb(name, shape, dt=F):
            return ctx.enter_context(nc.sbuf_tensor(name, shape, dt))

        def col0(t):
            return 0 if t == META else N_META + 128 * t

        def rows(t):
            return N_META if t == META else 128

        con = sb("con", [128, NCONST])
        ident, ones, mean512, tri = (con[:, c:c + 128] for c in (C_ID, C_ONE, C_512, C_TRI))
        gains = sb("gains", [128, 5, KT])
        G_RET, G_KV, G_SWA, G_MOE = 0, 1, 2, (3, 4)
        wr = sb("wr", [128, 2, KT, 20])
        h = sb("h", [128, 5, D])
        ss, var, rstd = sb("ss", [128, 5]), sb("var", [128, 5]), sb("rstd", [128, 5])
        eb_i = sb("eb_i", [1, 2, MAXBLK - EXPERTS], I)
        slot_i = sb("slot_i", [128, 2, 5], I)
        ps = ctx.enter_context(nc.psum_tensor("ps", [128, 8, 512], F))

        ARENA = 29440
        shared = (("ring", [128, RING, KT * 512]),
                  ("xT", [128, KT, POS]),
                  ("arena", [128, ARENA]))
        with ExitStack() as first:
            ring, xT, arena = (first.enter_context(nc.sbuf_tensor(n, shape, F)) for n, shape in shared)
        ring_r, xT_r = (sb(n + "_r", shape, R) for n, shape in shared[:2])
        y_lo = sb("y_lo", [128, 16, POS], R)
        x_hi = sb("x_hi", [128, KT, POS], R)
        y_hi_b = sb("y_hi_b", [128, KT, POS], R)
        sb("left_out", [128, 2 * POS], R)
        w_hi_b = sb("w_hi_b", [128, KT * 512], R)

        class Carve:

            def __init__(self):
                self.at = 0

            def __call__(self, *shape):
                n = int(np.prod(shape))
                v = arena[:, self.at:self.at + n]
                self.at += n
                assert self.at <= ARENA, self.at
                if len(shape) == 1:
                    return v
                names = "abcd"[:len(shape)]
                return v.rearrange(f"p ({' '.join(names)}) -> p {' '.join(names)}",
                                   **dict(zip(names[1:], shape[1:])))

        cv = Carve()
        ret_xn = cv(5, D)
        cv.at = 0
        yT = cv(16, POS)
        zero = arena[:, 14 * POS:14 * POS + D]
        cv(KT, POS)
        ROPE = cv.at
        rope_c, rope_s = cv(POS), cv(POS)
        decay = cv(HEADS, POS)
        qT, kT = cv(2, POS), cv(2, POS)
        VALUES = cv.at
        assert VALUES - ROPE == (KT + 2) * POS
        v_tm = cv(5, VD)
        s_meta, s_t = cv(POS), cv(NT, 512)
        gate = cv(4, POS)
        o_fm, sq = cv(4, POS), cv(4, POS)
        rs = sq[:, 0, :]
        ret_junk = s_t.rearrange("p a b -> p (a b)")[:, 0:D]
        x_lo = xT_r
        y_hi = [x_hi, y_hi_b]

        def pieces(chunk):
            return chunk.rearrange("p (m k c) -> p m k c", m=4, c=128)

        w_raw = [pieces(ring[:, n]) for n in range(2)]
        w_lo = [pieces(ring_r[:, n]) for n in range(2)]
        w_hi = [pieces(ring_r[:, 2]), pieces(w_hi_b[:, :])]
        cv = Carve()
        down = cv(RING, 2, D)
        xg = cv(RING, D)
        xgT = cv(RING, KT, 128)
        yo = cv(RING, D)
        moe_junk = [arena[:, VALUES + KT * 512:VALUES + KT * 512 + D], arena[:, cv.at:cv.at + D]]
        cv.at = 5 * D + KT * POS
        gat = cv(5, 2, D)
        next_junk = arena[:, cv.at:cv.at + D]
        th, hid1, hid = cv(RING, FF), cv(FF), cv(RING, FF)
        hidT = cv(2, 128)
        lg = cv(5, 20)
        small = cv(2200)
        xn = cv(5, D)
        cv = Carve()
        xn1 = cv(5, D)
        xTk = cv(KT, POS)
        kT2 = cv(4, POS)
        kr, kA, kB = cv(2, 4, 128), cv(4, 64), cv(4, 64)
        kvs = cv(2, 512)
        V, VX = cv(5, 256), cv(NT, 256)
        qs, qA, qr, oN = cv(D), cv(D), cv(D), cv(D)
        qT1, oT1 = cv(KT, 128), cv(KT, 128)
        stab = cv(NST)
        sink_b, mx, nmx, es, sx, sm, rc = (cv(16) for _ in range(7))
        kvb, qb, bo = cv(512), cv(D), cv(D)
        PT = cv(2, 4, 128)
        P = arena[:, 0:16 * 256].rearrange("p (h k) -> p h k", h=16)
        wo_b = arena[:, 5 * D:5 * D + KT * 512].rearrange("p (k n) -> p k n", k=KT)
        cv = Carve()
        fo = cv(NT, D)
        fin_g = cv(D)

        slot_rows = nc.dram_tensor("slot_rows", (SLOTS, D), F).ap()
        slot_out = nc.dram_tensor("slot_out", (SLOTS, D), F).ap()

        full = [sem(f"bank_full{b}") for b in range(8)]
        free = [sem(f"bank_free{b}") for b in range(8)]
        fl = Fills(full, free)
        w_in = [sem(f"weights_in{s}") for s in range(RING)]
        x_in = [sem(f"x_in_{t}") for t in range(5)]
        piece_in = [[sem(f"w_piece_in{n}_{m}") for m in range(4)] for n in range(2)]
        hi_made, lo_made, x_hi_made, x_lo_made, y_hi_made, y_split = (sem(n) for n in (
            "w_hi_made", "w_lo_made", "x_hi_made", "x_lo_made", "y_hi_made", "y_split"))
        s_const, s_zero, s_zeroed, s_rt, s_gains = (sem(n) for n in (
            "const_in", "zero_made", "slots_zeroed", "ret_tables_in", "gains_in"))

        TILES5 = [META, 0, 1, 2, 3]
        MOE_TILES = [[0, 1, 2, 3, META], [0, 1, 2, 3]]
        A, B, C, E = 0, 2, 4, 6

        def norm_plan(tag, tiles):
            fl.phase([(f"{tag}{t}", 2 * (n % 4)) for n, t in enumerate(tiles)])

        norm_plan("n0_", TILES5)

        def head_plan(z, rounds):
            names = ("Q1", "Q2", "K1", "K2", "MU", "V01", "V23", "V4", "SM", "S01", "S23", "VAR",
                     "G0", "G1", "G2", "G3", "O0", "O1", "O2", "O3")
            fl.phase([(x + z, (A, B, C, E)[n % 4]) for n, x in enumerate(names)
                      if z != "a" or x not in ("MU", "VAR")], rounds)

        head_plan("a", 1)
        head_plan("r", HEADS - 2)
        head_plan("s", 1)
        fl.phase([("MUt", A), ("VARt", A), ("W0_01", B), ("W0_23", C), ("W0_4", E),
                  ("W1_01", A), ("W1_23", B), ("W1_4", C)])
        t_blocks, t_blocks_end = {}, {}

        def moe_plan(l):
            norm_plan(f"m{l}_", MOE_TILES[l])
            fl.phase([(f"LG{l}", 0), (f"RK{l}", 2)])
            t_blocks[l] = list(fl.total)
            for b in range(8):
                fl.total[b] += (0, len(range(b - 2, NBLK[l], RING)), NBLK[l])[(b in (2, 3, 4)) + 2 * (b in (0, 5, 6, 7))]
            t_blocks_end[l] = list(fl.total)

        moe_plan(0)
        norm_plan("n1_", TILES5)
        t_norm1 = list(fl.total)
        fl.phase([(f"KV{t}", n) for n, t in enumerate(TILES5)])
        fl.phase([(f"KT{t}", 5 + n % 3) for n, t in enumerate(TILES5)])
        t_kv = list(fl.total)
        plan = [("Qa0", 4), ("Qb0", 5), ("QT0", 0)]
        for t in range(NT):
            plan += [(f"S{t}_{p}", p % 6) for p in range(8)]
            if t + 1 < NT:
                plan += [(f"Qa{t + 1}", 4), (f"Qb{t + 1}", 5)]
            plan += [(f"AV{t}", 6)] + [(f"PT{t}_{p}", p % 4) for p in range(8)]
            if t + 1 < NT:
                plan += [(f"QT{t + 1}", 0)]
            plan += [(f"OT{t}", 2), (f"WO{t}", 4)]
        fl.phase(plan)
        t_swa = list(fl.total)
        moe_plan(1)

        def all_read(eng, totals):
            for b in range(8):
                if totals[b]:
                    eng.wait_ge(free[b], totals[b])

        def pair(b):
            return ps[:, b:b + 2, 0:HALF]

        def halves(ap):
            return ap.rearrange("p (g c) -> p g c", g=2)

        def sigs(names, tag):
            return {n: sem(f"{n}{tag}") for n in names.split()}

        nrm = {k: sigs("sq_done var_done rstd_done xn_done", k) for k in ("_r", "_m0", "_s", "_m1", "_f")}
        q_ready, k_ready, gt_done, squared, y_ready, wo_used = (sem(n) for n in (
            "q_ready", "k_ready", "gate_tanh_done", "squared", "y_ready", "w_out_used"))
        mo = [sigs("lg_ready eg_in eg_out d_in d_out mask_ready eb_ready slot_ready scattered blocks_stored "
                   "tanh_done y_out0 y_out1 y_out2 x_in0 x_in1 x_in2 down_in0 down_in1 down_in2 "
                   "gathered0 gathered1 gathered2 gathered3 gathered4 gath_used", f"_{l}") for l in range(2)]
        s_swat, kv_evac, kr_ready, V_ready, VX_zero, VX_ready = (sem(n) for n in (
            "swa_tables_in", "kv_evac", "k_rotated", "V_ready", "VX_zeroed", "VX_ready"))
        q_rot, m_ready, p_exp, snk_exp, bo_added = (sem(n) for n in (
            "q_rotated", "max_ready", "p_exp", "sink_exp", "bo_added"))
        wo_b_in = sem("w_o_b_in")
        fin_done, s_out, fin_in = sem("final_done"), sem("out_stored"), sem("final_gain_in")
        dsem = {k: sem(f"dve_steps_{k}") for k in "nraskf"}
        dsem_m = [sem(f"dve_steps_moe{l}") for l in range(2)]

        N_M = [0, NBLK[0] + 4]
        N_KV = NBLK[0]
        N_Q, N_O = N_KV + 1, N_KV + 3

        def w_at(n):
            return ring[:, n % RING].rearrange("p (k c) -> p k c", k=KT)

        def w_wait(eng, n, i=0):
            eng.wait_ge(w_in[n % RING], i * 16 + 16 * (n // RING + 1))

        QK_, V_C, G_ = 0, 1, 2

        def head_of(z, i):
            return {"a": 0, "r": i + 1, "s": HEADS - 1}[z]

        def piece_number(z, i, c, m):
            return i * 12 + (12 + 4 * c + m + 1) if z == "r" else 12 * head_of(z, i) + 4 * c + m + 1

        def out_piece_number(n, m):
            return 12 * HEADS + 4 * n + m + 1

        def piece_arrived(eng, z, i, c, m):
            if c == V_C:
                eng.wait_ge(piece_in[1][m], i * 16 + 32 if z == "r" else 16 * head_of(z, i) + 16)
            else:
                late = 16 if c == G_ else 0
                eng.wait_ge(piece_in[0][m], i * 32 + (48 + late) if z == "r" else 32 * head_of(z, i) + 16 + late)

        def out_piece_arrived(eng, n, m):
            eng.wait_ge(piece_in[1 - n % 2][m], 16 * ((HEADS if n % 2 == 0 else 2 * HEADS) + n // 2 + 1))

        def out_chunk_used(eng, n):
            if n % 2:
                fl.wait_full(eng, f"W{n // 2}_4")
            else:
                eng.wait_ge(wo_used, n // 2 + 1)

        def flat(ap):
            return ap.rearrange("p a b -> p (a b)")

        def view(at, *shape):
            v = small[:, at:at + int(np.prod(shape))]
            if len(shape) == 1:
                return v
            names = "abc"[:len(shape)]
            return v.rearrange(f"p ({' '.join(names)}) -> p {' '.join(names)}", **dict(zip(names[1:], shape[1:])))

        sizes = dict(MASK=80, OV=80, T1=5, TOP=5, EQ=20, OHG=20, EG=20, G44=80, SEL=20, M1=5, M2=5, OH1=20, OH2=20, DX=5,
                     MA=80, MB=80, W1=5, W2=5, PRE=96, C5=80, NB=16, Z16=16, INCL=16, EB=16 * MAXBLK, EBS=MAXBLK,
                     BASE=16, SL=80, SF=10)
        ends = np.cumsum([0] + list(sizes.values())).tolist()
        (MASK, OV, T1, TOP, EQ, OHG, EG, G44, SEL, M1, M2, OH1, OH2, DX, MA, MB, W1, W2, PRE, C5, NB, Z16, INCL, EB, EBS,
         BASE, SL, SF) = ends[:-1]
        block = ctx.enter_context(nc.Block())

        B_ROWS, B_HID, B_YA, B_YB = 0, 5, 6, 7

        def gu_bank(k):
            return 2 + k % RING

        def block_count(l, b, k, i):
            if b in (2, 3, 4):
                return i + (t_blocks[l][b] + k // RING + 1)
            return i * RING + (t_blocks[l][b] + k + 1)

        def block_full(eng, l, b, k, i=0):
            eng.wait_ge(full[b], block_count(l, b, k, i))

        def block_read(eng, l, b, k, i=0):
            eng.wait_ge(free[b], block_count(l, b, k, i))

        def stage(k, i, unit=16):
            return i * unit + unit * (k // RING + 1)

        def block_index(k, i):
            return slice(k, k + 1) if isinstance(i, int) else bass.ds(i * RING + k, 1)

        def outputs_read(eng, n):
            for m in range(4):
                b, at, _ = fl.at[f"O{m}a"]
                per = fl.at[f"O{m}r"][2]
                eng.wait_ge(free[b], n * per + (at + 1))

        def head_pair(p):
            return (4 * (p // 2) + p % 2, 4 * (p // 2) + p % 2 + 2)

        def masks(l):
            return small[:, 0:EXPERTS * 5]

        @block.sync
        def _(sp):
            def chunk(n, src):
                sp.dma_start(ring[:, n % RING], src).then_inc(w_in[n % RING], 16)

            for t in range(NT):
                sp.dma_start(h[:, t, :], a["x"][0, 128 * t:128 * t + 128, :]).then_inc(x_in[t], 16)

            def piece(slot, m, src):
                sp.dma_start(w_raw[slot][:, m].rearrange("p k c -> p (k c)"), src).then_inc(piece_in[slot][m], 16)

            for slot, c in ((0, QK_), (1, V_C)):
                for m in range(4):
                    piece(slot, m, a["w_ret"][0, c, m])

            def head(z, i):
                w = a["w_ret"][1:HEADS]
                for m, last in enumerate(("Q1", "Q2", "K1", "K2")):
                    fl.wait_full(sp, last + z, i)
                    piece(0, m, w[bass.ds(i, 1), G_, m].rearrange("a p c -> p (a c)") if z == "r" else
                          a["w_ret"][head_of(z, i), G_, m])
                fl.wait_full(sp, "V4" + z, i)
                for m in range(4):
                    piece(1, m, a["w_ret_out"][0, m] if z == "s" else a["w_ret"][1, V_C, m] if z == "a" else
                          w[1:][bass.ds(i, 1), V_C, m].rearrange("a p c -> p (a c)"))
                for m in range(4):
                    fl.wait_full(sp, f"G{m}{z}", i)
                    piece(0, m, a["w_ret_out"][1, m] if z == "s" else a["w_ret"][1, QK_, m] if z == "a" else
                          w[1:][bass.ds(i, 1), QK_, m].rearrange("a p c -> p (a c)"))

            head("a", 0)
            with sp.Fori(0, HEADS - 2) as i:
                head("r", i)
            head("s", 0)
            for n in (2, 3):
                out_chunk_used(sp, n - 2)
                for m in range(4):
                    piece(1 - n % 2, m, a["w_ret_out"][n, m])

            def first_weights(l, readers):
                for k, used in readers:
                    used()
                    chunk(N_M[l] + k, a["w_gu"][l, k])
                for k in range(RING):
                    sp.dma_start(flat(down[:, k]), a["w_down"][l, k]).then_inc(mo[l][f"down_in{k}"], 16)

            def experts(l):
                m = mo[l]
                gu_d, dn_d = a["w_gu"][l], a["w_down"][l]
                x_blocks = slot_rows.rearrange("(b p) c -> b p c", p=BLK)

                def load_rows(k, i):
                    sp.dma_start(xg[:, k % RING, :], x_blocks[block_index(k, i)].rearrange("a p c -> p (a c)"))\
                        .then_inc(m[f"x_in{k % RING}"], 16)

                def load_block(k, i):
                    if k < EXPERTS:
                        e = block_index(k, i)
                    else:
                        e = sp.value_load(eb_i[0:1, l, k - EXPERTS:k - EXPERTS + 1], min_val=0, max_val=EXPERTS - 1)
                        e = bass.ds(e, 1)
                    block_full(sp, l, B_ROWS, k - RING, i)
                    load_rows(k, i)
                    block_full(sp, l, gu_bank(k), k - RING, i)
                    chunk(N_M[l] + k, gu_d[e].rearrange("a p c -> p (a c)"))
                    block_full(sp, l, B_YB, k - RING, i)
                    sp.dma_start(flat(down[:, k % RING]), dn_d[e].rearrange("a p c -> p (a c)"))\
                        .then_inc(m[f"down_in{k % RING}"], 16)

                sp.wait_ge(m["scattered"], 16 * 2 * (5 - l))
                for k in range(RING):
                    load_rows(k, 0)
                rounds = EXPERTS // RING - 1
                with sp.Fori(0, rounds) as i:
                    for k in range(RING, 2 * RING):
                        load_block(k, i)
                sp.wait_ge(m["eb_ready"], 1)
                for k in range(RING * (rounds + 1), NBLK[l]):
                    load_block(k, 0)

            first_weights(0, ((1, lambda: out_chunk_used(sp, 2)), (2, lambda: None),
                              (0, lambda: out_chunk_used(sp, 3))))
            experts(0)
            sp.wait_ge(mo[0]["gath_used"], 5)
            chunk(N_KV, a["w_kv"][0])
            for dst, src in ((stab, a["t_swa"]), (sink_b, a["swa_sinks"][0].partition_broadcast(128)),
                             (kvb, a["kv_b"].partition_broadcast(128)),
                             (qb, a["swa_b_q"][0].partition_broadcast(128)),
                             (bo, a["swa_b_o"][0].partition_broadcast(128))):
                sp.dma_start(dst, src).then_inc(s_swat, 16)
            chunk(N_Q, a["w_q"][0])
            chunk(N_Q + 1, a["w_q"][1])
            fl.wait_full(sp, f"KV{TILES5[-1]}")
            chunk(N_O, a["w_o"][0])
            sp.dma_start(flat(wo_b), a["w_o"][1]).then_inc(wo_b_in, 16)
            first_weights(1, ((0, lambda: fl.wait_full(sp, f"Qa{NT - 1}")), (1, lambda: fl.wait_full(sp, f"Qb{NT - 1}")),
                              (2, lambda: fl.wait_full(sp, f"WO{NT - 1}"))))
            experts(1)
            for j in range(RING):
                sp.wait_ge(mo[1][f"y_out{j}"], 16 * (len(range(j, NBLK[1], RING)) + 1))
            sp.dma_start(fin_g, a["final_norm"].partition_broadcast(128)).then_inc(fin_in, 16)
            for t in range(NT):
                sp.wait_ge(fin_done, t + 1)
                sp.dma_start(out[0, 128 * t:128 * t + 128, :], fo[:, t, :]).then_inc(s_out, 16)
            sp.wait_ge(s_out, 16 * NT)

        @block.tensor
        def _(pe):
            mm = nc.tensor.matmul

            def transposed(tag, tiles, src, sig):
                for n, t in enumerate(tiles):
                    r, b = rows(t), fl.bank(f"{tag}{t}")
                    fl.wait_free(pe, f"{tag}{t}")
                    pe.wait_ge(sig["xn_done"], n + 1)
                    for k in range(KT):
                        last = nc.tensor.transpose(ps[:, b + k // 4, 128 * (k % 4):128 * (k % 4) + r],
                                                   src[0:r, t, 128 * k:128 * k + 128], ident[0:r, 0:r])
                    last.then_inc(full[b], 1)

            pe.wait_ge(s_const, 16)
            transposed("n0_", TILES5, ret_xn, nrm["_r"])
            pe.wait_ge(x_lo_made, 5)

            def split_product(dst, a_parts, b_parts, start, stop):
                terms = ((0, 0), (0, 1), (1, 0))
                for n, (x, y) in enumerate(terms):
                    last = mm(dst, a_parts[x], b_parts[y], start=(start and n == 0), stop=(stop and n == 2))
                return last

            def feature_major_product(name, i, m):
                b = fl.bank(name)
                fl.wait_free(pe, name, i)
                for g in range(2):
                    c = slice(HALF * g, HALF * g + HALF)
                    for k in range(KT):
                        last = split_product(ps[:, b + g, 0:HALF], (w_hi[0][:, m, k, :], w_lo[0][:, m, k, :]),
                                             (x_hi[:, k, c], x_lo[:, k, c]), k == 0, k == KT - 1)
                last.then_inc(full[b], 1)

            def columns(bank, r):
                return ps[0:r, bank, :].rearrange("p (m c) -> p m c", m=4)

            def head_mean(name, src, i):
                b = fl.bank(name)
                fl.wait_free(pe, name, i)
                for g in range(2):
                    for m in range(4):
                        last = mm(ps[:, b + g, 0:HALF], mean512, src[:, m, HALF * g:HALF * g + HALF],
                                  start=(m == 0), stop=(m == 3))
                last.then_inc(full[b], 1)

            def head(z, i):
                for m, name in enumerate(("Q1", "Q2", "K1", "K2")):
                    pe.wait_ge(lo_made, piece_number(z, i, QK_, m))
                    feature_major_product(name + z, i, m)
                if z != "a":
                    outputs_read(pe, i if z == "r" else HEADS - 2)
                    head_mean("MU" + z, o_fm, i)
                pe.wait_ge(lo_made, piece_number(z, i, V_C, 3))
                for name, tiles in (("V01", (0, 1)), ("V23", (2, 3)), ("V4", (META,))):
                    b = fl.bank(name + z)
                    fl.wait_free(pe, name + z, i)
                    for g, t in enumerate(tiles):
                        c = slice(col0(t), col0(t) + rows(t))
                        for k in range(KT):
                            last = split_product(columns(b + g, rows(t)), (x_hi[:, k, c], x_lo[:, k, c]),
                                                 (w_hi[0][:, :, k, :], w_lo[1][:, :, k, :]), k == 0, k == KT - 1)
                    last.then_inc(full[b], 1)
                hd = head_of(z, i)
                pe.wait_ge(q_ready, hd * 2 + 2)
                pe.wait_ge(k_ready, hd * 2 + 2)
                b = fl.bank("SM" + z)
                fl.wait_free(pe, "SM" + z, i)
                for g in range(2):
                    for k in range(2):
                        last = mm(ps[0:N_META, b + g, 0:HALF], kT[:, k, 0:N_META],
                                  qT[:, k, HALF * g:HALF * g + HALF], start=(k == 0), stop=(k == 1))
                last.then_inc(full[b], 1)
                for name, tiles in (("S01", (0, 1)), ("S23", (2, 3))):
                    b = fl.bank(name + z)
                    fl.wait_free(pe, name + z, i)
                    for g, t in enumerate(tiles):
                        for k in range(2):
                            last = mm(ps[:, b + g, 0:POS - col0(t)], kT[:, k, col0(t):col0(t) + 128],
                                      qT[:, k, col0(t):POS], start=(k == 0), stop=(k == 1))
                    last.then_inc(full[b], 1)
                if z != "a":
                    pe.wait_ge(squared, hd)
                    head_mean("VAR" + z, sq, i)
                for m in range(4):
                    pe.wait_ge(lo_made, piece_number(z, i, G_, m))
                    feature_major_product(f"G{m}{z}", i, m)
                for name in ("SM", "S01", "S23"):
                    fl.wait_read(pe, name + z, i)
                for m in range(4):
                    b = fl.bank(f"O{m}{z}")
                    fl.wait_free(pe, f"O{m}{z}", i)
                    for g in range(2):
                        lo, hi = HALF * g, HALF * g + HALF
                        tiles = [t for t in range(NT) if col0(t) < hi]
                        mm(ps[:, b + g, 0:HALF], v_tm[0:N_META, META, 128 * m:128 * m + 128],
                           s_meta[0:N_META, lo:hi], start=True, stop=False)
                        for t in tiles:
                            c = max(col0(t), lo)
                            last = mm(ps[:, b + g, c - lo:HALF], v_tm[:, t, 128 * m:128 * m + 128],
                                      s_t[:, t, c - col0(t):hi - col0(t)], start=False, stop=(t == tiles[-1]))
                    last.then_inc(full[b], 1)

            head("a", 0)
            with pe.Fori(0, HEADS - 2) as i:
                head("r", i)
            head("s", 0)
            outputs_read(pe, HEADS - 1)
            head_mean("MUt", o_fm, 0)
            for hf in range(2):
                groups = [(f"W{hf}_01", (0, 1)), (f"W{hf}_23", (2, 3)), (f"W{hf}_4", (META,))]
                for c in range(2):
                    n = 2 * hf + c
                    pe.wait_ge(y_split, HEADS if hf or c else HEADS // 2)
                    pe.wait_ge(lo_made, out_piece_number(n, 3))
                    for name, tiles in groups:
                        b = fl.bank(name)
                        if c == 0:
                            fl.wait_free(pe, name)
                        for g, t in enumerate(tiles):
                            at = slice(col0(t), col0(t) + rows(t))
                            for k in range(KT):
                                last = split_product(columns(b + g, rows(t)),
                                                     (y_hi[c][:, k, at], y_lo[:, KT * c + k, at]),
                                                     (w_hi[n % 2][:, :, k, :], w_lo[1 - n % 2][:, :, k, :]),
                                                     c == 0 and k == 0, c == 1 and k == KT - 1)
                        if c == 1:
                            last.then_inc(full[b], 1)
                        elif name == "W0_01":
                            pe.wait_ge(squared, HEADS)
                            head_mean("VARt", sq, 0)
                    if c == 0:
                        last.then_inc(wo_used, 1)

            def experts(l):
                m, tiles = mo[l], MOE_TILES[l]
                transposed(f"m{l}_", tiles, xn, nrm[f"_m{l}"])
                for n, t in enumerate(tiles):
                    fl.wait_read(pe, f"m{l}_{t}")
                    if n == 0:
                        fl.wait_free(pe, f"LG{l}")
                    for k in range(KT):
                        last = mm(ps[0:rows(t), 0, 20 * t:20 * t + 20], xT[:, k, col0(t):col0(t) + rows(t)],
                                  wr[:, l, k, :], start=(k == 0), stop=(k == KT - 1))
                last.then_inc(full[0], 1)
                n = EXPERTS * (5 - l)
                pe.wait_ge(m["mask_ready"], 1)
                mm(ps[:, 2, 0:n], tri, masks(l)[:, 0:n], start=True, stop=True)
                mm(ps[:, 2, 128:128 + n], ones, masks(l)[:, 0:n], start=True, stop=True).then_inc(full[2], 1)
                all_read(pe, t_blocks[l])

                def rows_to_features(k, i):
                    pe.wait_ge(m[f"x_in{k % RING}"], stage(k, i))
                    if k:
                        block_read(pe, l, B_ROWS, k - 1, i)
                    for c in range(KT):
                        last = nc.tensor.transpose(ps[:, c // 4, 128 * (c % 4):128 * (c % 4) + 128],
                                                   xg[:, k % RING, 128 * c:128 * c + 128], ident)
                    last.then_inc(full[B_ROWS], 1)

                def gate_up(k, i):
                    b = gu_bank(k)
                    w_wait(pe, N_M[l] + k, i)
                    block_read(pe, l, B_ROWS, k, i)
                    if k >= RING:
                        block_read(pe, l, b, k - RING, i)
                    for c in range(KT):
                        last = mm(ps[:, b, :], xgT[:, k % RING, c, :], w_at(N_M[l] + k)[:, c, :],
                                  start=(c == 0), stop=(c == KT - 1))
                    last.then_inc(full[b], 1)

                def hidden_to_features(k, i):
                    block_read(pe, l, gu_bank(k), k, i)
                    for c in range(2):
                        last = nc.tensor.transpose(ps[:, B_HID, 128 * c:128 * c + 128],
                                                   hid[:, k % RING, 128 * c:128 * c + 128], ident)
                    last.then_inc(full[B_HID], 1)

                def down_project(k, i):
                    pe.wait_ge(m[f"down_in{k % RING}"], stage(k, i))
                    block_read(pe, l, B_HID, k, i)
                    for half, b in enumerate((B_YA, B_YB)):
                        if k:
                            block_read(pe, l, b, k - 1, i)
                        for c in range(2):
                            last = mm(ps[:, b, :], hidT[:, c, :], down[:, k % RING, c, 512 * half:512 * half + 512],
                                      start=(c == 0), stop=(c == 1))
                        last.then_inc(full[b], 1)

                def block_step(k, i):
                    gate_up(k, i)
                    hidden_to_features(k - 1, i)
                    if k + 1 < NBLK[l]:
                        rows_to_features(k + 1, i)
                    down_project(k - 1, i)

                rows_to_features(0, 0)
                gate_up(0, 0)
                rows_to_features(1, 0)
                for k in range(1, RING):
                    block_step(k, 0)
                rounds = (NBLK[l] - 1 - RING) // RING
                with pe.Fori(0, rounds) as i:
                    for k in range(RING, 2 * RING):
                        block_step(k, i)
                for k in range(RING * (1 + rounds), NBLK[l]):
                    block_step(k, 0)
                hidden_to_features(NBLK[l] - 1, 0)
                down_project(NBLK[l] - 1, 0)

            experts(0)

            all_read(pe, t_blocks_end[0])
            transposed("n1_", TILES5, xn1, nrm["_s"])
            w_wait(pe, N_KV)
            all_read(pe, t_norm1)
            for t in TILES5:
                b = fl.bank(f"KV{t}")
                fl.wait_free(pe, f"KV{t}")
                for k in range(KT):
                    last = mm(ps[0:rows(t), b, :], xTk[:, k, col0(t):col0(t) + rows(t)], w_at(N_KV)[:, k, :],
                              start=(k == 0), stop=(k == KT - 1))
                last.then_inc(full[b], 1)
            for n, t in enumerate(TILES5):
                b, r = fl.bank(f"KT{t}"), rows(t)
                fl.wait_free(pe, f"KT{t}")
                pe.wait_ge(kr_ready, n + 1)
                for j in range(KV_HEADS):
                    last = nc.tensor.transpose(ps[:, b, 128 * j:128 * j + r], kr[0:r, n % 2, j, :], ident[0:r, 0:r])
                last.then_inc(full[b], 1)
            all_read(pe, t_kv)

            def project_q(t):
                for c, name in enumerate((f"Qa{t}", f"Qb{t}")):
                    w_wait(pe, N_Q + c)
                    fl.wait_free(pe, name)
                    for k in range(KT):
                        last = mm(ps[:, 4 + c, :], xT[:, k, col0(t):col0(t) + 128], w_at(N_Q + c)[:, k, :],
                                  start=(k == 0), stop=(k == KT - 1))
                    last.then_inc(full[4 + c], 1)

            def transpose_q(t):
                fl.wait_free(pe, f"QT{t}")
                pe.wait_ge(q_rot, t + 1)
                for k in range(KT):
                    last = nc.tensor.transpose(ps[:, k // 4, 128 * (k % 4):128 * (k % 4) + 128],
                                               qr[:, 128 * k:128 * k + 128], ident)
                last.then_inc(full[0], 1)

            project_q(0)
            transpose_q(0)
            for t in range(NT):
                fl.wait_read(pe, f"QT{t}")
                prev = col0(t) - CHUNK if t else 0
                for p in range(8):
                    b = fl.bank(f"S{t}_{p}")
                    fl.wait_free(pe, f"S{t}_{p}")
                    for g, hd in enumerate(head_pair(p)):
                        o = 64 * (hd % 2)
                        q = qT1[o:o + 64, hd // 2, :]
                        for at, c, n in ((0, col0(t), 128), (128, 0, CHUNK), (128 + CHUNK, prev, CHUNK)):
                            last = mm(ps[:, b, 256 * g + at:256 * g + at + n], q,
                                      kT2[o:o + 64, hd // 4, c:c + n], start=True, stop=True)
                    last.then_inc(full[b], 1)
                if t + 1 < NT:
                    project_q(t + 1)
                fl.wait_free(pe, f"AV{t}")

                def weigh(p):
                    fl.wait_read(pe, f"PT{t}_{p}")
                    for g in range(2):
                        hd = 2 * p + g
                        dst = ps[:, 6 + hd // 8, 64 * (hd % 8):64 * (hd % 8) + 64]
                        j = 64 * (hd // 4)
                        mm(dst, PT[:, p % 2, 2 * g, :], V[:, t, j:j + 64], start=True, stop=False)
                        last = mm(dst, PT[:, p % 2, 2 * g + 1, :], VX[:, t, j:j + 64], start=False, stop=True)
                    if p == 7:
                        last.then_inc(full[6], 1)

                if t == 0:
                    pe.wait_ge(V_ready, 5)
                    pe.wait_ge(VX_ready, 2 * NT - 1)
                for p in range(8):
                    b = fl.bank(f"PT{t}_{p}")
                    fl.wait_free(pe, f"PT{t}_{p}")
                    pe.wait_ge(p_exp, 16 * t + 2 * p + 2)
                    for g in range(2):
                        for c in range(2):
                            last = nc.tensor.transpose(ps[:, b, 128 * (2 * g + c):128 * (2 * g + c) + 128],
                                                       P[:, 2 * p + g, 128 * c:128 * c + 128], ident)
                    last.then_inc(full[b], 1)
                    if p:
                        weigh(p - 1)
                weigh(7)
                if t + 1 < NT:
                    transpose_q(t + 1)
                fl.wait_free(pe, f"OT{t}")
                fl.wait_read(pe, f"AV{t}")
                for k in range(KT):
                    last = nc.tensor.transpose(ps[:, 2 + k // 4, 128 * (k % 4):128 * (k % 4) + 128],
                                               oN[:, 128 * k:128 * k + 128], ident)
                last.then_inc(full[2], 1)
                fl.wait_free(pe, f"WO{t}")
                if t + 1 < NT:
                    fl.wait_read(pe, f"Qb{t + 1}")
                fl.wait_read(pe, f"OT{t}")
                w_wait(pe, N_O)
                pe.wait_ge(wo_b_in, 16)
                for c, w in enumerate((w_at(N_O), wo_b)):
                    for k in range(KT):
                        last = mm(ps[:, 4 + c, :], oT1[:, k, :], w[:, k, :],
                                  start=(k == 0), stop=(k == KT - 1))
                last.then_inc(full[4], 1)
            all_read(pe, t_swa)
            experts(1)

        @block.scalar
        def _(act):
            def squares(tiles, sig, junk, ready):
                for n, t in enumerate(tiles):
                    ready(t)
                    r = rows(t)
                    if n:
                        act.wait_ge(sig["sq_done"], n)
                    nc.scalar.activation(junk[0:r], h[0:r, t, :], ACT.Square,
                                         accum_out=ss[0:r, t:t + 1]).then_inc(sig["sq_done"], 1)

            act.dma_start(h[0:N_META, META, :], a["meta_tokens"]).then_inc(x_in[META], 16)
            act.dma_start(con[:, :], a["t_con"]).then_inc(s_const, 16)
            act.dma_start(flat(gains[:, :, :]), a["gains"]).then_inc(s_gains, 16)
            act.dma_start(wr[:, :, :, :].rearrange("p a b c -> p (a b c)"), a["w_route"]).then_inc(s_gains, 16)
            act.dma_start(arena[:, ROPE:ROPE + NRT], a["t_ret"]).then_inc(s_rt, 16)
            squares(TILES5, nrm["_r"], ret_junk, lambda t: act.wait_ge(x_in[t], 16))

            def hi_part(slot, to, m):
                nc.scalar.activation(w_hi[to][:, m], w_raw[slot][:, m], ACT.Copy).then_inc(hi_made, 1)

            for n, t in enumerate(TILES5):
                fl.wait_read(act, f"n0_{t}")
                c = slice(col0(t), col0(t) + rows(t))
                nc.scalar.activation(x_hi[:, :, c], xT[:, :, c], ACT.Copy).then_inc(x_hi_made, 1)
                if n >= 2:
                    piece_arrived(act, "a", 0, QK_, n - 2)
                    hi_part(0, 0, n - 2)
            piece_arrived(act, "a", 0, QK_, 3)
            hi_part(0, 0, 3)

            def square_outputs(z, i):
                fl.wait_read(act, "MU" + z, i)
                nc.scalar.activation(flat(sq), flat(o_fm), ACT.Square).then_inc(squared, 1)

            def deviation(z, i):
                b = fl.bank("VAR" + z)
                fl.wait_full(act, "VAR" + z, i)
                nc.scalar.activation(halves(rs), pair(b), ACT.Sqrt, bias=con[:, C_EPS:C_EPS + 1]).then_inc(free[b], 1)

            def head(z, i):
                def copy_outputs(m):
                    b = fl.bank(f"O{m}{z}")
                    fl.wait_full(act, f"O{m}{z}", i)
                    nc.scalar.activation(halves(o_fm[:, m, :]), pair(b), ACT.Copy).then_inc(free[b], 1)

                def clear_slots(j):
                    n = MAXBLK // (2 * HEADS)
                    dst = slot_rows.rearrange("(h j b p) c -> h j p b c", j=2, b=n, p=BLK)
                    dst = dst[1:][bass.ds(i, 1), j].rearrange("a p b c -> p (a b) c") if z == "r" else dst[head_of(z, i), j]
                    act.dma_start(dst, zero.unsqueeze(1).to_broadcast([128, n, D])).then_inc(s_zeroed, 16)

                for m, last in enumerate(("Q1", "Q2", "K1", "K2")):
                    fl.wait_full(act, last + z, i)
                    piece_arrived(act, z, i, V_C, m)
                    hi_part(1, 0, m)
                if z != "a":
                    square_outputs(z, i)
                for name, t, n in (("V01", 0, 2), ("V23", 2, 2)):
                    b = fl.bank(name + z)
                    fl.wait_full(act, name + z, i)
                    nc.scalar.activation(v_tm[:, t:t + n, :], ps[:, b:b + 2, :], ACT.Copy).then_inc(free[b], 1)
                clear_slots(0)
                b = fl.bank("V4" + z)
                fl.wait_full(act, "V4" + z, i)
                nc.scalar.activation(v_tm[0:N_META, META, :], ps[0:N_META, b, :], ACT.Copy).then_inc(free[b], 1)
                for m in range(4):
                    piece_arrived(act, z, i, G_, m)
                    hi_part(0, 0, m)
                if z != "a":
                    deviation(z, i)
                    act.wait_ge(y_ready, i + 1 if z == "r" else HEADS - 1)
                clear_slots(1)
                for m in range(4):
                    fl.wait_full(act, f"G{m}{z}", i)
                    nc.scalar.activation(halves(gate[:, m, :]), pair(fl.bank(f"G{m}{z}")), ACT.Tanh, scale=0.5)\
                        .then_inc(gt_done, 1)
                    if m == 3:
                        copy_outputs(0)
                    if z == "a":
                        piece_arrived(act, "r", 0, QK_, m)
                        hi_part(0, 0, m)
                    elif z == "r":
                        act.wait_ge(piece_in[0][m], i * 32 + 80)
                        hi_part(0, 0, m)
                    else:
                        out_piece_arrived(act, 0, m)
                        hi_part(1, 0, m)
                for m in range(1, 4):
                    copy_outputs(m)

            act.wait_ge(s_zero, 1)
            head("a", 0)
            with act.Fori(0, HEADS - 2) as i:
                head("r", i)
            head("s", 0)

            def out_weights(n):
                for m in range(4):
                    out_piece_arrived(act, n, m)
                    hi_part(1 - n % 2, n % 2, m)

            out_weights(1)
            square_outputs("t", 0)
            deviation("t", 0)
            for n in (2, 3):
                out_chunk_used(act, n - 2)
                out_weights(n)

            def experts(l, ready):
                m = mo[l]
                squares(MOE_TILES[l], nrm[f"_m{l}"], moe_junk[l], ready)
                act.wait_ge(m["eg_in"], 1)
                nc.scalar.activation(view(EG, 5 - l, 4), view(EG, 5 - l, 4), ACT.Exp).then_inc(m["eg_out"], 1)
                act.wait_ge(m["d_in"], 1)
                nc.scalar.activation(view(DX, 5 - l), view(DX, 5 - l), ACT.Exp).then_inc(m["d_out"], 1)

                def tanh_of(k, i):
                    b = gu_bank(k)
                    block_full(act, l, b, k, i)
                    if k >= RING:
                        block_read(act, l, b, k - RING, i)
                    nc.scalar.activation(th[:, k % RING, :], ps[:, b, 0:FF], ACT.Tanh, scale=0.5)\
                        .then_inc(m["tanh_done"], 1)

                def hidden_of(k, i):
                    block_full(act, l, B_HID, k, i)
                    nc.scalar.activation(flat(hidT), ps[:, B_HID, 0:FF], ACT.Copy).then_inc(free[B_HID], 1)

                def results_of(k, i):
                    j = k % RING
                    block_full(act, l, B_YA, k, i)
                    act.wait_ge(m[f"y_out{j}"], stage(k, i))
                    nc.scalar.activation(yo[:, j, 0:512], ps[:, B_YA, :], ACT.Copy).then_inc(free[B_YA], 1)
                    block_read(act, l, B_YA, k, i)
                    block_read(act, l, B_YB, k, i)
                    act.dma_start(slot_out.rearrange("(b p) c -> b p c", p=BLK)[block_index(k, i)]
                                  .rearrange("a p c -> p (a c)"), yo[:, j, :]).then_inc(m[f"y_out{j}"], 16)

                tanh_of(0, 0)

                def block_step(k, i):
                    hidden_of(k - 1, i)
                    tanh_of(k, i)
                    results_of(k - 1, i)

                for k in range(1, RING):
                    block_step(k, 0)
                rounds = NBLK[l] // RING - 1
                with act.Fori(0, rounds) as i:
                    for k in range(RING, 2 * RING):
                        block_step(k, i)
                for k in range(RING * (1 + rounds), NBLK[l]):
                    block_step(k, 0)
                hidden_of(NBLK[l] - 1, 0)
                results_of(NBLK[l] - 1, 0)

            def after_retention(t):
                for hf in range(2):
                    fl.wait_read(act, f"W{hf}_4" if t == META else f"W{hf}_{'01' if t < 2 else '23'}")

            experts(0, after_retention)
            squares(TILES5, nrm["_s"], next_junk, lambda t: act.wait_ge(mo[0]["gath_used"], TILES5.index(t) + 1))
            for n, t in enumerate(TILES5):
                b, r = fl.bank(f"KT{t}"), rows(t)
                fl.wait_full(act, f"KT{t}")
                nc.scalar.activation(kT2[:, :, col0(t):col0(t) + r],
                                     ps[:, b, :].rearrange("p (j c) -> p j c", j=4)[:, :, 0:r], ACT.Copy)\
                    .then_inc(free[b], 1)

            def q_out(t):
                fl.wait_full(act, f"QT{t}")
                nc.scalar.activation(flat(qT1), flat(ps[:, 0:2, :]), ACT.Copy).then_inc(free[0], 1)

            q_out(0)
            for t in range(NT):
                for g in range(2):
                    act.wait_ge(m_ready, 2 * t + g + 1)
                    for hd in range(8 * g, 8 * g + 8):
                        nc.scalar.activation(P[:, hd, :], P[:, hd, :], ACT.Exp, bias=nmx[:, hd:hd + 1],
                                             accum_out=sm[:, hd:hd + 1]).then_inc(p_exp, 1)
                    nc.scalar.activation(sx[:, 8 * g:8 * g + 8], es[:, 8 * g:8 * g + 8], ACT.Exp).then_inc(snk_exp, 1)
                for p in range(1, 8, 2):
                    b = fl.bank(f"PT{t}_{p}")
                    fl.wait_full(act, f"PT{t}_{p}")
                    nc.scalar.activation(flat(PT[:, 1]), ps[:, b, :], ACT.Copy).then_inc(free[b], 1)
                if t + 1 < NT:
                    q_out(t + 1)
                fl.wait_full(act, f"OT{t}")
                nc.scalar.activation(flat(oT1), flat(ps[:, 2:4, :]), ACT.Copy).then_inc(free[2], 1)
            experts(1, lambda t: fl.wait_read(act, f"WO{t}"))
            squares(MOE_TILES[1], nrm["_f"], next_junk, lambda t: act.wait_ge(mo[1]["gath_used"], t + 1))

        @block.vector
        def _(dve):
            V_ = nc.vector

            def low_x(n, t):
                c = slice(col0(t), col0(t) + rows(t))
                dve.wait_ge(x_hi_made, n + 1)
                V_.tensor_tensor(x_lo[:, :, c], xT[:, :, c], x_hi[:, :, c], ALU.subtract).then_inc(x_lo_made, 1)

            def norm_tile(sig, n, t, dst):
                r = rows(t)
                dve.wait_ge(sig["rstd_done"], n + 1)
                V_.tensor_scalar(dst[0:r, t, :], h[0:r, t, :], rstd[0:r, t:t + 1], None, ALU.mult)\
                    .then_inc(sig["xn_done"], 1)

            def gained(dst, b, g, gain, c0, r, j=None):
                src = ps[:, b + g, :].rearrange("p (k c) -> p k c", k=4)[:, :, 0:r]
                return V_.tensor_tensor(dst[:, 4 * g:4 * g + 4, c0:c0 + r], src,
                                        gains[:, gain, 4 * g:4 * g + 4].unsqueeze(2).to_broadcast([128, 4, r]), ALU.mult)

            def feature_major(tag, t, gain):
                b = fl.bank(f"{tag}{t}")
                fl.wait_full(dve, f"{tag}{t}")
                gained(xT, b, 0, gain, col0(t), rows(t))
                gained(xT, b, 1, gain, col0(t), rows(t)).then_inc(free[b], 1)

            V_.memset(zero, 0.0).then_inc(s_zero, 1)
            for n, t in enumerate(TILES5):
                norm_tile(nrm["_r"], n, t, ret_xn)
                if n == 1:
                    dve.wait_ge(s_gains, 32)
                if n:
                    feature_major("n0_", TILES5[n - 1], G_RET)
                if n >= 2:
                    low_x(n - 2, TILES5[n - 2])
            feature_major("n0_", TILES5[-1], G_RET)
            low_x(3, TILES5[3])
            low_x(4, TILES5[4])
            dve.wait_ge(s_rt, 16)
            step = Steps(dve, dsem["r"])
            tmp = [sq[:, n, :] for n in range(4)]

            def center(z, i):
                fl.wait_full(dve, "MU" + z, i)
                b = fl.bank("MU" + z)
                for m in range(4):
                    last = V_.tensor_tensor(halves(o_fm[:, m, :]), halves(o_fm[:, m, :]), pair(b), ALU.subtract)
                last.then_inc(free[b], 1)

            def gated(z, i):
                fl.wait_read(dve, "VAR" + z, i)
                step(V_.reciprocal(rs, rs))
                for m in range(4):
                    last = V_.tensor_tensor(o_fm[:, m, :], o_fm[:, m, :], rs, ALU.mult)
                step(last)
                before = {"s": HEADS - 2, "t": HEADS - 1}
                dst = yT[:, bass.ds(i * 4, 4), :] if z == "r" else yT[:, 4 * before[z]:4 * before[z] + 4, :]
                V_.scalar_tensor_tensor(dst, o_fm, 0.5, gate, ALU.mult, ALU.mult).then_inc(y_ready, 1)
                dve.wait_ge(y_ready, i + 1 if z == "r" else before[z] + 1)

            def head(z, i):
                hd = head_of(z, i)
                for lo, hi, dst, sig in (("Q1", "Q2", qT, q_ready), ("K1", "K2", kT, k_ready)):
                    bl, bh = fl.bank(lo + z), fl.bank(hi + z)
                    fl.wait_full(dve, lo + z, i)
                    V_.tensor_tensor(halves(tmp[0]), pair(bl), halves(rope_c), ALU.mult)
                    fl.wait_full(dve, hi + z, i)
                    step.done(V_.tensor_tensor(halves(tmp[1]), pair(bh), halves(rope_s), ALU.mult))
                    V_.tensor_tensor(halves(tmp[2]), pair(bh), halves(rope_c), ALU.mult).then_inc(free[bh], 1)
                    V_.tensor_tensor(halves(tmp[3]), pair(bl), halves(rope_s), ALU.mult).then_inc(free[bl], 1)
                    step.wait()
                    V_.tensor_tensor(dst[:, 0, :], tmp[0], tmp[1], ALU.subtract).then_inc(sig, 1)
                    fl.wait_read(dve, hi + z, i)
                    fl.wait_read(dve, lo + z, i)
                    V_.tensor_tensor(dst[:, 1, :], tmp[2], tmp[3], ALU.add).then_inc(sig, 1)
                    dve.wait_ge(sig, hd * 2 + 2)
                if z != "a":
                    center(z, i)
                dec = decay[:, bass.ds(hd, 1), :].rearrange("p a c -> p (a c)") if z == "r" else decay[:, hd, :]
                b = fl.bank("SM" + z)
                fl.wait_full(dve, "SM" + z, i)
                V_.tensor_tensor(halves(s_meta[0:N_META, :]), pair(b)[0:N_META], halves(dec[0:N_META, :]),
                                 ALU.mult).then_inc(free[b], 1)
                for name, tiles in (("S01", (0, 1)), ("S23", (2, 3))):
                    b = fl.bank(name + z)
                    fl.wait_full(dve, name + z, i)
                    for g, t in enumerate(tiles):
                        n = POS - col0(t)
                        last = V_.tensor_tensor(s_t[:, t, 0:n], ps[:, b + g, 0:n], dec[:, 0:n], ALU.mult)
                    last.then_inc(free[b], 1)
                if z != "a":
                    gated(z, i)
                for m in range(4):
                    b = fl.bank(f"G{m}{z}")
                    dve.wait_ge(gt_done, hd * 4 + (m + 1))
                    V_.scalar_tensor_tensor(halves(gate[:, m, :]), halves(gate[:, m, :]), 1.0, pair(b),
                                            ALU.add, ALU.mult).then_inc(free[b], 1)

            head("a", 0)
            with dve.Fori(0, HEADS - 2) as i:
                step.rounds(i, 4)
                head("r", i)
            step.end(HEADS - 2)
            head("s", 0)

            def split_y(hd):
                k = slice(4 * hd, 4 * hd + 4)
                hi = y_hi[hd // 2][:, 4 * (hd % 2):4 * (hd % 2) + 4, :]
                V_.tensor_copy(hi, yT[:, k, :]).then_inc(y_hi_made, 1)
                dve.wait_ge(y_hi_made, hd + 1)
                V_.tensor_tensor(y_lo[:, k, :], yT[:, k, :], hi, ALU.subtract).then_inc(y_split, 1)

            fl.wait_full(dve, "G3s")
            for name in ("SM", "S01", "S23"):
                fl.wait_read(dve, name + "s")
            for hd in range(HEADS - 1):
                split_y(hd)
            center("t", 0)
            dve.wait_ge(s_zeroed, 32 * HEADS)
            gated("t", 0)
            split_y(HEADS - 1)
            for hf in range(2):
                for name, t, n in ((f"W{hf}_01", 0, 2), (f"W{hf}_23", 2, 2)):
                    b = fl.bank(name)
                    fl.wait_full(dve, name)
                    hh = h[:, t:t + n, 512 * hf:512 * hf + 512]
                    V_.tensor_tensor(hh, ps[:, b:b + 2, :], hh, ALU.add).then_inc(free[b], 1)
                    if hf == 1:
                        for tt in (t, t + 1):
                            norm_tile(nrm["_m0"], tt, tt, xn)
                b = fl.bank(f"W{hf}_4")
                fl.wait_full(dve, f"W{hf}_4")
                hh = h[0:N_META, META, 512 * hf:512 * hf + 512]
                V_.tensor_tensor(hh, ps[0:N_META, b, :], hh, ALU.add).then_inc(free[b], 1)

            def experts(l):
                m, tiles, nt = mo[l], MOE_TILES[l], 5 - l
                step = Steps(dve, dsem_m[l])
                if l == 0:
                    step.done(V_.memset(lg[:, META, :], 0.0))
                feature_major(f"m{l}_", tiles[0], G_MOE[l])
                norm_tile(nrm[f"_m{l}"], nt - 1, tiles[-1], xn)
                for t in tiles[1:]:
                    feature_major(f"m{l}_", t, G_MOE[l])
                fl.wait_full(dve, f"LG{l}")
                if l == 0:
                    step.wait()
                    V_.tensor_copy(lg[0:N_META, META, :], ps[0:N_META, 0, 20 * META:20 * META + 20])
                V_.tensor_copy(flat(lg[:, 0:NT, :]), ps[:, 0, 0:20 * NT]).then_inc(free[0], 1)
                fl.wait_read(dve, f"LG{l}")
                g, e = lg[:, 0:nt, 0:GROUPS], lg[:, 0:nt, GROUPS:20]
                ge = e.rearrange("p t (g e) -> p t g e", g=GROUPS)
                rev = con[:, C_REV:C_REV + 4].unsqueeze(1).to_broadcast([128, nt, 4])

                def v(at, *shape):
                    return view(at, *shape)

                def over4(x):
                    return x.unsqueeze(2).to_broadcast([128, nt, 4])

                def first_max(src, top, eq, one):
                    step(V_.tensor_reduce(top, src, X, ALU.max))
                    step(V_.tensor_tensor(eq, src, over4(top), ALU.is_ge))
                    step(V_.tensor_tensor(eq, eq, rev, ALU.mult))
                    step(V_.tensor_reduce(v(T1, nt), eq, X, ALU.max))
                    step(V_.tensor_tensor(one, eq, over4(v(T1, nt)), ALU.is_equal))

                first_max(g, v(TOP, nt), v(EQ, nt, 4), v(OHG, nt, 4))
                V_.tensor_tensor(v(EG, nt, 4), g, over4(v(TOP, nt)), ALU.subtract).then_inc(m["eg_in"], 1)
                g4 = v(G44, nt, 4, 4)
                for t in range(nt):
                    last = V_.tensor_tensor(g4[:, t], ge[:, t],
                                            v(OHG, nt, 4)[:, t].unsqueeze(2).to_broadcast([128, 4, 4]), ALU.mult)
                step(last)
                step(V_.tensor_reduce(v(SEL, nt, 4), g4.rearrange("p t g e -> p t e g"), X, ALU.add))
                first_max(v(SEL, nt, 4), v(M1, nt), v(EQ, nt, 4), v(OH1, nt, 4))
                step(V_.scalar_tensor_tensor(v(SEL, nt, 4), v(OH1, nt, 4), -1e30, v(SEL, nt, 4), ALU.mult, ALU.add))
                first_max(v(SEL, nt, 4), v(M2, nt), v(EQ, nt, 4), v(OH2, nt, 4))
                V_.tensor_tensor(v(DX, nt), v(M2, nt), v(M1, nt), ALU.subtract).then_inc(m["d_in"], 1)
                if l == 0:
                    step(V_.tensor_tensor(v(OHG, nt, 4), v(OHG, nt, 4), over4(con[:, C_VALID:C_VALID + nt]), ALU.mult))
                for at, oh in ((MA, OH1), (MB, OH2)):
                    for t in range(nt):
                        last = V_.tensor_tensor(v(at, nt, 4, 4)[:, t],
                                                v(OHG, nt, 4)[:, t].unsqueeze(2).to_broadcast([128, 4, 4]),
                                                v(oh, nt, 4)[:, t].unsqueeze(1).to_broadcast([128, 4, 4]), ALU.mult)
                step(last)
                V_.tensor_tensor(masks(l)[:, 0:16 * nt], v(MA, 16 * nt), v(MB, 16 * nt), ALU.add)\
                    .then_inc(m["mask_ready"], 1)
                dve.wait_ge(m["eg_out"], 1)
                step(V_.tensor_reduce(v(T1, nt), v(EG, nt, 4), X, ALU.add))
                step(V_.reciprocal(v(TOP, nt), v(T1, nt)))
                dve.wait_ge(m["d_out"], 1)
                step(V_.tensor_scalar(v(T1, nt), v(DX, nt), 1.0, None, ALU.add))
                step(V_.reciprocal(v(T1, nt), v(T1, nt)))
                step(V_.tensor_tensor(v(W1, nt), v(TOP, nt), v(T1, nt), ALU.mult))
                step(V_.tensor_tensor(v(W2, nt), v(W1, nt), v(DX, nt), ALU.mult))
                fl.wait_full(dve, f"RK{l}")
                before = v(PRE, 6, 16)
                step(V_.memset(before[:, 0, :], 0.0))
                for t in range(nt):
                    step(V_.tensor_tensor(before[:, t + 1, :], ps[:, 2, 128 + 16 * t:144 + 16 * t], before[:, t, :], ALU.add))
                count = before[:, nt, :]
                step(V_.tensor_tensor(v(C5, 16, 4), count.unsqueeze(2).to_broadcast([128, 16, 4]),
                                      con[:, C_THR:C_THR + 4].unsqueeze(1).to_broadcast([128, 16, 4]), ALU.is_gt))
                step(V_.tensor_reduce(v(NB, 16), v(C5, 16, 4), X, ALU.add))
                step(V_.memset(v(Z16, 16), 0.0))
                step(V_.tensor_tensor_scan(v(INCL, 16), v(NB, 16), v(Z16, 16), 0.0, ALU.add, ALU.add))
                first = con[:, C_FIRST:C_FIRST + 16].unsqueeze(1).to_broadcast([128, nt, 16])
                step(V_.tensor_tensor(v(BASE, 16), v(INCL, 16), v(NB, 16), ALU.subtract))
                step(V_.tensor_tensor(v(BASE, 16), v(BASE, 16), con[:, C_OVER:C_OVER + 16], ALU.add))
                step(V_.tensor_scalar(v(BASE, 16), v(BASE, 16), float(BLK), None, ALU.mult))
                sl, over = v(SL, nt, 16), v(OV, nt, 16)
                V_.tensor_tensor(sl, ps[:, 2, 0:16 * nt].rearrange("p (t e) -> p t e", e=16), before[:, 0:nt, :],
                                 ALU.add).then_inc(free[2], 1)
                fl.wait_read(dve, f"RK{l}")
                step(V_.scalar_tensor_tensor(over, sl, BLK - 0.5, v(BASE, 16).unsqueeze(1).to_broadcast([128, nt, 16]),
                                             ALU.is_gt, ALU.mult))
                step(V_.tensor_tensor(sl, sl, first, ALU.add))
                step(V_.tensor_tensor(sl, sl, over, ALU.add))
                for n, at in enumerate((MA, MB)):
                    step(V_.tensor_tensor(v(at, nt, 16), v(at, nt, 16), sl, ALU.mult))
                    step(V_.tensor_reduce(v(SF, 2, 5)[:, n, 0:nt], v(at, nt, 16), X, ALU.add))
                V_.tensor_copy(slot_i[:, :, 0:nt], v(SF, 2, 5)[:, :, 0:nt]).then_inc(m["slot_ready"], 1)
                no = NBLK[l] - EXPERTS
                eb = v(EB, no, 16)[0:1]
                step(V_.tensor_tensor(eb, v(INCL, 16)[0:1].unsqueeze(1).to_broadcast([1, no, 16]),
                                      con[0:1, C_BLK:C_BLK + no].unsqueeze(2).to_broadcast([1, no, 16]), ALU.is_le))
                step(V_.tensor_reduce(v(EBS, no)[0:1], eb, X, ALU.add))
                V_.tensor_scalar(eb_i[0:1, l, 0:no], v(EBS, no)[0:1], float(EXPERTS - 1), None, ALU.min)\
                    .then_inc(m["eb_ready"], 1)

                def widen(k, i):
                    block_full(dve, l, B_ROWS, k, i)
                    for g in range(2):
                        last = gained(xgT[:, k % RING], 0, g, G_MOE[l], 0, BLK)
                    last.then_inc(free[B_ROWS], 1)

                def hidden(k, i):
                    b, j = gu_bank(k), k % RING
                    dve.wait_ge(m["tanh_done"], i * RING + (k + 1))
                    step(V_.scalar_tensor_tensor(hid1, th[:, j, :], 1.0, ps[:, b, 0:FF], ALU.add, ALU.mult))
                    V_.scalar_tensor_tensor(hid[:, j, :], hid1, 0.5, ps[:, b, FF:2 * FF], ALU.mult, ALU.mult)\
                        .then_inc(free[b], 1)

                def results_of(k, i):
                    j = k % RING
                    block_full(dve, l, B_YB, k, i)
                    dve.wait_ge(m[f"y_out{j}"], stage(k, i))
                    V_.tensor_copy(yo[:, j, 512:1024], ps[:, B_YB, :]).then_inc(free[B_YB], 1)

                for j in range(RING):
                    V_.memset(v(Z16, 16)[:, j:j + 1], 0.0).then_inc(m[f"y_out{j}"], 16)
                widen(0, 0)
                widen(1, 0)
                hidden(0, 0)
                rounds = (NBLK[l] - 2) // RING
                with dve.Fori(0, rounds) as i:
                    step.rounds(i, RING)
                    for k in range(1, 1 + RING):
                        widen(k + 1, i)
                        hidden(k, i)
                        results_of(k - 1, i)
                step.end(rounds)
                for k in range(1 + RING * rounds, NBLK[l]):
                    if k + 1 < NBLK[l]:
                        widen(k + 1, 0)
                    hidden(k, 0)
                    results_of(k - 1, 0)
                results_of(NBLK[l] - 1, 0)
                def combine(t):
                    r, n = rows(t), tiles.index(t)
                    dve.wait_ge(m[f"gathered{t}"], 32)
                    step(V_.scalar_tensor_tensor(h[0:r, t, :], gat[0:r, t, 0, :], v(W1, nt)[0:r, t:t + 1],
                                                 h[0:r, t, :], ALU.mult, ALU.add))
                    V_.scalar_tensor_tensor(h[0:r, t, :], gat[0:r, t, 1, :], v(W2, nt)[0:r, t:t + 1],
                                            h[0:r, t, :], ALU.mult, ALU.add).then_inc(m["gath_used"], 1)
                return combine

            combine = experts(0)

            step = Steps(dve, dsem["a"])

            def kv_features(t):
                b = fl.bank(f"n1_{t}")
                fl.wait_full(dve, f"n1_{t}")
                for gx in range(2):
                    last = gained(xTk, b, gx, G_KV, col0(t), rows(t))
                if t != META:
                    for gx in range(2):
                        last = gained(xT, b, gx, G_SWA, col0(t), rows(t))
                last.then_inc(free[b], 1)

            for n in range(len(TILES5) + 2):
                if n < len(TILES5):
                    combine(TILES5[n])
                if 1 <= n <= len(TILES5):
                    norm_tile(nrm["_s"], n - 1, TILES5[n - 1], xn1)
                if n >= 2:
                    kv_features(TILES5[n - 2])
            dve.wait_ge(s_swat, 80)

            def rotate(x, t, r, nh, A_, B_, outs):
                cos = stab[0:r, 32 * t:32 * t + 32].unsqueeze(1)
                sin = stab[0:r, 160 + 64 * t:160 + 64 * t + 64]
                xv = x.rearrange("p (h c) -> p h c", c=32)
                step.done(V_.tensor_tensor(A_.rearrange("p (h c) -> p h c", c=32), xv,
                                           cos.to_broadcast([r, 2 * nh, 32]), ALU.mult))
                x4, b4 = (y.rearrange("p (h s c) -> p h s c", s=2, c=32) for y in (x, B_))
                for s in range(2):
                    step.done(V_.tensor_tensor(b4[:, :, s, :], x4[:, :, 1 - s, :],
                                               sin[:, 32 * s:32 * s + 32].unsqueeze(1).to_broadcast([r, nh, 32]), ALU.mult))
                step.wait()
                for o in outs:
                    last = V_.tensor_tensor(o, A_.rearrange("p (h c) -> p h c", c=64),
                                            B_.rearrange("p (h c) -> p h c", c=64), ALU.add)
                return last

            for n, t in enumerate(TILES5):
                b, r = fl.bank(f"KV{t}"), rows(t)
                fl.wait_full(dve, f"KV{t}")
                if n >= 2:
                    dve.wait_ge(V_ready, n - 1)
                V_.tensor_tensor(kvs[0:r, n % 2, :], ps[0:r, b, :], kvb[0:r, :], ALU.add).then_inc(free[b], 1)
                fl.wait_read(dve, f"KV{t}")
                if n >= 2:
                    fl.wait_full(dve, f"KT{TILES5[n - 2]}")
                if n:
                    dve.wait_ge(kr_ready, n)
                rotate(kvs[0:r, n % 2, 0:256], t, r, 4, flat(kA)[0:r], flat(kB)[0:r],
                       [kr[0:r, n % 2, :, 0:64], kr[0:r, n % 2, :, 64:128]]).then_inc(kr_ready, 1)

            def rotate_q(t):
                for c, name in enumerate((f"Qa{t}", f"Qb{t}")):
                    fl.wait_full(dve, name)
                    if c == 0 and t:
                        fl.wait_full(dve, f"QT{t - 1}")
                        dve.wait_ge(q_rot, t)
                    V_.tensor_tensor(qs[:, 512 * c:512 * c + 512], ps[:, 4 + c, :], qb[:, 512 * c:512 * c + 512],
                                     ALU.add).then_inc(free[4 + c], 1)
                fl.wait_read(dve, f"Qa{t}")
                fl.wait_read(dve, f"Qb{t}")
                rotate(qs, t, 128, 16, qA, qr, [qr.rearrange("p (h c) -> p h c", c=64)]).then_inc(q_rot, 1)

            rotate_q(0)
            for t in range(NT):
                mask = stab[:, 480 + 256 * min(t, 1):480 + 256 * min(t, 1) + 256].unsqueeze(1).to_broadcast([128, 2, 256])
                for g in range(2):
                    for p in range(4 * g, 4 * g + 4):
                        b = fl.bank(f"S{t}_{p}")
                        fl.wait_full(dve, f"S{t}_{p}")
                        h0 = head_pair(p)[0]
                        V_.scalar_tensor_tensor(P[:, h0:h0 + 3:2, :], ps[:, b, :].rearrange("p (h k) -> p h k", h=2),
                                                HD ** -0.5, mask, ALU.mult, ALU.add).then_inc(free[b], 1)
                        fl.wait_read(dve, f"S{t}_{p}")
                        step.done(V_.tensor_reduce(mx[:, h0:h0 + 3:2], P[:, h0:h0 + 3:2, :], X, ALU.max))
                    step.wait()
                    c = slice(8 * g, 8 * g + 8)
                    step(V_.tensor_tensor(mx[:, c], mx[:, c], sink_b[:, c], ALU.max))
                    if t:
                        dve.wait_ge(p_exp, 16 * t)
                        dve.wait_ge(snk_exp, 2 * t)
                    step(V_.tensor_tensor(es[:, c], sink_b[:, c], mx[:, c], ALU.subtract))
                    V_.tensor_scalar(nmx[:, c], mx[:, c], -1.0, None, ALU.mult).then_inc(m_ready, 1)
                if t + 1 < NT:
                    rotate_q(t + 1)
                for p in range(0, 8, 2):
                    b = fl.bank(f"PT{t}_{p}")
                    fl.wait_full(dve, f"PT{t}_{p}")
                    V_.tensor_copy(flat(PT[:, 0]), ps[:, b, :]).then_inc(free[b], 1)
                dve.wait_ge(snk_exp, 2 * t + 2)
                dve.wait_ge(p_exp, 16 * t + 16)
                step(V_.tensor_tensor(rc, sm, sx, ALU.add))
                step(V_.reciprocal(rc, rc))
                fl.wait_full(dve, f"AV{t}")
                if t:
                    fl.wait_full(dve, f"OT{t - 1}")
                V_.tensor_tensor(oN.rearrange("p (h c) -> p h c", c=64),
                                 flat(ps[:, 6:8, :]).rearrange("p (h c) -> p h c", c=64),
                                 rc.unsqueeze(2).to_broadcast([128, 16, 64]), ALU.mult).then_inc(free[6], 1)
                if t == NT - 1:
                    for n in range(t):
                        norm_tile(nrm["_m1"], n, n, xn)
                fl.wait_full(dve, f"WO{t}")
                dve.wait_ge(bo_added, t + 1)
                V_.tensor_tensor(h[:, t, :], flat(ps[:, 4:6, :]), h[:, t, :], ALU.add).then_inc(free[4], 1)
            combine = experts(1)
            dve.wait_ge(fin_in, 16)
            for n in range(NT + 1):
                if n < NT:
                    combine(n)
                if n:
                    t = n - 1
                    dve.wait_ge(nrm["_f"]["rstd_done"], t + 1)
                    V_.scalar_tensor_tensor(fo[:, t, :], h[:, t, :], rstd[:, t:t + 1], fin_g, ALU.mult, ALU.mult)\
                        .then_inc(fin_done, 1)

        @block.gpsimd
        def _(pool):
            G = nc.gpsimd

            def deviations(tiles, sig):
                for n, t in enumerate(tiles):
                    r = rows(t)
                    pool.wait_ge(sig["sq_done"], n + 1)
                    G.tensor_scalar(var[0:r, t:t + 1], ss[0:r, t:t + 1], 1.0 / D, EPS, ALU.mult, ALU.add)\
                        .then_inc(sig["var_done"], 1)
                    pool.wait_ge(sig["var_done"], n + 1)
                    G.tensor_tensor(rstd[0:r, t:t + 1], var[0:r, t:t + 1], con[0:r, C_NH:C_NH + 1], ALU.pow)\
                        .then_inc(sig["rstd_done"], 1)

            pool.wait_ge(s_const, 16)
            deviations(TILES5, nrm["_r"])

            def low_piece(slot, to, m, number):
                pool.wait_ge(hi_made, number)
                G.tensor_tensor(w_lo[slot][:, m], w_raw[slot][:, m], w_hi[to][:, m], ALU.subtract).then_inc(lo_made, 1)

            def head(z, i):
                for slot, c in ((0, QK_), (1, V_C), (0, G_)):
                    for m in range(4):
                        low_piece(slot, 0, m, piece_number(z, i, c, m))

            head("a", 0)
            with pool.Fori(0, HEADS - 2) as i:
                head("r", i)
            head("s", 0)
            for n in range(4):
                for m in range(4):
                    low_piece(1 - n % 2, n % 2, m, out_piece_number(n, m))

            def experts(l):
                m, tiles = mo[l], MOE_TILES[l]
                deviations(tiles, nrm[f"_m{l}"])
                pool.wait_ge(m["slot_ready"], 1)
                if l == 0:
                    pool.wait_ge(s_zeroed, 32 * HEADS)
                for t in tiles:
                    r = rows(t)
                    for c in range(2):
                        G.indirect_dma_start(slot_rows, bass.IndirectOffsetOnAxis(slot_i[0:r, c, t:t + 1], 0),
                                             xn[0:r, t, :], None).then_inc(m["scattered"], 16)
                for j in range(RING):
                    pool.wait_ge(m[f"y_out{j}"], 16 * (len(range(j, NBLK[l], RING)) + 1))
                for t in TILES5[l:]:
                    r = rows(t)
                    for c in range(2):
                        G.indirect_dma_start(gat[0:r, t, c, :], None, slot_out,
                                             bass.IndirectOffsetOnAxis(slot_i[0:r, c, t:t + 1], 0))\
                            .then_inc(m[f"gathered{t}"], 16)

            experts(0)
            deviations(TILES5, nrm["_s"])
            pool.wait_ge(s_swat, 80)
            for t in range(NT):
                pool.wait_ge(nrm["_s"]["xn_done"], t + 2)
                G.tensor_tensor(h[:, t, :], h[:, t, :], bo, ALU.add).then_inc(bo_added, 1)
            G.memset(flat(VX), 0.0).then_inc(VX_zero, 1)
            for n, t in enumerate(TILES5):
                r = rows(t)
                fl.wait_read(pool, f"KV{t}")
                G.tensor_copy(V[0:r, t, :], kvs[0:r, n % 2, 256:512]).then_inc(V_ready, 1)
            pool.wait_ge(VX_zero, 1)
            pool.wait_ge(V_ready, 5)
            for t in range(NT):
                G.tensor_copy(VX[0:N_META, t, :], V[0:N_META, META, :]).then_inc(VX_ready, 1)
                if t:
                    G.tensor_copy(VX[64:128, t, :], V[64:128, t - 1, :]).then_inc(VX_ready, 1)
            experts(1)
            deviations(MOE_TILES[1], nrm["_f"])



_NAMES = ["x", "meta_tokens", "kv_b", "swa_b_q", "swa_sinks", "swa_b_o", "final_norm"]


def _chunks(w):
    kk, nn = w.shape[0] // D, w.shape[1] // 512
    w = w.reshape(kk, KT, 128, nn, 512).transpose(3, 0, 2, 1, 4)
    return np.ascontiguousarray(w.reshape(nn * kk, 128, KT * 512))


def _pieces(w):
    return np.ascontiguousarray(w.reshape(KT, 128, 4, 128).transpose(2, 1, 0, 3)).reshape(4, 128, KT * 128)


def _layout(i):
    out = {n: np.ascontiguousarray(i[n]) for n in _NAMES}
    w = i["ret_w_in"][0]
    heads = []
    for hd in range(HEADS):
        qk = np.concatenate([w[:, QK * hd:QK * hd + QK], w[:, D + QK * hd:D + QK * hd + QK]], axis=1)
        vg = [w[:, 2 * D + n * HEADS * VD + VD * hd:2 * D + n * HEADS * VD + VD * hd + VD] for n in range(2)]
        heads.append(np.stack([_pieces(x) for x in (qk, *vg)]))
    out["w_ret"] = np.stack(heads)
    w = i["ret_w_out"][0]
    out["w_ret_out"] = np.stack([_pieces(w[D * c:D * c + D, 512 * hf:512 * hf + 512])
                                 for hf in range(2) for c in range(2)])
    out["w_kv"], out["w_q"], out["w_o"] = _chunks(i["kv_w"]), _chunks(i["swa_w_q"][0]), _chunks(i["swa_w_o"][0])
    gu = np.concatenate([i["moe_w_gate"], i["moe_w_up"]], axis=3)
    out["w_gu"] = np.ascontiguousarray(gu.reshape(2, EXPERTS, KT, 128, 512).transpose(0, 1, 3, 2, 4)).reshape(
        2, EXPERTS, 128, KT * 512)
    dn = i["moe_w_down"].reshape(2, EXPERTS, 2, 128, D).transpose(0, 1, 3, 2, 4)
    out["w_down"] = np.ascontiguousarray(dn).reshape(2, EXPERTS, 128, 2 * D)
    route = np.concatenate([i["moe_w_group"], i["moe_w_router"]], axis=2)
    out["w_route"] = np.ascontiguousarray(route.reshape(2, KT, 128, 20).transpose(2, 0, 1, 3)).reshape(128, -1)
    g = np.stack([i["ret_norm"][0], i["kv_norm"], i["swa_norm"][0], i["moe_norm"][0], i["moe_norm"][1]])
    out["gains"] = np.ascontiguousarray(g.reshape(5, KT, 128).transpose(2, 0, 1)).reshape(128, -1)
    return out


def kernel(**inputs):
    import concourse.bacc as _bacc
    from concourse.bass_utils import run_bass_kernel_spmd as _run

    nc = _bacc.Bacc("TRN2", target_bir_lowering=False, num_devices=1)
    arrays = _layout({n: np.asarray(v) for n, v in inputs.items()})
    arrays["t_con"], arrays["t_ret"], arrays["t_swa"] = tables()
    aps = {n: nc.dram_tensor(f"in_{n}", v.shape, mybir.dt.from_np(v.dtype), kind="ExternalInput").ap()
           for n, v in arrays.items()}
    out = nc.dram_tensor("out", (1, SEQ, D), mybir.dt.float32, kind="ExternalOutput").ap()
    build(nc, aps, out)
    return _run(nc, [{f"in_{n}": v for n, v in arrays.items()}], core_ids=[0]).results[0]["out"]
```
